# Optimizing a Trainium2 kernel written in Bass

```python
import math
import jax, jax.numpy as jnp
from jax import lax
import numpy as np

D_MODEL = 1024
BATCH = 1
SEQ = 1024
DEPTH = 1

DSA_HEADS = D_MODEL // 128
DSA_HEAD_DIM = 64
DSA_LATENT = D_MODEL // 8
IDX_HEADS = 4
IDX_DIM = 32
TOPK_MAX = 256
DIFF_HEADS = D_MODEL // 256
DIFF_QK_DIM = 64
DIFF_V_DIM = 2 * DIFF_QK_DIM
DSA_OUT = DSA_HEADS * DSA_HEAD_DIM
DIFF_OUT = DIFF_HEADS * DIFF_V_DIM
MIX_WIDTH = DSA_OUT + DIFF_OUT
IN_SPLITS = (DSA_HEADS * DSA_HEAD_DIM,
             DSA_LATENT,
             IDX_HEADS * IDX_DIM,
             IDX_DIM,
             IDX_HEADS,
             DIFF_HEADS * 2 * DIFF_QK_DIM,
             DIFF_HEADS * 2 * DIFF_QK_DIM,
             DIFF_HEADS * DIFF_V_DIM)
IN_WIDTH = sum(IN_SPLITS)
Q_BLOCK = 128
N_GROUPS = 4
EXPERTS_PER_GROUP = 8
N_EXPERTS = N_GROUPS * EXPERTS_PER_GROUP
EXPERT_TOPK = 2
D_EXPERT = D_MODEL // 4
EPS = 1e-6

kernel_name = "hybrid_dsa_diffattn_hmoe_block"

def rms_norm(x, g):
    xf = x.astype(jnp.float32)
    y = xf * lax.rsqrt(jnp.mean(xf * xf, axis=-1, keepdims=True) + EPS)
    return (y * g.astype(jnp.float32)).astype(x.dtype)

def alibi_slopes(n):
    return jnp.asarray([2.0 ** (-8.0 * (i + 1) / n) for i in range(n)], dtype=jnp.float32)

def lambda_init(layer):
    return 0.8 - 0.6 * math.exp(-0.3 * layer)

def to_blocks(a):
    b, s = a.shape[:2]
    a = a.reshape((b, s // Q_BLOCK, Q_BLOCK) + a.shape[2:])
    return jnp.moveaxis(a, 1, 0)

def from_blocks(a):
    a = jnp.moveaxis(a, 0, 1)
    return a.reshape((a.shape[0], -1) + a.shape[3:])

def dsa_attention(q, c_kv, q_idx, k_idx, w_idx, w_uk, w_uv, slopes):
    L = q.shape[1]
    n_blocks = L // Q_BLOCK
    topk = min(TOPK_MAX, L // 4)
    key_pos = jnp.arange(L)
    q_abs = jnp.einsum('bshd,hcd->bshc', q, w_uk)
    scale = DSA_HEAD_DIM ** -0.5
    idx_scale = IDX_DIM ** -0.5

    def block(args):
        blk, qa, qi, wi = args
        q_pos = blk * Q_BLOCK + jnp.arange(Q_BLOCK)
        causal = key_pos[None, :] <= q_pos[:, None]
        rel = jax.nn.relu(jnp.einsum('bqhd,bsd->bqhs', qi, k_idx) * idx_scale)
        score = jnp.einsum('bqhs,bqh->bqs', rel, wi)
        score = jnp.where(causal[None], score, -jnp.inf)
        _, sel = lax.top_k(score, topk)
        kv_sel = jax.vmap(lambda ck, i: ck[i])(c_kv, sel)
        s = jnp.einsum('bqhc,bqkc->bqhk', qa, kv_sel).astype(jnp.float32) * scale
        dist = (q_pos[None, :, None] - sel).astype(jnp.float32)
        s = s - slopes[None, None, :, None] * dist[:, :, None, :]
        s = jnp.where((dist >= 0)[:, :, None, :], s, -jnp.inf)
        p = jax.nn.softmax(s, axis=-1).astype(kv_sel.dtype)
        o_lat = jnp.einsum('bqhk,bqkc->bqhc', p, kv_sel)
        return jnp.einsum('bqhc,hcd->bqhd', o_lat, w_uv)

    out = lax.map(block, (jnp.arange(n_blocks), to_blocks(q_abs), to_blocks(q_idx), to_blocks(w_idx)))
    return from_blocks(out)

def diff_attention(q, k, v, lam, lam_init, sub_g, slopes):
    L = q.shape[1]
    n_blocks = L // Q_BLOCK
    key_pos = jnp.arange(L)
    scale = DIFF_QK_DIM ** -0.5

    def block(args):
        blk, qb = args
        q_pos = blk * Q_BLOCK + jnp.arange(Q_BLOCK)
        dist = (q_pos[:, None] - key_pos[None, :]).astype(jnp.float32)
        s = jnp.einsum('bqhmd,bshmd->bhmqs', qb, k).astype(jnp.float32) * scale
        s = s - slopes[None, :, None, None, None] * dist
        s = jnp.where(dist >= 0, s, -jnp.inf)
        p = jax.nn.softmax(s, axis=-1)
        a = p[:, :, 0] - lam * p[:, :, 1]
        return jnp.einsum('bhqs,bshe->bqhe', a.astype(v.dtype), v)

    o = from_blocks(lax.map(block, (jnp.arange(n_blocks), to_blocks(q))))
    return rms_norm(o, sub_g) * (1.0 - lam_init)

def hier_moe(h, w_group, b_group, w_router, b_router, w_gate, w_up, w_down):
    T = h.shape[0]
    g_logits = jnp.dot(h, w_group).astype(jnp.float32) + b_group.astype(jnp.float32)
    g_prob = jax.nn.softmax(g_logits, axis=-1)
    g_sel = jnp.argmax(g_logits, axis=-1)
    p_g = jnp.take_along_axis(g_prob, g_sel[:, None], axis=-1)
    e_logits = (jnp.dot(h, w_router).astype(jnp.float32) + b_router.astype(jnp.float32))
    e_logits = e_logits.reshape(T, N_GROUPS, EXPERTS_PER_GROUP)
    e_logits = jnp.take_along_axis(e_logits, g_sel[:, None, None], axis=1)[:, 0]
    top_v, top_i = lax.top_k(e_logits, EXPERT_TOPK)
    top_w = jax.nn.softmax(top_v, axis=-1) * p_g
    eid = g_sel[:, None] * EXPERTS_PER_GROUP + top_i
    gates = jnp.sum(jax.nn.one_hot(eid, N_EXPERTS, dtype=jnp.float32) * top_w[..., None], axis=1)
    gates = gates.astype(h.dtype)
    y = jnp.zeros_like(h)
    for e in range(N_EXPERTS):
        hid = jax.nn.silu(jnp.dot(h, w_gate[e])) * jnp.dot(h, w_up[e])
        y = y + gates[:, e:e + 1] * jnp.dot(hid, w_down[e])
    return y

def setup_inputs(seed: int = 0) -> dict:
    key = jax.random.key(seed)
    ks = jax.random.split(key, 26)
    f32 = jnp.float32
    D = D_MODEL

    def nrm(k, shape, std):
        return jax.random.normal(k, shape, f32) * std

    def gain(k, shape):
        return 1.0 + 0.05 * jax.random.normal(k, shape, f32)

    return {
        "x": nrm(ks[0], (BATCH, SEQ, D), 1.0),
        "c": nrm(ks[1], (BATCH, D), 1.0),
        "w_ada": nrm(ks[2], (DEPTH, D, 6 * D), 0.5 * D ** -0.5),
        "b_ada": nrm(ks[3], (DEPTH, 6 * D), 0.02),
        "g_attn": gain(ks[4], (DEPTH, D)),
        "w_in": nrm(ks[5], (DEPTH, D, IN_WIDTH), D ** -0.5),
        "g_kv": gain(ks[6], (DEPTH, DSA_LATENT)),
        "w_uk": nrm(ks[7], (DEPTH, DSA_HEADS, DSA_LATENT, DSA_HEAD_DIM), DSA_LATENT ** -0.5),
        "w_uv": nrm(ks[8], (DEPTH, DSA_HEADS, DSA_LATENT, DSA_HEAD_DIM), DSA_LATENT ** -0.5),
        "lam_q1": nrm(ks[9], (DEPTH, DIFF_QK_DIM), 0.1),
        "lam_k1": nrm(ks[10], (DEPTH, DIFF_QK_DIM), 0.1),
        "lam_q2": nrm(ks[11], (DEPTH, DIFF_QK_DIM), 0.1),
        "lam_k2": nrm(ks[12], (DEPTH, DIFF_QK_DIM), 0.1),
        "g_sub": gain(ks[13], (DEPTH, DIFF_V_DIM)),
        "w_out": nrm(ks[14], (DEPTH, MIX_WIDTH, D), MIX_WIDTH ** -0.5),
        "g_moe": gain(ks[15], (DEPTH, D)),
        "w_group": nrm(ks[16], (DEPTH, D, N_GROUPS), D ** -0.5),
        "b_group": nrm(ks[17], (DEPTH, N_GROUPS), 0.01),
        "w_router": nrm(ks[18], (DEPTH, D, N_EXPERTS), D ** -0.5),
        "b_router": nrm(ks[19], (DEPTH, N_EXPERTS), 0.01),
        "w_gate": nrm(ks[20], (DEPTH, N_EXPERTS, D, D_EXPERT), D ** -0.5),
        "w_up": nrm(ks[21], (DEPTH, N_EXPERTS, D, D_EXPERT), D ** -0.5),
        "w_down": nrm(ks[22], (DEPTH, N_EXPERTS, D_EXPERT, D), D_EXPERT ** -0.5),
        "g_final": gain(ks[23], (D,)),
    }

def reference(x, c, w_ada, b_ada, g_attn, w_in, g_kv, w_uk, w_uv, lam_q1, lam_k1, lam_q2, lam_k2,
              g_sub, w_out, g_moe, w_group, b_group, w_router, b_router, w_gate, w_up, w_down, g_final):
    B, S, D = x.shape
    dsa_slopes = alibi_slopes(DSA_HEADS)
    diff_slopes = alibi_slopes(DIFF_HEADS)
    split_pts = list(np.cumsum(IN_SPLITS)[:-1])
    c_act = jax.nn.silu(c)
    for l in range(DEPTH):
        mod = jnp.dot(c_act, w_ada[l]) + b_ada[l]
        shift_a, scale_a, gate_a, shift_m, scale_m, gate_m = jnp.split(mod, 6, axis=-1)

        h = rms_norm(x, g_attn[l]) * (1.0 + scale_a[:, None]) + shift_a[:, None]
        proj = jnp.dot(h, w_in[l])
        dq, dlat, iq, ik, iw, fq, fk, fv = jnp.split(proj, split_pts, axis=-1)
        dq = dq.reshape(B, S, DSA_HEADS, DSA_HEAD_DIM)
        dlat = rms_norm(dlat, g_kv[l])
        iq = iq.reshape(B, S, IDX_HEADS, IDX_DIM)
        iw = iw * (IDX_HEADS ** -0.5)
        fq = fq.reshape(B, S, DIFF_HEADS, 2, DIFF_QK_DIM)
        fk = fk.reshape(B, S, DIFF_HEADS, 2, DIFF_QK_DIM)
        fv = fv.reshape(B, S, DIFF_HEADS, DIFF_V_DIM)

        o_dsa = dsa_attention(dq, dlat, iq, ik, iw, w_uk[l], w_uv[l], dsa_slopes)
        lam0 = lambda_init(l)
        lam = (jnp.exp(jnp.sum(lam_q1[l].astype(jnp.float32) * lam_k1[l].astype(jnp.float32)))
               - jnp.exp(jnp.sum(lam_q2[l].astype(jnp.float32) * lam_k2[l].astype(jnp.float32)))
               + lam0)
        o_diff = diff_attention(fq, fk, fv, lam, lam0, g_sub[l], diff_slopes)
        o = jnp.concatenate([o_dsa.reshape(B, S, DSA_OUT), o_diff.reshape(B, S, DIFF_OUT)], axis=-1)
        x = x + gate_a[:, None] * jnp.dot(o, w_out[l])

        h = rms_norm(x, g_moe[l]) * (1.0 + scale_m[:, None]) + shift_m[:, None]
        y = hier_moe(h.reshape(B * S, D), w_group[l], b_group[l], w_router[l], b_router[l],
                     w_gate[l], w_up[l], w_down[l]).reshape(B, S, D)
        x = x + gate_m[:, None] * y
    return rms_norm(x, g_final)


_drawn_inputs = setup_inputs


def setup_inputs(seed=0):
    import zlib

    import numpy as np

    out = dict(_drawn_inputs(seed))
    spreads = {}
    factors = {'g_kv': 7.386,
     'lam_q1': 8.0,
     'lam_k1': 8.0,
     'lam_k2': 43.744,
     'g_sub': 5.134,
     'g_moe': 3.457,
     'b_group': 8.0,
     'b_router': 8.0,
     'lam_q2': 8.0}
    for name, (base, spread) in spreads.items():
        noise = np.random.default_rng([zlib.crc32(name.encode()), seed]).standard_normal(out[name].shape)
        drawn = base * np.exp(spread * noise) if base else spread * noise
        out[name] = __import__('jax').numpy.asarray(drawn.astype(out[name].dtype))
    for name, factor in factors.items():
        out[name] = (out[name] * factor).astype(out[name].dtype)
    return out
```

```python
import math
from contextlib import ExitStack

import concourse.bass as bass
from concourse import mybir

F32 = mybir.dt.float32
I32 = mybir.dt.int32
U32 = mybir.dt.uint32
ALU = mybir.AluOpType
ACT = mybir.ActivationFunctionType
AX_X = mybir.AxisListType.X
P = 128
BANK = 512


def groups_of(t):
    return [(m, b, min(b + 4, t + 1)) for m in range(2) for b in range(0, t + 1, 4)]


def hybrid_layer(nc, x, c, w_ada, b_ada, g_attn, w_in, g_kv, w_uk, w_uv, lam_q1, lam_k1, lam_q2, lam_k2,
                 g_sub, w_out, g_moe, w_group, b_group, w_router, b_router, w_gate, w_up, w_down, g_final, out):
    _, S, D = x.shape
    T = S // P
    KC = D // P
    _, NH, LAT, DH = w_uk.shape
    DV = g_sub.shape[1]
    QD = lam_q1.shape[1]
    NG = w_group.shape[2]
    NE = w_router.shape[2]
    EPG = NE // NG
    NR = NG + NE
    DE = w_gate.shape[3]
    IH = 4
    ID = 32
    OFF_LAT = NH * DH
    OFF_FQ = OFF_LAT + LAT + IH * ID + ID + IH
    NIDX = OFF_FQ - OFF_LAT
    DIFF = (w_in.shape[2] - OFF_FQ) // 3
    NDIFF = DIFF // DV
    TOPK = min(256, S // 4)
    T0 = TOPK // P
    EPS = 1e-6
    LAM0 = 0.8 - 0.6 * math.exp(0.0)
    NEG = -1e30
    LOW = -3.0e38
    NOV = 2 * S // P - 1
    NT = NE + NOV
    MODS = 6 * KC
    UNITS = 4
    assert D == 1024 and S == 1024 and DH == 64 and QD == 64 and DV == 128 and LAT == 128
    assert NH == 2 * UNITS and NDIFF == UNITS and DE == 256 and NE == 32 and NG == 4 and T0 == 2

    sel_tiles = list(range(T0, T))
    sc_off, at = {}, 0
    for t in sel_tiles:
        sc_off[t] = at
        at += P * (t + 1)
    SCW = at
    NS = len(sel_tiles)

    h2_dram = nc.dram_tensor("h2_rows", [S, D], F32, kind="Internal").ap()
    y_dram = nc.dram_tensor("expert_rows", [NT * P, D], F32, kind="Internal").ap()

    ctx = ExitStack()
    with ctx:
        def sb(name, shape, dt=F32):
            return ctx.enter_context(nc.sbuf_tensor(name, shape, dt))

        def sem(name):
            return ctx.enter_context(nc.semaphore(name))

        class Chain:

            def __init__(self, eng, s):
                self.eng, self.s, self.base, self.n = eng, s, 0, 0

            def __call__(self, ins):
                ins.then_inc(self.s, 1)
                self.n += 1
                self.eng.wait_ge(self.s, self.base + self.n)

            def loop(self, u, per):
                self.start = self.n if isinstance(self.base, int) and self.base == 0 else self.start
                self.base, self.n, self.per = self.start + u * per, 0, per

            def leave(self, times):
                assert self.n == self.per, (self.n, self.per)
                self.n, self.base = self.start + times * self.per, 0

        HT = sb("HT", [P, KC, S])
        QKV = sb("QKV", [P, 6 * 4096])
        X = sb("X", [P, 8192])
        SC = sb("SC", [P, SCW])
        BIAS = sb("BIAS", [P, 3, S])
        R = sb("R", [P, S])
        ident = sb("ident", [P, P])
        ones = sb("ones", [P, P])
        before = sb("before", [P, P])
        iota_p = sb("iota_p", [P, P])
        iota_t = sb("iota_t", [P, NT])
        tok = sb("tok", [P, T])
        neghalf = sb("neghalf", [P, T])
        slopes = sb("slopes", [P, 4])
        cols = sb("cols", [P, MODS + 3 * KC])
        cact = sb("cact", [P, KC])
        cexp = sb("cexp", [P, KC])
        mod = sb("mod", [P, MODS])
        sc1 = sb("sc1", [P, KC])
        ss = sb("ss", [P, 4 * T])
        gkv = sb("gkv", [P, LAT])
        gsub = sb("gsub", [P, DV])
        lam2 = sb("lam2", [P, 4])
        wuk = sb("wuk", [P, NH, DH])
        wuv = sb("wuv", [P, NH, DH])
        wgr = sb("wgr", [P, KC, NR])
        bgr = sb("bgr", [P, NR])
        iw = sb("iw", [P, T, IH])
        tk = sb("tk", [P, 6, NS], U32)
        cnt = sb("cnt", [P, 2, NS])
        nmx = sb("nmx", [P, 2, 2])
        rs = sb("rs", [P, 2, 2])
        rin = sb("rin", [P, 2, 2])
        osb = sb("osb", [P, 2, P])
        osq = sb("osq", [P, P])
        oss = sb("oss", [P, 4])
        logits = sb("logits", [P, T, NR])
        rt = sb("rt", [P, 14, T])
        lst = sb("lst", [P, NT], I32)
        slot = sb("slot", [P, 2, T], I32)
        idx = sb("idx", [P, 2], I32)
        ovi = sb("ovi", [P, NOV + 1], I32)
        PS = ctx.enter_context(nc.psum_tensor("PS", [P, 8, BANK], F32))

        vrows = BIAS[0:MODS + 3 * KC, 0, 0:P]
        lamv = BIAS[:, 1, 0:4 * QD].rearrange("p (a n) -> p a n", a=4)
        ada = [QKV[:, 4096 * i:4096 * (i + 1)].rearrange("p (j n) -> p j n", j=KC) for i in range(4)]
        WI = QKV[:, 4 * 4096:4 * 4096 + KC * NIDX].rearrange("p (j n) -> p j n", j=KC)
        WIK = QKV[:, 5 * 4096:5 * 4096 + KC * P].rearrange("p (j n) -> p j n", j=KC)
        WD = QKV[:, 5 * 4096 + 1024:5 * 4096 + 1024 + KC * (LAT + IH)].rearrange("p (j n) -> p j n", j=KC)
        XT = X[:, :].rearrange("p (t d) -> p t d", t=T)
        iqT, ikT = X[:, 0:S], X[:, S:2 * S]
        ckvT, ckv = X[:, 0:S], X[:, 2 * S:3 * S]
        RL = X[:, 3 * S:5 * S].rearrange("p (a n) -> p a n", a=2)
        WS = X[:, 5 * S:7 * S].rearrange("p (a j n) -> p a j n", a=2, j=KC)
        zero_rows = X[:, 7 * S:8 * S]
        kT = {"dsa": QKV[:, 0:4096], "diff": QKV[:, 4 * 4096:5 * 4096]}
        qT = {"dsa": QKV[:, 2 * 4096:3 * 4096], "diff": QKV[:, 3 * 4096:4 * 4096]}
        vd = QKV[:, 4096:2 * 4096].rearrange("p (t n) -> p t n", t=T)
        vf = QKV[:, 5 * 4096:6 * 4096]
        SP_ = X[:, 0:4 * S].rearrange("p (a m n) -> p a m n", a=2, m=2)
        qst, kst = X[:, 4 * S:5 * S], X[:, 5 * S:6 * S]
        PT = X[:, 6 * S:8 * S].rearrange("p (g n) -> p g n", g=4)
        wo = QKV[:, 3 * 4096:5 * 4096].rearrange("p (k n) -> p k n", k=KC)
        rows = [BIAS[:, 0, :], BIAS[:, 1, :], BIAS[:, 2, :], R[:, :]]
        h2 = SC[:, 0:2 * D].rearrange("p (a n) -> p a n", a=2)
        h2T = SC[:, 2 * D:4 * D].rearrange("p (a n) -> p a n", a=2)
        junk = QKV[:, 20480:21504]
        proj = QKV[:, 21504:22528].rearrange("p (a n) -> p a n", a=2)
        diag = QKV[:, 22528:24576].rearrange("p (a j n) -> p a j n", a=2, j=KC)

        def dist(t):
            return R[:, S - P * (t + 1):S]

        consts, pchain = sem("consts"), sem("pchain")
        small_in = sem("small_in")
        x_in = [sem(f"x_in{i}") for i in range(T)]
        ada_in = [sem(f"ada_in{i}") for i in range(4)]
        ada_done, mod_copied = sem("ada_done"), sem("mod_copied")
        wi_in, ws_in = sem("wi_in"), [sem(f"ws_in{i}") for i in range(2)]
        lam_ready, lam_exp, op_sb = sem("lam_ready"), sem("lam_exp"), sem("op_sb")
        cols_ps, cols_sb, cexp_done, cact_done = sem("cols_ps"), sem("cols_sb"), sem("cexp_done"), sem("cact_done")
        sq_done, rstd_done, xn_done = sem("sq_done"), sem("rstd_done"), sem("xn_done")
        xt_ps, xt_act, xt_dve, aff_done = sem("xt_ps"), sem("xt_act"), sem("xt_dve"), sem("aff_done")
        wcopy = sem("wcopy")
        iqk_ps, iqk_sb, lat_ps, lat_sb, lat_sq, lat_rstd, ckv_done = (
            sem(n) for n in ("iqk_ps", "iqk_sb", "lat_ps", "lat_sb", "lat_sq", "lat_rstd", "ckv_done"))
        ckvT_ps, ckvT_sb = sem("ckvT_ps"), sem("ckvT_sb")
        ix_ps, ix_relu, ix_acc, ix_mask = sem("ix_ps"), sem("ix_relu"), sem("ix_acc"), sem("ix_mask")
        kv_ps, kv_sb, pj_ps, pj_sb = sem("kv_ps"), sem("kv_sb"), sem("pj_ps"), sem("pj_sb")
        dchain, sel_done = sem("dchain"), sem("sel_done")
        at_s = {k: {n: sem(f"{k}_{n}") for n in (
            "qk_loaded", "bias_ready", "qk_done", "max_done", "exp_done", "tr_done", "pt_act", "pt_dve",
            "pv_done", "o_done", "o_square", "o_rstd", "ot_done", "ot_copied")} for k in ("diff", "dsa")}
        wo_in, x2_in, gf_in = sem("wo_in"), sem("x2_in"), sem("gf_in")
        mod_done, diag_done, row_ps, row_sb = sem("mod_done"), sem("diag_done"), sem("row_ps"), sem("row_sb")
        op_ps, x2_done, x2_sq, x2_rstd, h2_done = (
            sem(n) for n in ("op_ps", "x2_done", "x2_sq", "x2_rstd", "h2_done"))
        h2_out = [sem(f"h2_out{i}") for i in range(2)]
        h2T_ps, h2T_sb, lg_ps, lg_sb = (sem(n) for n in ("h2T_ps", "h2T_sb", "lg_ps", "lg_sb"))
        gexp_done, gmax_done, e2_in, e2_done, sel_ps, sel_in = (
            sem(n) for n in ("gexp_done", "gmax_done", "e2_in", "e2_done", "sel_ps", "sel_in"))
        oh_done, lst_ps, route_done = sem("oh_done"), sem("lst_ps"), sem("route_done")
        w_in_s = [sem(f"w_expert{i}") for i in range(4)]
        xg_in = [sem(f"xg_in{i}") for i in range(2)]
        y_out = [sem(f"y_out{i}") for i in range(2)]
        idx_done, t_ps, t_act, t_dve, gu_ps, sg_done, hid_done, ht_ps, ht_sb, dn_ps, y_act, y_dve = (
            sem(n) for n in ("idx_done", "t_ps", "t_act", "t_dve", "gu_ps", "sg_done", "hid_done", "ht_ps",
                             "ht_sb", "dn_ps", "y_act", "y_dve"))
        ov = {n: sem("ov_" + n) for n in ("w_in", "idx", "xg_in", "t_ps", "t_sb", "gu_ps", "sg", "hid", "ht_ps",
                                          "ht_sb", "dn_ps", "y_sb", "y_out")}
        yg_in = [sem(f"yg_in{i}") for i in range(2)]
        cb_done, fin_sq, fin_rstd, fin_done, fin_out = (
            sem(n) for n in ("cb_done", "fin_sq", "fin_rstd", "fin_done", "fin_out"))

        HF = HT[:, :, :].rearrange("p k n -> p (k n)")
        WE = [QKV[:, 6144 * i:6144 * (i + 1)] for i in range(4)]
        WGU = [w[:, 0:4096].rearrange("p (g c n) -> p c g n", g=2, c=KC) for w in WE]
        WG = [w[:, 0:2048].rearrange("p (c n) -> p c n", c=KC) for w in WE]
        WU = [w[:, 2048:4096].rearrange("p (c n) -> p c n", c=KC) for w in WE]
        WDN = [w[:, 4096:6144].rearrange("p (c n) -> p c n", c=2) for w in WE]
        xg = [HF[:, 1024 * i:1024 * (i + 1)] for i in range(2)]
        hgT = [HF[:, 2048 + 1024 * i:3072 + 1024 * i] for i in range(2)]
        ysb = [HF[:, 4096 + 1024 * i:5120 + 1024 * i] for i in range(2)]
        sg = [HF[:, 6144 + 256 * i:6400 + 256 * i] for i in range(2)]
        hh_done, ov_hh, x2_half = sem("hh_done"), sem("ov_hh"), sem("x2_half")
        hh = HF[:, 6656:6912]
        hid = [HF[:, 6912 + 256 * i:7168 + 256 * i] for i in range(2)]
        hidT = [HF[:, 7424 + 256 * i:7680 + 256 * i] for i in range(2)]
        gfin = SC[:, 0:D]
        yg = [[HF[:, 2048 * i + 1024 * k:2048 * i + 1024 * (k + 1)] for k in range(2)] for i in range(2)]
        rbig = [HF[:, T * NE * i:T * NE * (i + 1)].rearrange("p (t e) -> p t e", t=T) for i in range(14)]
        gx = HF[:, 3584:3584 + T * NG].rearrange("p (t g) -> p t g", g=NG)
        gk = HF[:, 3616:3616 + T * NG].rearrange("p (t g) -> p t g", g=NG)
        ohr = [HF[:, 4096 + P * i:4096 + P * (i + 1)] for i in range(2 * T)]
        oht = [HF[:, 6144 + NT * i:6144 + NT * (i + 1)] for i in range(2 * T)]
        ovt = HF[:, 7000:7000 + NE * (NOV + 1)].rearrange("p (j e) -> p j e", e=NE)
        ovx = HF[:, 7800:7800 + NOV + 1]
        ovc = HF[:, 7600:7600 + 5 * NE].rearrange("p (a e) -> p a e", e=NE)

        wg_d = w_gate[0].rearrange("e (p c) n -> e p (c n)", c=KC)
        wu_d = w_up[0].rearrange("e (p c) n -> e p (c n)", c=KC)
        wd_d = w_down[0].rearrange("e (p c) n -> e p (c n)", c=2)
        x_d = x[0].rearrange("(t p) d -> t p d", p=P)
        win_d = w_in[0].rearrange("(j p) n -> p j n", p=P)

        def expert_load(sp, e, b, s):
            for dst, src in ((WE[b][:, 0:2048], wg_d), (WE[b][:, 2048:4096], wu_d), (WE[b][:, 4096:6144], wd_d)):
                sp.dma_start(dst, src[bass.ds(e, 1)].rearrange("o p n -> (o p) n")).then_inc(s, 16)

        passed, zero_done, fill_out = sem("passed"), sem("zero_done"), sem("fill_out")

        def settle(eng):
            eng.sem_inc(passed, 1)

        def start_at_one(eng, names):
            for kind in ("diff", "dsa"):
                for n in names:
                    eng.sem_inc(at_s[kind][n], 1)

        block = ctx.enter_context(nc.Block())

        @block.sync
        def _(sp):
            for i in range(4):
                sp.dma_start(ada[i], w_ada[0, :, BANK * i:BANK * (i + 1)].rearrange("(j p) n -> p j n", p=P)
                             ).then_inc(ada_in[i], 16)
                for t in (2 * i, 2 * i + 1):
                    sp.dma_start(XT[:, t, :], x_d[t]).then_inc(x_in[t], 16)
            sp.dma_start(WI, win_d[:, :, OFF_LAT:OFF_FQ]).then_inc(wi_in, 16)
            with sp.Fori(1, 3) as a:
                for b in range(4):
                    sp.wait_ge(ada_done, 4 * a + b - 3)
                    sp.dma_start(ada[b], w_ada[0, :, bass.ds((4 * a + b) * BANK, BANK)].rearrange(
                        "(j p) n -> p j n", p=P)).then_inc(ada_in[b], 16)
            sp.wait_ge(xt_ps, 16)
            for i in range(4):
                if i >= 2:
                    sp.wait_ge(pj_ps, 2 * (i - 1))
                sp.dma_start(WS[:, i % 2], win_d[:, :, P * i:P * (i + 1)]).then_inc(ws_in[i % 2], 16)
            sp.wait_ge(zero_done, 1)
            for j in range(NOV - 12):
                sp.dma_start(y_dram[(NE + j) * P:(NE + j + 1) * P, :], zero_rows).then_inc(fill_out, 16)
            with sp.Fori(2, 8) as a:
                for b in range(2):
                    sp.wait_ge(pj_ps, 4 * a + 2 * b - 2)
                    sp.dma_start(WS[:, b], win_d[:, :, bass.ds(a * (2 * P) + (OFF_FQ + P * (b - 4)), P)]
                                 ).then_inc(ws_in[b], 16)
                    sp.dma_start(y_dram[bass.ds(a * (2 * P) + (NE + NOV - 16 + b) * P, P), :], zero_rows
                                 ).then_inc(fill_out, 16)
            sp.wait_ge(at_s["diff"]["pv_done"], 24 * UNITS + 1)
            sp.dma_start(wo, w_out[0].rearrange("(k p) n -> p k n", p=P)).then_inc(wo_in, 16)
            sp.wait_ge(at_s["dsa"]["pv_done"], 24 * UNITS + 1)
            for t in range(T):
                sp.dma_start(XT[:, t, :], x_d[t]).then_inc(x2_in, 16)
            for e in range(2):
                expert_load(sp, e, e, w_in_s[e])
            for t in range(T):
                sp.wait_ge(h2_done, t + 1)
                sp.dma_start(h2_dram[P * t:P * (t + 1), :], h2[:, t % 2, :]).then_inc(h2_out[t % 2], 16)
            for e in range(2, 4):
                sp.wait_ge(op_ps, 2 * T)
                sp.wait_ge(h2_done, T)
                expert_load(sp, e, e, w_in_s[e])

            def store(e, b):
                sp.wait_ge(y_act, e + 1)
                sp.wait_ge(y_dve, e + 1)
                sp.dma_start(y_dram[bass.ds(e * P, P), :], ysb[b]).then_inc(y_out[b], 16)

            with sp.Fori(0, NE // 4 - 1) as i:
                for j in range(4):
                    store(4 * i + j, j % 2)
                    sp.wait_ge(dn_ps, 4 * i + j + 1)
                    expert_load(sp, 4 * i + j + 4, j, w_in_s[j])
            for j in range(4):
                store(NE - 4 + j, j % 2)
            sp.wait_ge(route_done, 1)
            n_ov = sp.value_load(ovi[0:1, NOV:NOV + 1], min_val=0, max_val=NOV)
            with sp.Fori(0, NOV) as j:
                with sp.If(n_ov > j):
                    e = sp.value_load(ovi[0:1, bass.ds(j, 1)], min_val=0, max_val=NE - 1)
                    expert_load(sp, e, 0, ov["w_in"])
                    sp.wait_ge(ov["y_sb"], j + 1)
                    sp.dma_start(y_dram[bass.ds(NE * P + j * P, P), :], ysb[0]).then_inc(ov["y_out"], 16)
                    sp.wait_ge(ov["y_out"], 16 * j + 16)
                    settle(sp)
            for t in range(T):
                sp.wait_ge(fin_done, t + 1)
                sp.dma_start(out[0, P * t:P * (t + 1), :], XT[:, t, :]).then_inc(fin_out, 16)
            sp.wait_ge(fin_out, 16 * T)

        @block.gpsimd
        def _(pool):
            start_at_one(pool, ("qk_loaded", "bias_ready", "o_rstd"))
            link = Chain(pool, pchain)
            pool.memset(ident[:, :], 0.0).then_inc(pchain, 1)
            pool.memset(before[:, :], 1.0).then_inc(pchain, 1)
            link.n = 2
            pool.wait_ge(pchain, 2)
            pool.affine_select(out=ident[:, :], in_=ident[:, :], compare_op=ALU.not_equal, fill=1.0, base=0,
                               pattern=[[-1, P]], channel_multiplier=1).then_inc(consts, 1)
            pool.memset(ones[:, :], 1.0).then_inc(consts, 1)
            pool.affine_select(out=before[:, :], in_=before[:, :], compare_op=ALU.is_ge, fill=0.0, base=-1,
                               pattern=[[1, P]], channel_multiplier=-1).then_inc(consts, 1)
            pool.memset(neghalf[:, :], -0.5).then_inc(consts, 1)
            pool.iota(iota_p[:, :], pattern=[[1, P]], base=0, channel_multiplier=0,
                      allow_small_or_imprecise_dtypes=True).then_inc(consts, 1)
            pool.iota(iota_t[:, :], pattern=[[1, NT]], base=0, channel_multiplier=0,
                      allow_small_or_imprecise_dtypes=True).then_inc(consts, 1)
            pool.iota(tok[:, :], pattern=[[P, T]], base=0, channel_multiplier=1,
                      allow_small_or_imprecise_dtypes=True).then_inc(consts, 1)
            link(pool.iota(R[:, :], pattern=[[1, S]], base=P - S, channel_multiplier=-1,
                           allow_small_or_imprecise_dtypes=True))
            pool.affine_select(out=R[:, :], in_=R[:, :], compare_op=ALU.is_ge, fill=NEG, base=S - P,
                               pattern=[[-1, S]], channel_multiplier=1).then_inc(consts, 1)
            for i, v in enumerate((2.0 ** (-8 / NDIFF), 2.0 ** (-8 / NDIFF), 2.0 ** (-8 / NH), 2.0 ** (-16 / NH))):
                link(pool.memset(slopes[:, i:i + 1], v))

            def rstd(col, n, width, scale=1.0):
                link(pool.tensor_scalar(ss[:, col:col + n], ss[:, col:col + n], 1.0 / width, EPS, ALU.mult, ALU.add))
                return pool.tensor_tensor(ss[:, col:col + n], ss[:, col:col + n], neghalf[:, 0:n], ALU.pow)

            pool.wait_ge(sq_done, T)
            rstd(0, T, D).then_inc(rstd_done, 1)
            pool.wait_ge(xt_ps, 2 * KC)
            pool.memset(zero_rows, 0.0).then_inc(zero_done, 1)
            pool.wait_ge(wi_in, 16)
            for k in range(4):
                pool.tensor_copy(WIK[:, :, ID * k:ID * (k + 1)], WI[:, :, LAT + IH * ID:LAT + IH * ID + ID]
                                 ).then_inc(wcopy, 1)
            pool.tensor_copy(WD[:, :, 0:LAT], WI[:, :, 0:LAT]).then_inc(wcopy, 1)
            pool.tensor_copy(WD[:, :, LAT:LAT + IH], WI[:, :, NIDX - IH:NIDX]).then_inc(wcopy, 1)
            pool.wait_ge(lat_sq, T)
            rstd(T, T, LAT).then_inc(lat_rstd, 1)
            for i, t in enumerate(sel_tiles):
                pool.wait_ge(ix_acc, IH * (i + 1))
                diag = SC[:, sc_off[t] + P * t:sc_off[t] + P * (t + 1)]
                pool.affine_select(out=diag, in_=diag, compare_op=ALU.is_ge, fill=LOW, base=0,
                                   pattern=[[-1, P]], channel_multiplier=1).then_inc(ix_mask, 1)

            def load_qk(kind, u, lo):
                s = at_s[kind]
                c0 = 0 if lo else S // 2
                for dst, src in ((qst, qT[kind]), (kst, kT[kind])):
                    pool.tensor_copy(dst[:, c0:c0 + S // 2], src[:, bass.ds(u * S + c0, S // 2)]
                                     ).then_inc(s["qk_loaded"], 1)

            def biases(kind, u):
                s = at_s[kind]
                if kind == "diff":
                    pool.wait_ge(s["max_done"], u * 16 + 1)
                    settle(pool)
                    pool.tensor_scalar(BIAS[:, 0, :], R[:, :], slopes[:, 0:1], 0.0, ALU.mult, ALU.add
                                       ).then_inc(s["bias_ready"], 1)
                    pool.wait_ge(s["bias_ready"], u + 2)
                    settle(pool)
                    link(pool.tensor_scalar(slopes[:, 0:1], slopes[:, 0:1], 2.0 ** (-8 / NDIFF), 0.0,
                                            ALU.mult, ALU.add))
                    return
                for i in range(2 * T):
                    t, m = T - 1 - i // 2, i % 2
                    w = P * (t + 1)
                    src = SC[:, sc_off[t]:sc_off[t] + w] if t >= T0 else dist(t)
                    pool.wait_ge(s["max_done"], u * 16 + max(i - 2, 0) + 1)
                    settle(pool)
                    pool.tensor_scalar(BIAS[:, i % 3, 0:w], src, slopes[:, 2 + m:3 + m], 0.0, ALU.mult, ALU.add
                                       ).then_inc(s["bias_ready"], 1)
                pool.wait_ge(s["bias_ready"], u * 16 + 16 + 1)
                settle(pool)
                link(pool.tensor_scalar(slopes[:, 2:4], slopes[:, 2:4], 2.0 ** (-16 / NH), 0.0, ALU.mult, ALU.add))

            def o_rstd(kind, u):
                s = at_s[kind]
                for k in range(T):
                    pool.wait_ge(s["o_square"], u * T + k + 2)
                    settle(pool)
                    link(pool.tensor_scalar(oss[:, 2 + k % 2:3 + k % 2], oss[:, k % 2:k % 2 + 1], 1.0 / DV, EPS,
                                            ALU.mult, ALU.add))
                    pool.tensor_tensor(oss[:, 2 + k % 2:3 + k % 2], oss[:, 2 + k % 2:3 + k % 2], neghalf[:, 0:1],
                                       ALU.pow).then_inc(s["o_rstd"], 1)

            pool.wait_ge(sel_done, 1)
            for kind in ("diff", "dsa"):
                s = at_s[kind]
                per = 1 + T if kind == "diff" else 1
                if kind == "diff":
                    pool.wait_ge(pj_sb, 32)
                else:
                    pool.wait_ge(at_s["diff"]["qk_done"], 16 * UNITS + 1)
                load_qk(kind, 0, False)
                load_qk(kind, 0, True)
                with pool.Fori(0, UNITS - 1) as u:
                    link.loop(u, per)
                    biases(kind, u)
                    if kind == "diff":
                        o_rstd(kind, u)
                    pool.wait_ge(s["qk_done"], u * 16 + 8 + 1)
                    load_qk(kind, u + 1, False)
                    pool.wait_ge(s["qk_done"], u * 16 + 16 + 1)
                    load_qk(kind, u + 1, True)
                link.leave(UNITS - 1)
                biases(kind, UNITS - 1)
                if kind == "diff":
                    o_rstd(kind, UNITS - 1)

            for t in range(T):
                pool.wait_ge(x2_sq, t + 1)
                rstd(2 * T + t, 1, D).then_inc(x2_rstd, 1)

            def gather(e, b):
                if not isinstance(e, int):
                    pool.wait_ge(t_ps, e - 1)
                pool.tensor_copy(idx[:, b:b + 1], lst[:, bass.ds(e, 1)]).then_inc(idx_done, 1)
                pool.wait_ge(idx_done, e + 1)
                settle(pool)
                pool.indirect_dma_start(out=xg[b], out_offset=None, in_=h2_dram,
                                        in_offset=bass.IndirectOffsetOnAxis(ap=idx[:, b:b + 1].bitcast(U32), axis=0)
                                        ).then_inc(xg_in[b], 16)

            pool.wait_ge(route_done, 1)
            for i in range(2):
                pool.wait_ge(h2_out[i], 16 * (T // 2))
            gather(0, 0)
            gather(1, 1)
            with pool.Fori(0, NE // 2 - 1) as i:
                for b in range(2):
                    gather(2 * i + 2 + b, b)
            n_ov = pool.value_load(ovi[0:1, NOV:NOV + 1], min_val=0, max_val=NOV)
            with pool.Fori(0, NOV) as j:
                with pool.If(n_ov > j):
                    pool.wait_ge(t_ps, NE)
                    pool.wait_ge(ov["t_ps"], j + 1)
                    pool.tensor_copy(idx[:, 0:1], lst[:, bass.ds(j + NE, 1)]).then_inc(ov["idx"], 1)
                    pool.wait_ge(ov["idx"], j + 1)
                    settle(pool)
                    pool.indirect_dma_start(out=xg[0], out_offset=None, in_=h2_dram,
                                            in_offset=bass.IndirectOffsetOnAxis(ap=idx[:, 0:1].bitcast(U32), axis=0)
                                            ).then_inc(ov["xg_in"], 16)
            pool.wait_ge(y_out[0], 16 * (NE // 2))
            pool.wait_ge(y_out[1], 16 * (NE // 2))
            with pool.If(n_ov > 0):
                pool.wait_ge(ov["y_out"], n_ov * 16)
            for t in range(T):
                if t >= 2:
                    pool.wait_ge(cb_done, t - 1)
                for k in range(2):
                    pool.indirect_dma_start(out=yg[t % 2][k], out_offset=None, in_=y_dram,
                                            in_offset=bass.IndirectOffsetOnAxis(
                                                ap=slot[:, k, t:t + 1].bitcast(U32), axis=0)
                                            ).then_inc(yg_in[t % 2], 16)
            for t in range(T):
                pool.wait_ge(fin_sq, t + 1)
                rstd(3 * T + t, 1, D).then_inc(fin_rstd, 1)

        @block.scalar
        def _(act):
            start_at_one(act, ("exp_done", "pt_act", "o_square", "ot_copied"))
            act.dma_start(vrows[0:MODS, :], b_ada[0].rearrange("(j p) -> j p", p=P)).then_inc(small_in, 16)
            for i, v in enumerate((c, g_attn, g_moe)):
                act.dma_start(vrows[MODS + KC * i:MODS + KC * (i + 1), :], v[0].rearrange("(j p) -> j p", p=P)
                              ).then_inc(small_in, 16)
            act.dma_start(gkv[:, :], g_kv.partition_broadcast(P).rearrange("p o n -> p (o n)")).then_inc(small_in, 16)
            act.dma_start(gsub[:, :], g_sub.partition_broadcast(P).rearrange("p o n -> p (o n)")).then_inc(small_in, 16)
            for i, v in enumerate((lam_q1, lam_k1, lam_q2, lam_k2)):
                act.dma_start(lamv[:, i, :], v.partition_broadcast(P).rearrange("p o n -> p (o n)")
                              ).then_inc(small_in, 16)
            act.dma_start(bgr[:, 0:NG], b_group.partition_broadcast(P).rearrange("p o n -> p (o n)")
                          ).then_inc(small_in, 16)
            act.dma_start(bgr[:, NG:NR], b_router.partition_broadcast(P).rearrange("p o n -> p (o n)")
                          ).then_inc(small_in, 16)
            act.dma_start(wuk[:, :, :], w_uk[0].rearrange("h c d -> c h d")).then_inc(small_in, 16)
            act.dma_start(wuv[:, :, :], w_uv[0].rearrange("h c d -> c h d")).then_inc(small_in, 16)
            act.dma_start(wgr[:, :, 0:NG], w_group[0].rearrange("(j p) n -> p j n", p=P)).then_inc(small_in, 16)
            act.dma_start(wgr[:, :, NG:NR], w_router[0].rearrange("(j p) n -> p j n", p=P)).then_inc(small_in, 16)
            act.wait_ge(cols_sb, 1)
            act.activation(cexp[:, :], cols[:, MODS:MODS + KC], ACT.Exp, scale=-1.0).then_inc(cexp_done, 1)
            act.wait_ge(lam_ready, 2)
            act.activation(lam2[:, 2:4], lam2[:, 0:2], ACT.Exp).then_inc(lam_exp, 1)
            for t in range(T):
                act.wait_ge(x_in[t], 16)
                if t:
                    act.wait_ge(sq_done, t)
                act.activation(BIAS[:, 2, :], XT[:, t, :], ACT.Square, accum_out=ss[:, t:t + 1]).then_inc(sq_done, 1)
            act.wait_ge(aff_done, 1)
            for g in range(0, 2 * KC, 2):
                act.wait_ge(xt_ps, g + 1)
                act.activation(HT[:, g // 2, 0:BANK], PS[:, g % 4, :], ACT.Identity, bias=mod[:, g // 2:g // 2 + 1],
                               scale=sc1[:, g // 2:g // 2 + 1]).then_inc(xt_act, 1)
            for n in range(4):
                act.wait_ge(iqk_ps, n + 1)
                act.activation((iqT if n < 2 else ikT)[:, BANK * (n % 2):BANK * (n % 2 + 1)], PS[:, n, :], ACT.Copy
                               ).then_inc(iqk_sb, 1)
            for t in range(T):
                act.wait_ge(lat_sb, 2 * t + 2)
                if t:
                    act.wait_ge(lat_sq, t)
                act.activation(BIAS[:, 2, 0:LAT], X[:, 2 * S + LAT * t:2 * S + LAT * (t + 1)], ACT.Square,
                               accum_out=ss[:, T + t:T + t + 1]).then_inc(lat_sq, 1)
            for n in range(IH * NS):
                t = sel_tiles[n // IH]
                act.wait_ge(ix_ps, n + 1)
                if n >= 2:
                    act.wait_ge(ix_acc, n - 1)
                act.activation(RL[:, n % 2, 0:P * (t + 1)],
                               PS[:, 2 * (n % 2):2 * (n % 2) + 2, :].rearrange("p a n -> p (a n)")[:, 0:P * (t + 1)],
                               ACT.Relu, scale=ID ** -0.5).then_inc(ix_relu, 1)
            for n in range(2):
                act.wait_ge(ckvT_ps, n + 1)
                act.activation(ckvT[:, BANK * n:BANK * (n + 1)], PS[:, 4 + n, :], ACT.Copy).then_inc(ckvT_sb, 1)
            act.wait_ge(ada_done, 12)
            act.activation(mod[:, 2 * KC:MODS], PS[:, 7, 2 * KC:MODS], ACT.Copy).then_inc(mod_copied, 1)
            for n in range(2 * UNITS):
                act.wait_ge(kv_ps, n + 1)
                act.activation(kT["dsa"][:, BANK * n:BANK * (n + 1)], PS[:, 4 + n % 2, :], ACT.Copy).then_inc(kv_sb, 1)
            for t in range(T):
                act.wait_ge(kv_ps, 2 * UNITS + t + 1)
                act.activation(vd[:, t, :], PS[:, 4 + t % 2, :], ACT.Copy).then_inc(kv_sb, 1)
            for a0, a1, scale in ((0, 4, DH ** -0.5), (4, 8, 1.0)):
                with act.Fori(a0, a1) as a:
                    for n in range(4):
                        act.wait_ge(pj_ps, 4 * a + n + 1)
                        act.activation(QKV[:, bass.ds(a * (4 * BANK) + (2 * 4096 + BANK * n), BANK)], PS[:, n, :],
                                       ACT.Copy, scale=scale).then_inc(pj_sb, 1)

            def unit(kind, u):
                s = at_s[kind]

                def exp(k, m):
                    w = P * (T - k)
                    act.wait_ge(s["max_done"], u * 16 + 2 * k + m + 2)
                    act.activation(SP_[:, k % 2, m, 0:w], SP_[:, k % 2, m, 0:w], ACT.Exp,
                                   bias=nmx[:, k % 2, m:m + 1], scale=-1.0, accum_out=rs[:, k % 2, m:m + 1]
                                   ).then_inc(s["exp_done"], 1)

                def copy_out(k):
                    chunk = u + (UNITS if kind == "diff" else 0)
                    act.wait_ge(s["ot_done"], u * T + k + 2)
                    act.activation(HF[:, bass.ds(chunk * S + P * (T - 1 - k), P)], PS[:, 6 + k % 2, 256:384],
                                   ACT.Copy).then_inc(s["ot_copied"], 1)

                exp(0, 0)
                exp(0, 1)
                g = 0
                for k in range(T):
                    gs = groups_of(T - 1 - k)
                    for i in range(0, len(gs), 2):
                        _, b0, b1 = gs[i]
                        act.wait_ge(s["tr_done"], u * 24 + g + i + 2)
                        act.wait_ge(s["pv_done"], u * 24 + max(g + i - 3, 0) + 1)
                        act.activation(PT[:, (g + i) % 4, 0:P * (b1 - b0)], PS[:, 4 + (g + i) % 2, 0:P * (b1 - b0)],
                                       ACT.Copy).then_inc(s["pt_act"], 1)
                    g += len(gs)
                    if k + 1 < T:
                        exp(k + 1, 0)
                        exp(k + 1, 1)
                    if kind == "diff":
                        act.wait_ge(s["o_done"], u * 2 * T + 2 * k + 2)
                        act.activation(osq[:, :], osb[:, k % 2, :], ACT.Square, accum_out=oss[:, k % 2:k % 2 + 1]
                                       ).then_inc(s["o_square"], 1)
                    if k:
                        copy_out(k - 1)
                copy_out(T - 1)

            act.wait_ge(fill_out, 16 * NOV)
            for kind in ("diff", "dsa"):
                with act.Fori(0, UNITS) as u:
                    unit(kind, u)

            for r in range(4):
                for h in range(2):
                    act.wait_ge(row_ps, 2 * r + h + 1)
                    act.activation(rows[r][:, BANK * h:BANK * (h + 1)], PS[:, 2 * (r % 2) + h, :], ACT.Copy
                                   ).then_inc(row_sb, 1)
            for t in range(T + 2):
                if t < T:
                    act.wait_ge(x2_done, t + 1)
                    if t:
                        act.wait_ge(x2_sq, t)
                    act.activation(junk, XT[:, t, :], ACT.Square, accum_out=ss[:, 2 * T + t:2 * T + t + 1]
                                   ).then_inc(x2_sq, 1)
                if t >= 2:
                    for h in range(2):
                        act.wait_ge(h2T_ps, 2 * (t - 2) + h + 1)
                        if t >= 4:
                            act.wait_ge(lg_ps, t - 3)
                        act.activation(h2T[:, t % 2, BANK * h:BANK * (h + 1)], PS[:, 4 + h, :], ACT.Copy
                                       ).then_inc(h2T_sb, 1)
            act.wait_ge(gmax_done, 1)
            act.activation(gx, gx, ACT.Exp).then_inc(gexp_done, 1)
            act.wait_ge(e2_in, 1)
            act.activation(rt[:, 3, :], rt[:, 3, :], ACT.Exp).then_inc(e2_done, 1)

            def ev_t(e, b):
                act.wait_ge(t_ps, e + 1)
                if not isinstance(e, int) or e >= 2:
                    act.wait_ge(gu_ps, e - 1)
                act.activation(hgT[b][:, 0:BANK], PS[:, 0, :], ACT.Copy).then_inc(t_act, 1)

            def ev_sg(e, b):
                act.wait_ge(gu_ps, e + 1)
                if not isinstance(e, int) or e >= 2:
                    act.wait_ge(hid_done, e - 1)
                act.activation(sg[b], PS[:, 2 + b, 0:DE], ACT.Sigmoid).then_inc(sg_done, 1)

            def ev_h(e, b):
                act.wait_ge(ht_ps, e + 1)
                if not isinstance(e, int) or e >= 2:
                    act.wait_ge(dn_ps, e - 1)
                act.activation(hidT[b], PS[:, 4 + 3 * b, 0:DE], ACT.Copy).then_inc(ht_sb, 1)

            def ev_y(e, b, stored):
                act.wait_ge(dn_ps, e + 1)
                act.wait_ge(y_out[b], stored * 16)
                act.activation(ysb[b][:, 0:BANK], PS[:, 5, :], ACT.Copy).then_inc(y_act, 1)

            ev_t(0, 0)
            ev_sg(0, 0)
            ev_t(1, 1)
            for e in range(2):
                ev_h(e, e)
                ev_sg(e + 1, (e + 1) % 2)
                ev_t(e + 2, e % 2)
                ev_y(e, e, 0)
            with act.Fori(1, NE // 2 - 1) as i:
                for b in range(2):
                    e = 2 * i + b
                    ev_h(e, b)
                    ev_sg(e + 1, 1 - b)
                    ev_t(e + 2, b)
                    ev_y(e, b, i)
            for b in range(2):
                e = NE - 2 + b
                ev_h(e, b)
                if b == 0:
                    ev_sg(e + 1, 1)
                ev_y(e, b, NE // 2 - 1)
            n_ov = act.value_load(ovi[0:1, NOV:NOV + 1], min_val=0, max_val=NOV)
            with act.Fori(0, NOV) as j:
                with act.If(n_ov > j):
                    act.wait_ge(ov["t_ps"], j + 2)
                    act.activation(hgT[0], PS[:, 0:2, :].rearrange("p a n -> p (a n)"), ACT.Copy
                                   ).then_inc(ov["t_sb"], 1)
                    act.wait_ge(ov["gu_ps"], j + 1)
                    act.activation(sg[0], PS[:, 2, 0:DE], ACT.Sigmoid).then_inc(ov["sg"], 1)
                    act.wait_ge(ov["ht_ps"], j + 1)
                    act.activation(hidT[0], PS[:, 4, 0:DE], ACT.Copy).then_inc(ov["ht_sb"], 1)
                    act.wait_ge(ov["dn_ps"], j + 1)
                    act.wait_ge(y_out[0], 16 * (NE // 2))
                    act.activation(ysb[0], PS[:, 5:7, :].rearrange("p a n -> p (a n)"), ACT.Copy
                                   ).then_inc(ov["y_sb"], 1)
            act.wait_ge(route_done, 1)
            act.dma_start(gfin, g_final.partition_broadcast(P)).then_inc(gf_in, 16)
            for t in range(T):
                act.wait_ge(cb_done, t + 1)
                if t:
                    act.wait_ge(fin_sq, t)
                act.activation(QKV[:, 0:D], XT[:, t, :], ACT.Square, accum_out=ss[:, 3 * T + t:3 * T + t + 1]
                               ).then_inc(fin_sq, 1)

        @block.vector
        def _(dve):
            start_at_one(dve, ("max_done", "pt_dve", "o_done"))
            link = Chain(dve, dchain)
            dve.wait_ge(small_in, 16 * 16)
            dve.wait_ge(cols_ps, 1)
            dve.tensor_copy(cols[:, :], PS[:, 6, 0:MODS + 3 * KC]).then_inc(cols_sb, 1)
            for i in range(2):
                dve.tensor_tensor_reduce(lamv[:, 2 * i, :], lamv[:, 2 * i, :], lamv[:, 2 * i + 1, :], 1.0, 0.0,
                                         ALU.mult, ALU.add, lam2[:, i:i + 1]).then_inc(lam_ready, 1)
            link(dve.tensor_scalar(gsub[:, :], gsub[:, :], 1.0 - LAM0, None, ALU.mult))
            dve.wait_ge(cols_sb, 1)
            dve.wait_ge(cexp_done, 1)
            link(dve.tensor_scalar(cexp[:, :], cexp[:, :], 1.0, None, ALU.add))
            link(dve.reciprocal(cexp[:, :], cexp[:, :]))
            dve.tensor_tensor(cact[:, :], cexp[:, :], cols[:, MODS:MODS + KC], ALU.mult).then_inc(cact_done, 1)
            dve.wait_ge(lam_exp, 1)
            link(dve.tensor_tensor(lam2[:, 0:1], lam2[:, 3:4], lam2[:, 2:3], ALU.subtract))
            link(dve.tensor_scalar(lam2[:, 0:1], lam2[:, 0:1], -LAM0, None, ALU.add))
            dve.wait_ge(rstd_done, 1)
            for t in range(T):
                dve.tensor_scalar(XT[:, t, :], XT[:, t, :], ss[:, t:t + 1], None, ALU.mult).then_inc(xn_done, 1)
            dve.wait_ge(ada_done, 4)
            link(dve.tensor_tensor(mod[:, 0:2 * KC], PS[:, 7, 0:2 * KC], cols[:, 0:2 * KC], ALU.add))
            link(dve.tensor_scalar(sc1[:, :], mod[:, KC:2 * KC], 1.0, None, ALU.add))
            link(dve.tensor_tensor(sc1[:, :], sc1[:, :], cols[:, MODS + KC:MODS + 2 * KC], ALU.mult))
            dve.tensor_copy(cexp[:, :], sc1[:, :]).then_inc(aff_done, 1)
            for g in range(1, 2 * KC, 2):
                dve.wait_ge(xt_ps, g + 1)
                dve.tensor_scalar(HT[:, g // 2, BANK:2 * BANK], PS[:, g % 4, :], sc1[:, g // 2:g // 2 + 1],
                                  mod[:, g // 2:g // 2 + 1], ALU.mult, ALU.add).then_inc(xt_dve, 1)
            for t in range(T):
                dve.wait_ge(lat_ps, t + 1)
                dve.tensor_copy(ckv[:, LAT * t:LAT * (t + 1)], PS[:, 4 + t % 2, 0:LAT]).then_inc(lat_sb, 1)
                dve.tensor_scalar(iw[:, t, :], PS[:, 4 + t % 2, LAT:LAT + IH], IH ** -0.5, None, ALU.mult
                                  ).then_inc(lat_sb, 1)
            dve.wait_ge(lat_rstd, 1)
            for t in range(T):
                dve.scalar_tensor_tensor(out=ckv[:, LAT * t:LAT * (t + 1)], in0=ckv[:, LAT * t:LAT * (t + 1)],
                                         scalar=ss[:, T + t:T + t + 1], in1=gkv[:, :], op0=ALU.mult, op1=ALU.mult
                                         ).then_inc(ckv_done, 1)
            dve.wait_ge(lat_sb, 2 * T)
            for n in range(IH * NS):
                t, h = sel_tiles[n // IH], n % IH
                w = P * (t + 1)
                dst = SC[:, sc_off[t]:sc_off[t] + w]
                dve.wait_ge(ix_relu, n + 1)
                if h == 0:
                    dve.tensor_scalar(dst, RL[:, n % 2, 0:w], iw[:, t, h:h + 1], None, ALU.mult).then_inc(ix_acc, 1)
                else:
                    dve.wait_ge(ix_acc, n)
                    dve.scalar_tensor_tensor(out=dst, in0=RL[:, n % 2, 0:w], scalar=iw[:, t, h:h + 1], in1=dst,
                                             op0=ALU.mult, op1=ALU.add).then_inc(ix_acc, 1)

            u_, bit, trial, mask, thr, keep = (tk[:, i, :] for i in range(6))
            link(dve.memset(u_.bitcast(F32), 0.0))
            link(dve.memset(bit.bitcast(F32), -0.0))
            dve.wait_ge(ix_mask, NS)

            def threshold(src):
                link(dve.tensor_scalar(mask.bitcast(I32), src.bitcast(I32), 31, -1, ALU.arith_shift_right,
                                       ALU.bitwise_xor))
                link(dve.scalar_tensor_tensor(out=thr.bitcast(I32), in0=mask.bitcast(I32), scalar=-2147483648,
                                              in1=src.bitcast(I32), op0=ALU.bitwise_or, op1=ALU.bitwise_xor))

            with dve.Fori(0, 32) as it:
                link.loop(it, 6 + NS)
                link(dve.tensor_tensor(trial, u_, bit, ALU.bitwise_or))
                threshold(trial)
                for i, t in enumerate(sel_tiles):
                    w = P * (t + 1)
                    if i >= 3:
                        dve.wait_ge(dchain, link.base + (link.n + i - 2))
                    dve.tensor_scalar(BIAS[:, i % 3, 0:w], SC[:, sc_off[t]:sc_off[t] + w],
                                      thr.bitcast(F32)[:, i:i + 1], 0.0, ALU.is_ge, ALU.add,
                                      accum_out=cnt[:, 0, i:i + 1]).then_inc(dchain, 1)
                link.n += NS
                dve.wait_ge(dchain, link.base + link.n)
                link(dve.tensor_scalar(keep, cnt[:, 0, :], float(TOPK), None, ALU.is_ge))
                settle(dve)
                link(dve.copy_predicated(u_, keep, trial))
                link(dve.tensor_scalar(bit, bit, 1, None, ALU.logical_shift_right))
            link.leave(32)
            threshold(u_)
            for i, t in enumerate(sel_tiles):
                w = P * (t + 1)
                sc = SC[:, sc_off[t]:sc_off[t] + w]
                above, on, run = (BIAS[:, a, 0:w] for a in range(3))
                th = thr.bitcast(F32)[:, i:i + 1]
                link(dve.tensor_scalar(above, sc, th, 0.0, ALU.is_gt, ALU.add, accum_out=cnt[:, 1, i:i + 1]))
                link(dve.tensor_scalar(on, sc, th, None, ALU.is_equal))
                link(dve.tensor_tensor_scan(run, dist(t), on, 0.0, ALU.max, ALU.add))
                link(dve.tensor_scalar(cnt[:, 1, i:i + 1], cnt[:, 1, i:i + 1], -1.0, float(TOPK), ALU.mult, ALU.add))
                link(dve.scalar_tensor_tensor(out=run, in0=run, scalar=cnt[:, 1, i:i + 1], in1=on, op0=ALU.is_le,
                                              op1=ALU.mult))
                link(dve.tensor_tensor(run, run, above, ALU.add))
                link(dve.tensor_scalar(run, run, -1.0, -NEG, ALU.add, ALU.mult))
                link(dve.tensor_tensor(sc, run, dist(t), ALU.add))
            dve.wait_ge(mod_copied, 1)
            link(dve.tensor_tensor(mod[:, 2 * KC:MODS], mod[:, 2 * KC:MODS], cols[:, 2 * KC:MODS], ALU.add))
            link(dve.tensor_scalar(mod[:, 4 * KC:5 * KC], mod[:, 4 * KC:5 * KC], 1.0, None, ALU.add))
            link(dve.tensor_tensor(mod[:, 4 * KC:5 * KC], mod[:, 4 * KC:5 * KC], cols[:, MODS + 2 * KC:MODS + 3 * KC],
                                   ALU.mult))
            dve.tensor_copy(cexp[:, :], mod[:, 4 * KC:5 * KC]).then_inc(sel_done, 1)

            def unit(kind, u):
                s = at_s[kind]
                done = [0]
                for k in range(T):
                    done.append(done[-1] + len(groups_of(T - 1 - k)))

                def score(k, m):
                    w = P * (T - k)
                    dve.wait_ge(s["qk_done"], u * 16 + 2 * k + m + 2)
                    dve.wait_ge(s["bias_ready"], (u + 1 if kind == "diff" else u * 16 + 2 * k + m + 1) + 1)
                    dve.wait_ge(s["tr_done"], u * 24 + done[max(k - 1, 0)] + 1)
                    settle(dve)
                    bias = BIAS[:, 0, S - w:S] if kind == "diff" else BIAS[:, (2 * k + m) % 3, 0:w]
                    dve.tensor_tensor_reduce(
                        SP_[:, k % 2, m, 0:w],
                        PS[:, 2 * m:2 * m + 2, :].rearrange("p a n -> p (a n)")[:, 0:w], bias, -1.0, 3.0e38,
                        ALU.add, ALU.min, nmx[:, k % 2, m:m + 1]).then_inc(s["max_done"], 1)

                def norm(k):
                    a, b = k % 2, 6 + k % 2
                    dve.wait_ge(s["pv_done"], u * 24 + done[k + 1] + 1)
                    dve.wait_ge(s["ot_done"], u * T + max(k - 1, 0) + 1)
                    link(dve.reciprocal(rin[:, a, :], rs[:, a, :]))
                    if kind == "dsa":
                        for m in range(2):
                            dve.tensor_scalar(osb[:, a, DH * m:DH * (m + 1)], PS[:, b, DH * m:DH * (m + 1)],
                                              rin[:, a, m:m + 1], None, ALU.mult).then_inc(s["o_done"], 1)
                        return
                    link(dve.tensor_scalar(rin[:, a, 1:2], rin[:, a, 1:2], lam2[:, 0:1], None, ALU.mult))
                    link(dve.tensor_scalar(osb[:, a, :], PS[:, b, 0:DV], rin[:, a, 0:1], None, ALU.mult))
                    dve.scalar_tensor_tensor(out=osb[:, a, :], in0=PS[:, b, DV:2 * DV], scalar=rin[:, a, 1:2],
                                             in1=osb[:, a, :], op0=ALU.mult, op1=ALU.add).then_inc(s["o_done"], 1)

                def sub_norm(k):
                    dve.wait_ge(s["o_rstd"], u * T + k + 2)
                    dve.scalar_tensor_tensor(out=osb[:, k % 2, :], in0=osb[:, k % 2, :],
                                             scalar=oss[:, 2 + k % 2:3 + k % 2], in1=gsub[:, :], op0=ALU.mult,
                                             op1=ALU.mult).then_inc(s["o_done"], 1)

                score(0, 0)
                score(0, 1)
                for k in range(T):
                    gs = groups_of(T - 1 - k)
                    for i in range(1, len(gs), 2):
                        g = done[k] + i
                        _, b0, b1 = gs[i]
                        dve.wait_ge(s["tr_done"], u * 24 + g + 2)
                        dve.wait_ge(s["pv_done"], u * 24 + max(g - 3, 0) + 1)
                        dve.tensor_copy(PT[:, g % 4, 0:P * (b1 - b0)], PS[:, 4 + g % 2, 0:P * (b1 - b0)]
                                        ).then_inc(s["pt_dve"], 1)
                        if k + 1 < T and i == 1:
                            score(k + 1, 0)
                    if k + 1 < T:
                        score(k + 1, 1)
                    if kind == "diff" and k:
                        sub_norm(k - 1)
                    norm(k)
                if kind == "diff":
                    sub_norm(T - 1)

            dve.wait_ge(fill_out, 16 * NOV)
            for kind in ("diff", "dsa"):
                with dve.Fori(0, UNITS) as u:
                    link.loop(u, 3 * T if kind == "diff" else T)
                    unit(kind, u)
                link.leave(UNITS)

            for r, c0 in enumerate((2 * KC, 4 * KC, 3 * KC, 5 * KC)):
                if r >= 2:
                    dve.wait_ge(row_ps, 2 * r - 2)
                for j in range(KC):
                    dve.tensor_scalar(diag[:, r % 2, j, :], ident[:, :], mod[:, c0 + j:c0 + j + 1], None, ALU.mult
                                      ).then_inc(diag_done, 1)
            dve.wait_ge(row_sb, 8)
            dve.wait_ge(x2_in, 16 * T)
            for t in range(T + 3):
                if t < T:
                    for h in range(2):
                        n = 2 * t + h
                        part = slice(BANK * h, BANK * (h + 1))
                        dve.wait_ge(op_ps, n + 1)
                        if n >= 2:
                            dve.wait_ge(x2_half, n - 1)
                        dve.tensor_tensor(proj[:, h, :], PS[:, n % 4, :], rows[0][:, part], ALU.mult
                                          ).then_inc(op_sb, 1)
                        dve.wait_ge(op_sb, n + 1)
                        ins = dve.tensor_tensor(XT[:, t, part], proj[:, h, :], XT[:, t, part], ALU.add)
                        ins.then_inc(x2_half, 1)
                    dve.wait_ge(x2_half, 2 * t + 2)
                    dve.sem_inc(x2_done, 1)
                if 1 <= t <= T:
                    q = t - 1
                    if q >= 2:
                        dve.wait_ge(h2_out[q % 2], 16 * (q // 2))
                        dve.wait_ge(h2T_ps, 2 * (q - 1))
                    dve.wait_ge(x2_rstd, q + 1)
                    link(dve.scalar_tensor_tensor(out=h2[:, q % 2, :], in0=XT[:, q, :],
                                                  scalar=ss[:, 2 * T + q:2 * T + q + 1], in1=rows[1], op0=ALU.mult,
                                                  op1=ALU.mult))
                    dve.tensor_tensor(h2[:, q % 2, :], h2[:, q % 2, :], rows[2], ALU.add).then_inc(h2_done, 1)
                if t >= 3:
                    q = t - 3
                    dve.wait_ge(lg_ps, q + 1)
                    dve.tensor_tensor(logits[:, q, :], PS[:, 6 + q % 2, 0:NR], bgr[:, :], ALU.add
                                      ).then_inc(lg_sb, 1)

            def over(a, n):
                return a.unsqueeze(2).to_broadcast([P, T, n])

            gl, el = logits[:, :, 0:NG], logits[:, :, NG:NR]
            pg, v1, v2, e2, key, w1, w2 = (rt[:, i, :] for i in (0, 1, 2, 3, 4, 5, 6))
            tile_of, row_of = [rt[:, 7, :], rt[:, 8, :]], [rt[:, 9, :], rt[:, 10, :]]
            em, tmp, tmp2, carry, fl, tl = rbig[0], rbig[1], rbig[2], rbig[5], rbig[6], rbig[7]
            pick = [rbig[3], rbig[4]]
            down = iota_t[:, 0:NE].unsqueeze(1)
            dve.wait_ge(lg_sb, T)
            dve.wait_ge(op_ps, 2 * T)
            link(dve.tensor_reduce(v1, gl, AX_X, ALU.max))
            link(dve.tensor_tensor(gx, gl, over(v1, NG), ALU.subtract))
            link(dve.tensor_scalar(gk, gx, 0.0, None, ALU.is_ge))
            link(dve.tensor_scalar(tmp2[:, 0, :], iota_t[:, 0:NE], -1.0, float(NE), ALU.mult, ALU.add))
            link(dve.tensor_tensor(gk, gk, tmp2[:, 0, 0:NG].unsqueeze(1).to_broadcast([P, T, NG]), ALU.mult))
            link(dve.tensor_reduce(key, gk, AX_X, ALU.max))
            link(dve.tensor_tensor(gk, gk, over(key, NG), ALU.is_equal))
            dve.sem_inc(gmax_done, 1)
            dve.wait_ge(gexp_done, 1)
            link(dve.tensor_reduce(pg, gx, AX_X, ALU.add))
            link(dve.reciprocal(pg, pg))
            link(dve.tensor_scalar(gk, gk, -1.0, -NEG, ALU.add, ALU.mult))
            link(dve.tensor_tensor(em.rearrange("p t (g e) -> p t g e", g=NG),
                                   el.rearrange("p t (g e) -> p t g e", g=NG),
                                   gk.unsqueeze(3).to_broadcast([P, T, NG, EPG]), ALU.add))
            fall = rbig[8]
            for t in range(T):
                dve.tensor_scalar(fall[:, t, :], iota_t[:, 0:NE], -1.0, float(NE), ALU.mult, ALU.add
                                  ).then_inc(dchain, 1)
            link.n += T
            dve.wait_ge(dchain, link.n)
            for k, v in enumerate((v1, v2)):
                link(dve.tensor_reduce(v, em, AX_X, ALU.max))
                link(dve.tensor_tensor(tmp, em, over(v, NE), ALU.is_equal))
                link(dve.tensor_tensor(tmp, tmp, fall, ALU.mult))
                link(dve.tensor_reduce(key, tmp, AX_X, ALU.max))
                link(dve.tensor_tensor(pick[k], tmp, over(key, NE), ALU.is_equal))
                if k == 0:
                    link(dve.scalar_tensor_tensor(out=em.rearrange("p t e -> p (t e)"),
                                                  in0=pick[0].rearrange("p t e -> p (t e)"), scalar=2 * NEG,
                                                  in1=em.rearrange("p t e -> p (t e)"), op0=ALU.mult, op1=ALU.add))
            dve.tensor_tensor(e2, v2, v1, ALU.subtract).then_inc(e2_in, 1)
            dve.tensor_tensor(rbig[9], pick[0], pick[1], ALU.add).then_inc(sel_in, 1)
            dve.wait_ge(e2_done, 1)
            link(dve.tensor_scalar(w1, e2, 1.0, None, ALU.add))
            link(dve.reciprocal(w1, w1))
            link(dve.tensor_tensor(w1, w1, pg, ALU.mult))
            link(dve.tensor_tensor(w2, w1, e2, ALU.mult))
            dve.wait_ge(sel_ps, 1)
            rank, total = PS[:, 0, 0:T * NE], PS[:, 1, 0:T * NE].rearrange("p (t e) -> p t e", t=T)
            link(dve.memset(carry[:, 0, :], 0.0))
            for t in range(1, T):
                link(dve.tensor_tensor(carry[:, t, :], carry[:, t - 1, :], total[:, t - 1, :], ALU.add))
            n_e, n_ov, ov_end, ov_base = (ovc[:, i, :] for i in range(4))
            link(dve.tensor_tensor(n_e, carry[:, T - 1, :], total[:, T - 1, :], ALU.add))
            flat = lambda a: a.rearrange("p t e -> p (t e)")
            link(dve.tensor_tensor(flat(tmp), rank, flat(carry), ALU.add))
            link(dve.tensor_scalar(flat(fl), flat(tmp), float(P), None, ALU.is_ge))
            link(dve.tensor_scalar(n_ov, n_e, float(P), None, ALU.is_gt))
            for m in range(2, T):
                link(dve.scalar_tensor_tensor(out=flat(fl), in0=flat(tmp), scalar=float(P * m), in1=flat(fl),
                                              op0=ALU.is_ge, op1=ALU.add))
                link(dve.scalar_tensor_tensor(out=n_ov, in0=n_e, scalar=float(P * m), in1=n_ov, op0=ALU.is_gt,
                                              op1=ALU.add))
            link(dve.memset(ovc[:, 4, :], 0.0))
            link(dve.tensor_tensor_scan(ov_end, ovc[:, 4, :], n_ov, 0.0, ALU.add, ALU.add))
            link(dve.tensor_tensor(ov_base, ov_end, n_ov, ALU.subtract))
            link(dve.scalar_tensor_tensor(out=flat(tmp2), in0=flat(fl), scalar=-float(P), in1=flat(tmp),
                                          op0=ALU.mult, op1=ALU.add))
            link(dve.tensor_scalar(ov_base, ov_base, float(NE - 1), None, ALU.add))
            link(dve.tensor_tensor(ov_base, ov_base, iota_t[:, 0:NE], ALU.subtract))
            link(dve.tensor_tensor(tl, fl, ov_base.unsqueeze(1).to_broadcast([P, T, NE]), ALU.add))
            link(dve.tensor_scalar(flat(fl), flat(fl), 1.0, None, ALU.min))
            link(dve.tensor_tensor(tl, tl, fl, ALU.mult))
            link(dve.tensor_tensor(tl, tl, down.to_broadcast([P, T, NE]), ALU.add))
            for k in range(2):
                for src, dst in ((tl, tile_of[k]), (tmp2, row_of[k])):
                    link(dve.tensor_tensor(tmp, src, pick[k], ALU.mult))
                    link(dve.tensor_reduce(dst, tmp, AX_X, ALU.add))
                link(dve.scalar_tensor_tensor(out=key, in0=tile_of[k], scalar=float(P), in1=row_of[k],
                                              op0=ALU.mult, op1=ALU.add))
                link(dve.tensor_copy(slot[:, k, :], key))
            for k in range(2):
                for t in range(T):
                    i = k * T + t
                    dve.tensor_scalar(ohr[i], iota_p[:, :], row_of[k][:, t:t + 1], None, ALU.is_equal
                                      ).then_inc(oh_done, 1)
                    dve.tensor_scalar(oht[i], iota_t[:, :], tile_of[k][:, t:t + 1], tok[:, t:t + 1], ALU.is_equal,
                                      ALU.mult).then_inc(oh_done, 1)
            link(dve.tensor_tensor(ovt, ov_end.unsqueeze(1).to_broadcast([P, NOV + 1, NE]),
                                   iota_t[:, 0:NOV + 1].unsqueeze(2).to_broadcast([P, NOV + 1, NE]), ALU.is_le))
            link(dve.tensor_reduce(ovx[:, 0:NOV + 1], ovt, AX_X, ALU.add))
            link(dve.tensor_scalar(ovx[:, 0:NOV], ovx[:, 0:NOV], float(NE - 1), None, ALU.min))
            link(dve.tensor_copy(ovx[:, NOV:NOV + 1], ov_end[:, NE - 1:NE]))
            link(dve.tensor_copy(ovi[:, :], ovx[:, 0:NOV + 1]))
            dve.wait_ge(lst_ps, 1)
            dve.tensor_copy(lst[:, :], PS[:, 2, 0:NT]).then_inc(route_done, 1)

            def ev_t(e, b):
                dve.wait_ge(t_ps, e + 1)
                if not isinstance(e, int) or e >= 2:
                    dve.wait_ge(gu_ps, e - 1)
                dve.tensor_copy(hgT[b][:, BANK:2 * BANK], PS[:, 1, :]).then_inc(t_dve, 1)

            def ev_hid(e, b):
                dve.wait_ge(sg_done, e + 1)
                if not isinstance(e, int) or e >= 1:
                    dve.wait_ge(hid_done, e)
                if not isinstance(e, int) or e >= 2:
                    dve.wait_ge(ht_ps, e - 1)
                dve.tensor_tensor(hh, PS[:, 2 + b, 0:DE], sg[b], ALU.mult).then_inc(hh_done, 1)
                dve.wait_ge(hh_done, e + 1)
                dve.tensor_tensor(hid[b], hh, PS[:, 2 + b, DE:2 * DE], ALU.mult).then_inc(hid_done, 1)

            def ev_y(e, b, stored):
                dve.wait_ge(dn_ps, e + 1)
                dve.wait_ge(y_out[b], stored * 16)
                dve.tensor_copy(ysb[b][:, BANK:2 * BANK], PS[:, 6, :]).then_inc(y_dve, 1)

            ev_t(0, 0)
            ev_hid(0, 0)
            ev_t(1, 1)
            for e in range(2):
                ev_hid(e + 1, (e + 1) % 2)
                ev_t(e + 2, e % 2)
                ev_y(e, e, 0)
            with dve.Fori(1, NE // 2 - 1) as i:
                for b in range(2):
                    e = 2 * i + b
                    ev_hid(e + 1, 1 - b)
                    ev_t(e + 2, b)
                    ev_y(e, b, i)
            ev_hid(NE - 1, 1)
            ev_y(NE - 2, 0, NE // 2 - 1)
            ev_y(NE - 1, 1, NE // 2 - 1)
            n_ov = dve.value_load(ovi[0:1, NOV:NOV + 1], min_val=0, max_val=NOV)
            with dve.Fori(0, NOV) as j:
                with dve.If(n_ov > j):
                    dve.wait_ge(ov["sg"], j + 1)
                    dve.tensor_tensor(hh, PS[:, 2, 0:DE], sg[0], ALU.mult).then_inc(ov_hh, 1)
                    dve.wait_ge(ov_hh, j + 1)
                    dve.tensor_tensor(hid[0], hh, PS[:, 2, DE:2 * DE], ALU.mult).then_inc(ov["hid"], 1)

            for t in range(T):
                y1, y2 = yg[t % 2]
                dve.wait_ge(yg_in[t % 2], 32 * (t // 2 + 1))
                link(dve.tensor_scalar(y1, y1, w1[:, t:t + 1], None, ALU.mult))
                link(dve.scalar_tensor_tensor(out=y1, in0=y2, scalar=w2[:, t:t + 1], in1=y1, op0=ALU.mult,
                                              op1=ALU.add))
                link(dve.tensor_tensor(y1, y1, rows[3], ALU.mult))
                dve.tensor_tensor(XT[:, t, :], XT[:, t, :], y1, ALU.add).then_inc(cb_done, 1)
            dve.wait_ge(gf_in, 16)
            for t in range(T):
                dve.wait_ge(fin_rstd, t + 1)
                dve.scalar_tensor_tensor(out=XT[:, t, :], in0=XT[:, t, :], scalar=ss[:, 3 * T + t:3 * T + t + 1],
                                         in1=gfin, op0=ALU.mult, op1=ALU.mult).then_inc(fin_done, 1)

        @block.tensor
        def _(pe):
            start_at_one(pe, ("qk_done", "tr_done", "pv_done", "ot_done"))
            pe.sem_inc(ov["t_ps"], 1)
            pe.wait_ge(consts, 8)
            pe.wait_ge(small_in, 16 * 16)
            nv = MODS + 3 * KC
            pe.transpose(PS[:, 6, 0:nv], vrows, ident[0:nv, 0:nv]).then_inc(cols_ps, 1)

            def ada_chunk(b, column):
                for q in range(4):
                    for j in range(KC):
                        last = pe.matmul(PS[:, 7, bass.ds(column(q), 1)], ada[b][:, j, P * q:P * (q + 1)],
                                         cact[:, j:j + 1], start=(j == 0), stop=(j == KC - 1))
                last.then_inc(ada_done, 1)

            pe.wait_ge(cact_done, 1)
            for b in range(4):
                pe.wait_ge(ada_in[b], 16)
                ada_chunk(b, lambda q: 4 * b + q)
            pe.wait_ge(xn_done, T)
            for g in range(2 * KC):
                j, half = g // 2, g % 2
                if g >= 4:
                    pe.wait_ge(xt_act if half == 0 else xt_dve, (g - 4) // 2 + 1)
                for i in range(4):
                    last = pe.transpose(PS[:, g % 4, P * i:P * (i + 1)], XT[:, 4 * half + i, P * j:P * (j + 1)],
                                        ident[:, :])
                last.then_inc(xt_ps, 1)
            pe.wait_ge(xt_act, KC)
            pe.wait_ge(xt_dve, KC)
            pe.wait_ge(wcopy, 6)
            for n in range(4):
                for j in range(KC):
                    last = pe.matmul(PS[:, n, :], WI[:, j, LAT:LAT + P] if n < 2 else WIK[:, j, :],
                                     HT[:, j, BANK * (n % 2):BANK * (n % 2 + 1)], start=(j == 0), stop=(j == KC - 1))
                last.then_inc(iqk_ps, 1)
            for t in range(T):
                if t >= 2:
                    pe.wait_ge(lat_sb, 2 * (t - 1))
                for j in range(KC):
                    last = pe.matmul(PS[:, 4 + t % 2, 0:LAT + IH], HT[:, j, P * t:P * (t + 1)], WD[:, j, :],
                                     start=(j == 0), stop=(j == KC - 1))
                last.then_inc(lat_ps, 1)
            pe.wait_ge(iqk_sb, 4)
            for n in range(IH * NS):
                t, h = sel_tiles[n // IH], n % IH
                w = P * (t + 1)
                if n >= 2:
                    pe.wait_ge(ix_relu, n - 1)
                for c0 in range(0, w, BANK):
                    c1 = min(c0 + BANK, w)
                    last = pe.matmul(PS[:, 2 * (n % 2) + c0 // BANK, 0:c1 - c0], iqT[ID * h:ID * (h + 1), P * t:P * (t + 1)],
                                     ikT[ID * h:ID * (h + 1), c0:c1], start=True, stop=True)
                last.then_inc(ix_ps, 1)
            pe.wait_ge(ckv_done, T)
            for n in range(2):
                for i in range(4):
                    last = pe.transpose(PS[:, 4 + n, P * i:P * (i + 1)], ckv[:, P * (4 * n + i):P * (4 * n + i + 1)],
                                        ident[:, :])
                last.then_inc(ckvT_ps, 1)
            with pe.Fori(1, 3) as a:
                for b in range(4):
                    pe.wait_ge(ada_in[b], a * 16 + 16)
                    ada_chunk(b, lambda q: a * 16 + (4 * b + q))
            pe.wait_ge(ckvT_sb, 2)
            for n in range(2 * UNITS):
                if n >= 2:
                    pe.wait_ge(kv_sb, n - 1)
                pe.matmul(PS[:, 4 + n % 2, :], wuk[:, n // 2 * 2:n // 2 * 2 + 2, :].rearrange("p h d -> p (h d)"),
                          ckvT[:, BANK * (n % 2):BANK * (n % 2 + 1)], start=True, stop=True).then_inc(kv_ps, 1)
            for t in range(T):
                pe.wait_ge(kv_sb, 2 * UNITS + t - 1)
                pe.matmul(PS[:, 4 + t % 2, :], ckvT[:, P * t:P * (t + 1)],
                          wuv[:, :, :].rearrange("p h d -> p (h d)"), start=True, stop=True).then_inc(kv_ps, 1)

            def project(b, half):
                for j in range(KC):
                    last = pe.matmul(PS[:, 2 * b + half, :], WS[:, b, j, :], HT[:, j, BANK * half:BANK * (half + 1)],
                                     start=(j == 0), stop=(j == KC - 1))
                last.then_inc(pj_ps, 1)

            def project_rows(b, half):
                for i in range(4):
                    t = 4 * half + i
                    for j in range(KC):
                        last = pe.matmul(PS[:, 2 * b + half, P * i:P * (i + 1)], HT[:, j, P * t:P * (t + 1)],
                                         WS[:, b, j, :], start=(j == 0), stop=(j == KC - 1))
                last.then_inc(pj_ps, 1)

            pe.wait_ge(ix_relu, IH * NS)
            for b in range(2):
                pe.wait_ge(ws_in[b], 16)
                for half in range(2):
                    project(b, half)
            for a0, a1, what in ((1, 6, project), (6, 8, project_rows)):
                with pe.Fori(a0, a1) as a:
                    for b in range(2):
                        pe.wait_ge(ws_in[b], a * 16 + 16)
                        for half in range(2):
                            pe.wait_ge(pj_sb, a * 4 + (2 * b + half - 3))
                            what(b, half)
            pe.wait_ge(kv_sb, 2 * UNITS + T)
            pe.wait_ge(pj_sb, 32)

            def unit(kind, u):
                s = at_s[kind]
                width = DH if kind == "dsa" else DV
                done = [0]
                for k in range(T):
                    done.append(done[-1] + len(groups_of(T - 1 - k)))

                def qk(k, m):
                    t, w = T - 1 - k, P * (T - k)
                    pe.wait_ge(s["max_done"], u * 16 + max(2 * k + m - 1, 0) + 1)
                    for c0 in range(0, w, BANK):
                        c1 = min(c0 + BANK, w)
                        last = pe.matmul(PS[:, 2 * m + c0 // BANK, 0:c1 - c0],
                                         qst[DH * m:DH * (m + 1), P * t:P * (t + 1)], kst[DH * m:DH * (m + 1), c0:c1],
                                         start=True, stop=True)
                    last.then_inc(s["qk_done"], 1)

                def turn(k, i):
                    g = done[k] + i
                    m, b0, b1 = groups_of(T - 1 - k)[i]
                    pe.wait_ge(s["exp_done"], u * 16 + 2 * k + m + 2)
                    pe.wait_ge(s["pt_dve" if g % 2 else "pt_act"], u * 12 + max(g // 2, 0) + 1)
                    for b in range(b0, b1):
                        last = pe.transpose(PS[:, 4 + g % 2, P * (b - b0):P * (b - b0 + 1)],
                                            SP_[:, k % 2, m, P * b:P * (b + 1)], ident[:, :])
                    last.then_inc(s["tr_done"], 1)

                def pv(k, i):
                    g = done[k] + i
                    m, b0, b1 = groups_of(T - 1 - k)[i]
                    if i == 0:
                        pe.wait_ge(s["ot_copied"], u * T + max(k - 1, 0) + 1)
                    pe.wait_ge(s["pt_dve" if g % 2 else "pt_act"], u * 12 + g // 2 + 2)
                    for b in range(b0, b1):
                        v = (vd[:, b, bass.ds(u * (2 * DH) + DH * m, DH)] if kind == "dsa"
                             else vf[:, bass.ds(u * S + P * b, DV)])
                        last = pe.matmul(PS[:, 6 + k % 2, width * m:width * (m + 1)],
                                         PT[:, g % 4, P * (b - b0):P * (b - b0 + 1)], v, start=(b == 0),
                                         stop=(b == T - 1 - k))
                    last.then_inc(s["pv_done"], 1)

                def turn_out(k):
                    pe.wait_ge(s["o_done"], u * 2 * T + 2 * k + 2 + 1)
                    pe.transpose(PS[:, 6 + k % 2, 256:384], osb[:, k % 2, :], ident[:, :]).then_inc(s["ot_done"], 1)

                pe.wait_ge(s["qk_loaded"], u * 4 + 4 + 1)
                qk(0, 0)
                qk(0, 1)
                for k in range(T):
                    four = len(groups_of(T - 1 - k)) == 4
                    turn(k, 0)
                    turn(k, 1)
                    if k + 1 < T:
                        qk(k + 1, 0)
                    pv(k, 0)
                    if four:
                        turn(k, 2)
                        pv(k, 1)
                        turn(k, 3)
                    if k + 1 < T:
                        qk(k + 1, 1)
                    for i in ((2, 3) if four else (1,)):
                        pv(k, i)
                    if k:
                        turn_out(k - 1)
                turn_out(T - 1)

            for kind in ("diff", "dsa"):
                with pe.Fori(0, UNITS) as u:
                    unit(kind, u)
                pe.wait_ge(at_s[kind]["ot_copied"], UNITS * T + 1)

            for r in range(4):
                pe.wait_ge(diag_done, KC * (r + 1))
                for h in range(2):
                    if r >= 2:
                        pe.wait_ge(row_sb, 2 * (r - 2) + h + 1)
                    for i in range(4):
                        last = pe.matmul(PS[:, 2 * (r % 2) + h, P * i:P * (i + 1)], ones[:, :],
                                         diag[:, r % 2, 4 * h + i, :], start=True, stop=True)
                    last.then_inc(row_ps, 1)
            pe.wait_ge(row_sb, 8)
            pe.wait_ge(wo_in, 16)
            for t in range(T + 3):
                if t < T:
                    for h in range(2):
                        n = 2 * t + h
                        if n >= 4:
                            pe.wait_ge(op_sb, n - 3)
                        for k in range(KC):
                            last = pe.matmul(PS[:, n % 4, :], HT[:, k, P * t:P * (t + 1)],
                                             wo[:, k, BANK * h:BANK * (h + 1)], start=(k == 0), stop=(k == KC - 1))
                        last.then_inc(op_ps, 1)
                if 2 <= t < T + 2:
                    q = t - 2
                    pe.wait_ge(h2_done, q + 1)
                    for h in range(2):
                        if q:
                            pe.wait_ge(h2T_sb, 2 * (q - 1) + h + 1)
                        for i in range(4):
                            last = pe.transpose(PS[:, 4 + h, P * i:P * (i + 1)],
                                                h2[:, q % 2, P * (4 * h + i):P * (4 * h + i + 1)], ident[:, :])
                        last.then_inc(h2T_ps, 1)
                if t >= 3:
                    q = t - 3
                    pe.wait_ge(h2T_sb, 2 * q + 2)
                    if q >= 2:
                        pe.wait_ge(lg_sb, q - 1)
                    for j in range(KC):
                        last = pe.matmul(PS[:, 6 + q % 2, 0:NR], h2T[:, q % 2, P * j:P * (j + 1)],
                                         wgr[:, j, :], start=(j == 0), stop=(j == KC - 1))
                    last.then_inc(lg_ps, 1)

            pe.wait_ge(sel_in, 1)
            chosen = rbig[9].rearrange("p t e -> p (t e)")
            pe.matmul(PS[:, 0, 0:T * NE], before[:, :], chosen, start=True, stop=True)
            pe.matmul(PS[:, 1, 0:T * NE], ones[:, :], chosen, start=True, stop=True).then_inc(sel_ps, 1)
            for i in range(2 * T):
                pe.wait_ge(oh_done, 2 * i + 2)
                last = pe.matmul(PS[:, 2, 0:NT], ohr[i], oht[i], start=(i == 0), stop=(i == 2 * T - 1))
            last.then_inc(lst_ps, 1)
            pe.wait_ge(route_done, 1)

            def turn_rows(e, b, arrived):
                pe.wait_ge(xg_in[b], arrived)
                if not isinstance(e, int) or e >= 1:
                    pe.wait_ge(t_act, e)
                    pe.wait_ge(t_dve, e)
                for c_ in range(KC):
                    last = pe.transpose(PS[:, c_ // 4, P * (c_ % 4):P * (c_ % 4 + 1)],
                                        xg[b].rearrange("p (k c) -> p c k", c=KC)[:, c_, :], ident[:, :])
                last.then_inc(t_ps, 1)

            def gate_up(e, b, w, arrived):
                pe.wait_ge(t_act, e + 1)
                pe.wait_ge(t_dve, e + 1)
                pe.wait_ge(w_in_s[w], arrived)
                if not isinstance(e, int) or e >= 2:
                    pe.wait_ge(hid_done, e - 1)
                for c_ in range(KC):
                    last = pe.matmul(PS[:, 2 + b, :], hgT[b][:, P * c_:P * (c_ + 1)], WGU[w][:, c_, :, :],
                                     start=(c_ == 0), stop=(c_ == KC - 1))
                last.then_inc(gu_ps, 1)

            def turn_hidden(e, b):
                pe.wait_ge(hid_done, e + 1)
                if not isinstance(e, int) or e >= 2:
                    pe.wait_ge(ht_sb, e - 1)
                for c_ in range(2):
                    last = pe.transpose(PS[:, 4 + 3 * b, P * c_:P * (c_ + 1)],
                                        hid[b].rearrange("p (k c) -> p c k", c=2)[:, c_, :], ident[:, :])
                last.then_inc(ht_ps, 1)

            def down_proj(e, b, w):
                pe.wait_ge(ht_sb, e + 1)
                if not isinstance(e, int) or e >= 1:
                    pe.wait_ge(y_act, e)
                    pe.wait_ge(y_dve, e)
                for h in range(2):
                    for c_ in range(2):
                        last = pe.matmul(PS[:, 5 + h, :], hidT[b][:, P * c_:P * (c_ + 1)],
                                         WDN[w][:, c_, BANK * h:BANK * (h + 1)], start=(c_ == 0), stop=(c_ == 1))
                last.then_inc(dn_ps, 1)

            def step(e, j, i, last2=None):
                b = j % 2
                turn_hidden(e, b)
                if last2 != 1:
                    w = (j + 1) % 4
                    gate_up(e + 1, 1 - b, w, (i + 1 + (j + 1) // 4) * 48)
                if last2 is None:
                    turn_rows(e + 2, b, (2 * i + (j + 2) // 2 + 1) * 16)
                down_proj(e, b, j)

            turn_rows(0, 0, 16)
            gate_up(0, 0, 0, 48)
            turn_rows(1, 1, 16)
            for j in range(4):
                step(j, j, 0)
            with pe.Fori(1, NE // 4 - 1) as i:
                for j in range(4):
                    step(i * 4 + j, j, i)
            for j in range(4):
                step(NE - 4 + j, j, NE // 4 - 1, None if j < 2 else j - 2)

            n_ov = pe.value_load(ovi[0:1, NOV:NOV + 1], min_val=0, max_val=NOV)
            with pe.Fori(0, NOV) as j:
                with pe.If(n_ov > j):
                    pe.wait_ge(y_act, NE)
                    pe.wait_ge(y_dve, NE)
                    pe.wait_ge(ov["xg_in"], j * 16 + 16)
                    for c_ in range(KC):
                        last = pe.transpose(PS[:, c_ // 4, P * (c_ % 4):P * (c_ % 4 + 1)],
                                            xg[0].rearrange("p (k c) -> p c k", c=KC)[:, c_, :], ident[:, :])
                    last.then_inc(ov["t_ps"], 1)
                    pe.wait_ge(ov["t_sb"], j + 1)
                    pe.wait_ge(ov["w_in"], j * 48 + 48)
                    for c_ in range(KC):
                        last = pe.matmul(PS[:, 2, :], hgT[0][:, P * c_:P * (c_ + 1)], WGU[0][:, c_, :, :],
                                         start=(c_ == 0), stop=(c_ == KC - 1))
                    last.then_inc(ov["gu_ps"], 1)
                    pe.wait_ge(ov["hid"], j + 1)
                    for c_ in range(2):
                        last = pe.transpose(PS[:, 4, P * c_:P * (c_ + 1)],
                                            hid[0].rearrange("p (k c) -> p c k", c=2)[:, c_, :], ident[:, :])
                    last.then_inc(ov["ht_ps"], 1)
                    pe.wait_ge(ov["ht_sb"], j + 1)
                    for h in range(2):
                        for c_ in range(2):
                            last = pe.matmul(PS[:, 5 + h, :], hidT[0][:, P * c_:P * (c_ + 1)],
                                             WDN[0][:, c_, BANK * h:BANK * (h + 1)], start=(c_ == 0), stop=(c_ == 1))
                    last.then_inc(ov["dn_ps"], 1)


_INS = ["x", "c", "w_ada", "b_ada", "g_attn", "w_in", "g_kv", "w_uk", "w_uv", "lam_q1", "lam_k1", "lam_q2", "lam_k2",
        "g_sub", "w_out", "g_moe", "w_group", "b_group", "w_router", "b_router", "w_gate", "w_up", "w_down", "g_final"]


def kernel(**inputs):
    import numpy as _np
    import concourse.bacc as _bacc
    from concourse import mybir as _mybir
    from concourse.bass_utils import run_bass_kernel_spmd as _run

    nc = _bacc.Bacc("TRN2", target_bir_lowering=False, num_devices=1)
    arrays, args = {}, []
    for name in _INS:
        a = _np.ascontiguousarray(inputs[name])
        arrays[f"in_{name}_dram"] = a
        args.append(nc.dram_tensor(f"in_{name}_dram", a.shape, _mybir.dt.from_np(a.dtype), kind="ExternalInput").ap())
    shape = inputs["x"].shape
    args.append(nc.dram_tensor("out_0_dram", shape, _mybir.dt.float32, kind="ExternalOutput").ap())
    hybrid_layer(nc, *args)
    r = _run(nc, [arrays], core_ids=[0])
    return r.results[0]["out_0_dram"]
```

```python
import math
from contextlib import ExitStack

import concourse.bass as bass
from concourse import mybir

F32 = mybir.dt.float32
I32 = mybir.dt.int32
U32 = mybir.dt.uint32
ALU = mybir.AluOpType
ACT = mybir.ActivationFunctionType
AX_X = mybir.AxisListType.X
P = 128
BANK = 512


def groups_of(t):
    return [(m, b, min(b + 4, t + 1)) for m in range(2) for b in range(0, t + 1, 4)]


def place(k):
    return (k % 3, 0) if k < 6 else (2, 384 if k == 6 else 640)


def bias_place(i):
    return (i % 3, 0) if i < 12 else ((2, 384), (2, 640), (2, 896), (1, 384))[i - 12]


def hybrid_layer(nc, x, c, w_ada, b_ada, g_attn, w_in, g_kv, w_uk, w_uv, lam_q1, lam_k1, lam_q2, lam_k2,
                 g_sub, w_out, g_moe, w_group, b_group, w_router, b_router, w_gate, w_up, w_down, g_final, out):
    _, S, D = x.shape
    T = S // P
    KC = D // P
    _, NH, LAT, DH = w_uk.shape
    DV = g_sub.shape[1]
    QD = lam_q1.shape[1]
    NG = w_group.shape[2]
    NE = w_router.shape[2]
    EPG = NE // NG
    NR = NG + NE
    DE = w_gate.shape[3]
    IH = 4
    ID = 32
    OFF_LAT = NH * DH
    OFF_FQ = OFF_LAT + LAT + IH * ID + ID + IH
    NIDX = OFF_FQ - OFF_LAT
    DIFF = (w_in.shape[2] - OFF_FQ) // 3
    NDIFF = DIFF // DV
    TOPK = min(256, S // 4)
    T0 = TOPK // P
    EPS = 1e-6
    LAM0 = 0.8 - 0.6 * math.exp(0.0)
    NEG = -1e30
    LOW = -3.0e38
    NOV = 2 * S // P
    NT = NE + NOV
    MODC = 2 * KC
    NROW = 6 * D // BANK - 4
    UNITS = 4
    AT = 5
    last = UNITS // 2 - 1
    assert last == 1
    DONE = [0]
    for k in range(T):
        DONE.append(DONE[-1] + len(groups_of(T - 1 - k)))
    assert D == 1024 and S == 1024 and DH == 64 and QD == 64 and DV == 128 and LAT == 128
    assert NH == 2 * UNITS and NDIFF == UNITS and DE == 256 and NE == 32 and NG == 4 and T0 == 2

    sel_tiles = list(range(T0, T))
    sc_off, at = {}, 0
    for t in sel_tiles:
        sc_off[t] = at
        at += P * (t + 1)
    SCW = at
    NS = len(sel_tiles)

    h2_dram = nc.dram_tensor("h2_rows", [S, D], F32, kind="Internal").ap()
    mod_dram = nc.dram_tensor("modulation_row", [1, NROW * BANK], F32, kind="Internal").ap()
    y_dram = nc.dram_tensor("expert_rows", [NT * P, D], F32, kind="Internal").ap()

    ctx = ExitStack()
    with ctx:
        def sb(name, shape, dt=F32):
            return ctx.enter_context(nc.sbuf_tensor(name, shape, dt))

        def sem(name):
            return ctx.enter_context(nc.semaphore(name))

        class Chain:

            def __init__(self, eng, s):
                self.eng, self.s, self.base, self.n = eng, s, 0, 0

            def __call__(self, ins):
                ins.then_inc(self.s, 1)
                self.n += 1
                self.eng.wait_ge(self.s, self.base + self.n)

            def loop(self, u, per):
                self.start = self.n if isinstance(self.base, int) and self.base == 0 else self.start
                self.base, self.n, self.per = self.start + u * per, 0, per

            def leave(self, times, late=0):
                assert self.n == self.per - late, (self.n, self.per, late)
                self.n, self.base = self.start + times * self.per - late, 0

        HT = sb("HT", [P, KC, S])
        QKV = sb("QKV", [P, 6 * 4096])
        X = sb("X", [P, 8192])
        SC = sb("SC", [P, SCW])
        BIAS = sb("BIAS", [P, 3, S])
        R = sb("R", [P, S])
        ident = sb("ident", [P, P])
        ones = sb("ones", [P, P])
        before = sb("before", [P, P])
        iota_p = sb("iota_p", [P, P])
        iota_t = sb("iota_t", [P, NT])
        tok = sb("tok", [P, T])
        neghalf = sb("neghalf", [P, T])
        slopes = sb("slopes", [P, 4])
        cols = sb("cols", [P, MODC + 2 * KC])
        cact = sb("cact", [P, KC])
        cexp = sb("cexp", [P, KC])
        mod = sb("mod", [P, MODC])
        sc1 = sb("sc1", [P, KC])
        ss = sb("ss", [P, 4 * T])
        gkv = sb("gkv", [P, LAT])
        gsub = sb("gsub", [P, DV])
        lam2 = sb("lam2", [P, 4])
        wuk = sb("wuk", [P, NH, DH])
        wuv = sb("wuv", [P, NH, DH])
        wgr = sb("wgr", [P, KC, NR])
        bgr = sb("bgr", [P, NR])
        iw = sb("iw", [P, T, IH])
        tk = sb("tk", [P, 6, NS], U32)
        cnt = sb("cnt", [P, 2, NS])
        nmx = sb("nmx", [P, 4, 2])
        rs = sb("rs", [P, 4, 2])
        rin = sb("rin", [P, 4, 2])
        osb = sb("osb", [P, 2, P])
        osq = sb("osq", [P, P])
        oss = sb("oss", [P, 4])
        logits = sb("logits", [P, T, NR])
        rt = sb("rt", [P, 14, T])
        lst = sb("lst", [P, NT], I32)
        slot = sb("slot", [P, 2, T], I32)
        idx = sb("idx", [P, 2], I32)
        ovi = sb("ovi", [P, NOV + 2], I32)
        PS = ctx.enter_context(nc.psum_tensor("PS", [P, 8, BANK], F32))

        vrows = BIAS[0:MODC + 2 * KC, 0, 0:P]
        lamv = BIAS[:, 1, 0:4 * QD].rearrange("p (a n) -> p a n", a=4)
        ada = [QKV[:, 4096 * i:4096 * (i + 1)].rearrange("p (j n) -> p j n", j=KC) for i in range(4)]
        WI = QKV[:, 4 * 4096:4 * 4096 + KC * NIDX].rearrange("p (j n) -> p j n", j=KC)
        brow = QKV[0:1, 18720:18720 + 2 * BANK].rearrange("p (a n) -> p a n", a=2)
        mrow = QKV[0:1, 22560:22560 + 2 * BANK].rearrange("p (a n) -> p a n", a=2)
        WIK = QKV[:, 5 * 4096:5 * 4096 + KC * P].rearrange("p (j n) -> p j n", j=KC)
        WD = QKV[:, 5 * 4096 + 1024:5 * 4096 + 1024 + KC * (LAT + IH)].rearrange("p (j n) -> p j n", j=KC)
        XT = X[:, :].rearrange("p (t d) -> p t d", t=T)
        iqT, ikT = X[:, 0:S], X[:, S:2 * S]
        ckvT, ckv = X[:, 0:S], X[:, 2 * S:3 * S]
        RL = X[:, 3 * S:5 * S].rearrange("p (a n) -> p a n", a=2)
        WS = X[:, 5 * S:7 * S].rearrange("p (a j n) -> p a j n", a=2, j=KC)
        zero_rows = X[:, 7 * S:8 * S]
        k_at = {"dsa": 0, "diff": 4 * 4096}
        q_at = {"dsa": 2 * 4096, "diff": 3 * 4096}
        vd = QKV[:, 4096:2 * 4096].rearrange("p (t n) -> p t n", t=T)
        vf = QKV[:, 5 * 4096:6 * 4096]
        HF = HT[:, :, :].rearrange("p k n -> p (k n)")
        more = {"diff": HF[:, 0:4 * S], "dsa": QKV[:, 5 * 4096:6 * 4096]}
        sc_buf = {kind: [X[:, 0:2 * S], X[:, 2 * S:4 * S], m[:, 0:2 * S]] for kind, m in more.items()}
        qst = {kind: [X[:, 4 * S:5 * S], m[:, 2 * S:3 * S]] for kind, m in more.items()}
        kst = {kind: [X[:, 5 * S:6 * S], m[:, 3 * S:4 * S]] for kind, m in more.items()}
        PT = X[:, 6 * S:8 * S].rearrange("p (g n) -> p g n", g=4)
        wo = QKV[:, 3 * 4096:5 * 4096].rearrange("p (k n) -> p k n", k=KC)
        mod_rows = QKV[:, 5 * 4096:6 * 4096]
        rows = [mod_rows[:, D * i:D * (i + 1)] for i in range(3)] + [R[:, :]]
        gmoe = BIAS[:, 0, :]
        h2 = SC[:, 0:2 * D].rearrange("p (a n) -> p a n", a=2)
        h2T = SC[:, 2 * D:4 * D].rearrange("p (a n) -> p a n", a=2)
        junk = BIAS[:, 1, :]
        proj = BIAS[:, 2, :].rearrange("p (a n) -> p a n", a=2)

        def scores(kind, k, m):
            n, c0 = place(k)
            return sc_buf[kind][n][:, m * S + c0:m * S + c0 + P * (T - k)]

        def at(a, q):
            return a * 2 + q // T, q // T % 2, q % T

        def dist(t):
            return R[:, S - P * (t + 1):S]

        consts, pchain = sem("consts"), sem("pchain")
        small_in = sem("small_in")
        x_in = [sem(f"x_in{i}") for i in range(T // 2)]
        ada_in = [sem(f"ada_in{i}") for i in range(4)]
        vec_in, acc_cols, ada_done, acc_rows, arow_ps, arow_sb = (
            sem(n) for n in ("vec_in", "acc_cols", "ada_done", "acc_rows", "arow_ps", "arow_sb"))
        b_in, row_out = [sem(f"b_in{i}") for i in range(2)], [sem(f"row_out{i}") for i in range(2)]
        mod_rows_in, gmoe_in, rows_done = sem("mod_rows_in"), sem("gmoe_in"), sem("rows_done")
        wi_in, ws_in = sem("wi_in"), [sem(f"ws_in{i}") for i in range(2)]
        lam_ready, lam_exp, op_sb = sem("lam_ready"), sem("lam_exp"), sem("op_sb")
        cols_ps, cols_sb, cexp_done, cact_done = sem("cols_ps"), sem("cols_sb"), sem("cexp_done"), sem("cact_done")
        sq_done, rstd_done, xn_done = sem("sq_done"), sem("rstd_done"), sem("xn_done")
        xt_ps, xt_act, xt_dve, aff_done = sem("xt_ps"), sem("xt_act"), sem("xt_dve"), sem("aff_done")
        wcopy = sem("wcopy")
        iqk_ps, iqk_sb, lat_ps, lat_sb, lat_sq, lat_rstd, ckv_done = (
            sem(n) for n in ("iqk_ps", "iqk_sb", "lat_ps", "lat_sb", "lat_sq", "lat_rstd", "ckv_done"))
        ckvT_ps, ckvT_sb = sem("ckvT_ps"), sem("ckvT_sb")
        ix_ps, ix_relu, ix_acc, ix_mask = sem("ix_ps"), sem("ix_relu"), sem("ix_acc"), sem("ix_mask")
        kv_ps, kv_sb, pj_ps, pj_sb = sem("kv_ps"), sem("kv_sb"), sem("pj_ps"), sem("pj_sb")
        dchain, sel_done = sem("dchain"), sem("sel_done")
        at_s = {k: {n: sem(f"{k}_{n}") for n in (
            "qk_loaded", "bias_ready", "qk_done", "max_done", "exp_done", "tr_done", "pt_act", "pt_dve",
            "pv_done", "o_done", "ot_done", "ot_copied")} for k in ("diff", "dsa")}
        for n in ("o_square", "o_rstd"):
            at_s["diff"][n] = sem("diff_" + n)
        wo_in, gf_in = sem("wo_in"), sem("gf_in")
        op_ps, x2_done, x2_sq, x2_rstd, h2_done = (
            sem(n) for n in ("op_ps", "x2_done", "x2_sq", "x2_rstd", "h2_done"))
        h2_out = [sem(f"h2_out{i}") for i in range(2)]
        h2T_ps, h2T_sb, lg_ps, lg_sb = (sem(n) for n in ("h2T_ps", "h2T_sb", "lg_ps", "lg_sb"))
        gexp_done, gmax_done, e2_in, e2_done, sel_ps, sel_in = (
            sem(n) for n in ("gexp_done", "gmax_done", "e2_in", "e2_done", "sel_ps", "sel_in"))
        oh_done, lst_ps, route_done = sem("oh_done"), sem("lst_ps"), sem("route_done")
        w_in_s = [sem(f"w_expert{i}") for i in range(4)]
        xg_in = [sem(f"xg_in{i}") for i in range(2)]
        y_out = [sem(f"y_out{i}") for i in range(2)]
        idx_done, t_ps, t_sb, gu_ps, sg_done, hid_done, ht_ps, ht_sb, dn_ps, y_sb, rows_out = (
            sem(n) for n in ("idx_done", "t_ps", "t_sb", "gu_ps", "sg_done", "hid_done", "ht_ps",
                             "ht_sb", "dn_ps", "y_sb", "rows_out"))
        yg_in = [sem(f"yg_in{i}") for i in range(4)]
        cb_done, fin_sq, fin_rstd, fin_done, fin_out = (
            sem(n) for n in ("cb_done", "fin_sq", "fin_rstd", "fin_done", "fin_out"))

        WE = [QKV[:, 6144 * i:6144 * (i + 1)] for i in range(4)]
        WGU = [w[:, 0:4096].rearrange("p (g c n) -> p c g n", g=2, c=KC) for w in WE]
        WG = [w[:, 0:2048].rearrange("p (c n) -> p c n", c=KC) for w in WE]
        WU = [w[:, 2048:4096].rearrange("p (c n) -> p c n", c=KC) for w in WE]
        WDN = [w[:, 4096:6144].rearrange("p (c n) -> p c n", c=2) for w in WE]
        xg = [HF[:, 1024 * i:1024 * (i + 1)] for i in range(2)]
        hgT = [HF[:, 2048 + 1024 * i:3072 + 1024 * i] for i in range(2)]
        ysb = [HF[:, 4096 + 1024 * i:5120 + 1024 * i] for i in range(2)]
        sg = [HF[:, 6144 + 256 * i:6400 + 256 * i] for i in range(2)]
        hh_done, x2_half = sem("hh_done"), sem("x2_half")
        hh = HF[:, 6656:6912]
        hid = [HF[:, 6912 + 256 * i:7168 + 256 * i] for i in range(2)]
        hidT = [HF[:, 7424 + 256 * i:7680 + 256 * i] for i in range(2)]
        gfin = SC[:, 0:D]
        yg = [[QKV[:, D * (2 * i + k):D * (2 * i + k + 1)] for k in range(2)] for i in range(4)]
        rbig = [HF[:, T * NE * i:T * NE * (i + 1)].rearrange("p (t e) -> p t e", t=T) for i in range(14)]
        gx = HF[:, 3584:3584 + T * NG].rearrange("p (t g) -> p t g", g=NG)
        gk = HF[:, 3616:3616 + T * NG].rearrange("p (t g) -> p t g", g=NG)
        ohr = [HF[:, 4096 + P * i:4096 + P * (i + 1)] for i in range(2 * T)]
        oht = [HF[:, 6144 + NT * i:6144 + NT * (i + 1)] for i in range(2 * T)]
        ovt = HF[:, 7000:7000 + NE * (NOV + 1)].rearrange("p (j e) -> p j e", e=NE)
        ovx = HF[:, 7800:7800 + NOV + 1]
        ovc = HF[:, 7600:7600 + 5 * NE].rearrange("p (a e) -> p a e", e=NE)

        wg_d = w_gate[0].rearrange("e (p c) n -> e p (c n)", c=KC)
        wu_d = w_up[0].rearrange("e (p c) n -> e p (c n)", c=KC)
        wd_d = w_down[0].rearrange("e (p c) n -> e p (c n)", c=2)
        x_d = x[0].rearrange("(t p) d -> t p d", p=P)
        win_d = w_in[0].rearrange("(j p) n -> p j n", p=P)

        def expert_load(sp, e, b, s):
            for dst, src in ((WE[b][:, 0:2048], wg_d), (WE[b][:, 2048:4096], wu_d), (WE[b][:, 4096:6144], wd_d)):
                sp.dma_start(dst, src[bass.ds(e, 1)].rearrange("o p n -> (o p) n")).then_inc(s, 16)

        passed, zero_done, fill_out = sem("passed"), sem("zero_done"), sem("fill_out")

        def settle(eng):
            eng.sem_inc(passed, 1)

        def start_at(eng, names):
            for kind in ("diff", "dsa"):
                for n in names:
                    if n in at_s[kind]:
                        eng.sem_inc(at_s[kind][n], AT)

        block = ctx.enter_context(nc.Block())

        @block.sync
        def _(sp):
            sp.dma_start(vrows[0:MODC, :], b_ada[0, 0:2 * D].rearrange("(j p) -> j p", p=P)).then_inc(vec_in, 16)
            for i, v in enumerate((c, g_attn)):
                sp.dma_start(vrows[MODC + KC * i:MODC + KC * (i + 1), :], v[0].rearrange("(j p) -> j p", p=P)
                             ).then_inc(vec_in, 16)
            for t in range(0, T, 2):
                sp.dma_start(XT[:, t:t + 2, :], x[0, P * t:P * (t + 2), :].rearrange("(t p) d -> p t d", p=P)
                             ).then_inc(x_in[t // 2], 16)
            sp.dma_start(WI, win_d[:, :, OFF_LAT:OFF_FQ]).then_inc(wi_in, 16)

            def ada_load(i):
                sp.dma_start(ada[i % 4], w_ada[0, :, BANK * i:BANK * (i + 1)].rearrange("(j p) n -> p j n", p=P)
                             ).then_inc(ada_in[i % 4], 16)

            def b_load(r):
                sp.dma_start(brow[:, r % 2, :], b_ada[:, BANK * (4 + r):BANK * (5 + r)]).then_inc(b_in[r % 2], 16)

            for i in range(4):
                ada_load(i)
            for r in range(2):
                b_load(r)
            for i in range(4):
                sp.wait_ge(ada_done, i + 1)
                ada_load(4 + i)
            sp.wait_ge(xt_ps, 16)
            for i in range(2):
                sp.dma_start(WS[:, i], win_d[:, :, P * i:P * (i + 1)]).then_inc(ws_in[i], 16)
            for r in range(NROW):
                sp.wait_ge(arow_sb, r + 1)
                sp.dma_start(mod_dram[:, BANK * r:BANK * (r + 1)], mrow[:, r % 2, :]).then_inc(row_out[r % 2], 16)
                if r + 2 < NROW:
                    b_load(r + 2)
                if r + 4 < NROW:
                    ada_load(8 + r)
            for i in range(2, 4):
                sp.wait_ge(pj_ps, 2 * (i - 1))
                sp.dma_start(WS[:, i % 2], win_d[:, :, P * i:P * (i + 1)]).then_inc(ws_in[i % 2], 16)
            sp.wait_ge(zero_done, 1)
            for j in range(NOV - 12):
                sp.dma_start(y_dram[(NE + j) * P:(NE + j + 1) * P, :], zero_rows).then_inc(fill_out, 16)
            with sp.Fori(2, 8) as a:
                for b in range(2):
                    sp.wait_ge(pj_ps, 4 * a + 2 * b - 2)
                    sp.dma_start(WS[:, b], win_d[:, :, bass.ds(a * (2 * P) + (OFF_FQ + P * (b - 4)), P)]
                                 ).then_inc(ws_in[b], 16)
                    sp.dma_start(y_dram[bass.ds(a * (2 * P) + (NE + NOV - 16 + b) * P, P), :], zero_rows
                                 ).then_inc(fill_out, 16)
            sp.wait_ge(at_s["diff"]["pv_done"], 24 * UNITS + AT)
            sp.dma_start(wo, w_out[0].rearrange("(k p) n -> p k n", p=P)).then_inc(wo_in, 16)
            sp.wait_ge(at_s["dsa"]["pv_done"], 24 * UNITS + AT)
            for i in range(2):
                sp.wait_ge(row_out[i], 8 * NROW)
            sp.dma_start(mod_rows[:, 0:D], mod_dram[:, 0:D].partition_broadcast(P).rearrange("p o n -> p (o n)")
                         ).then_inc(vec_in, 16)
            for t in range(T):
                sp.dma_start(XT[:, t, :], x_d[t]).then_inc(x_in[min(t, 1)], 16)
                if t == 0:
                    sp.dma_start(mod_rows[:, D:4 * D], mod_dram[:, D:4 * D].partition_broadcast(P).rearrange(
                        "p o n -> p (o n)")).then_inc(mod_rows_in, 16)
                    sp.dma_start(gmoe, g_moe.partition_broadcast(P).rearrange("p o n -> p (o n)")
                                 ).then_inc(gmoe_in, 16)
            for e in range(2):
                expert_load(sp, e, e, w_in_s[e])
            for t in range(T):
                sp.wait_ge(h2_done, t + 1)
                sp.dma_start(h2_dram[P * t:P * (t + 1), :], h2[:, t % 2, :]).then_inc(h2_out[t % 2], 16)
            for e in range(2, 4):
                sp.wait_ge(op_ps, 2 * T)
                sp.wait_ge(h2_done, T)
                expert_load(sp, e, e, w_in_s[e])

            def store(e, b):
                sp.wait_ge(y_sb, e + 1)
                sp.dma_start(y_dram[bass.ds(e * P, P), :], ysb[b]).then_inc(y_out[b], 16)

            with sp.Fori(0, NE // 4 - 1) as i:
                for j in range(4):
                    store(4 * i + j, j % 2)
                    sp.wait_ge(dn_ps, 4 * i + j + 1)
                    expert_load(sp, 4 * i + j + 4, j, w_in_s[j])
            sp.wait_ge(route_done, 1)
            n_ov = sp.value_load(ovi[0:1, NOV:NOV + 1], min_val=0, max_val=NOV)

            def overflow_load(j, b):
                e = sp.value_load(ovi[0:1, bass.ds(j, 1)], min_val=0, max_val=NE - 1)
                expert_load(sp, e, b, w_in_s[b])

            for j in range(4):
                store(NE - 4 + j, j % 2)
                if j < 2:
                    sp.wait_ge(dn_ps, NE - 3 + j)
                    with sp.If(n_ov > j):
                        overflow_load(j, j)
            with sp.Fori(0, NOV // 2) as i:
                for b in range(2):
                    with sp.If(n_ov > 2 * i + b):
                        store(NE + 2 * i + b, b)
                        settle(sp)
                        with sp.If(n_ov > 2 * i + b + 2):
                            overflow_load(2 * i + b + 2, b)
                        sp.wait_ge(y_out[b], i * 16 + 16 * (NE // 2 + 1))
                        settle(sp)
            for b in range(2):
                sp.wait_ge(y_out[b], 16 * (NE // 2))
            sp.sem_inc(rows_out, 1)
            for t in range(T):
                sp.wait_ge(fin_done, t + 1)
                sp.dma_start(out[0, P * t:P * (t + 1), :], XT[:, t, :]).then_inc(fin_out, 16)
            sp.wait_ge(fin_out, 16 * T)

        @block.gpsimd
        def _(pool):
            start_at(pool, ("qk_loaded", "bias_ready", "o_rstd"))
            link = Chain(pool, pchain)
            pool.memset(ident[:, :], 0.0).then_inc(pchain, 1)
            pool.memset(before[:, :], 1.0).then_inc(pchain, 1)
            link.n = 2
            pool.wait_ge(pchain, 2)
            pool.affine_select(out=ident[:, :], in_=ident[:, :], compare_op=ALU.not_equal, fill=1.0, base=0,
                               pattern=[[-1, P]], channel_multiplier=1).then_inc(consts, 1)
            pool.memset(ones[:, :], 1.0).then_inc(consts, 1)
            pool.affine_select(out=before[:, :], in_=before[:, :], compare_op=ALU.is_ge, fill=0.0, base=-1,
                               pattern=[[1, P]], channel_multiplier=-1).then_inc(consts, 1)
            pool.memset(neghalf[:, :], -0.5).then_inc(consts, 1)
            pool.iota(iota_p[:, :], pattern=[[1, P]], base=0, channel_multiplier=0,
                      allow_small_or_imprecise_dtypes=True).then_inc(consts, 1)
            pool.iota(iota_t[:, :], pattern=[[1, NT]], base=0, channel_multiplier=0,
                      allow_small_or_imprecise_dtypes=True).then_inc(consts, 1)
            pool.iota(tok[:, :], pattern=[[P, T]], base=0, channel_multiplier=1,
                      allow_small_or_imprecise_dtypes=True).then_inc(consts, 1)
            link(pool.iota(R[:, :], pattern=[[1, S]], base=P - S, channel_multiplier=-1,
                           allow_small_or_imprecise_dtypes=True))
            pool.affine_select(out=R[:, :], in_=R[:, :], compare_op=ALU.is_ge, fill=NEG, base=S - P,
                               pattern=[[-1, S]], channel_multiplier=1).then_inc(consts, 1)
            for i, v in enumerate((2.0 ** (-8 / NDIFF), 2.0 ** (-8 / NDIFF), 2.0 ** (-8 / NH), 2.0 ** (-16 / NH))):
                link(pool.memset(slopes[:, i:i + 1], v))

            def rstd(col, n, width, scale=1.0):
                link(pool.tensor_scalar(ss[:, col:col + n], ss[:, col:col + n], 1.0 / width, EPS, ALU.mult, ALU.add))
                return pool.tensor_tensor(ss[:, col:col + n], ss[:, col:col + n], neghalf[:, 0:n], ALU.pow)

            pool.wait_ge(sq_done, T)
            rstd(0, T, D).then_inc(rstd_done, 1)
            pool.wait_ge(xt_ps, 2 * KC)
            pool.memset(zero_rows, 0.0).then_inc(zero_done, 1)
            pool.wait_ge(wi_in, 16)
            for k in range(4):
                pool.tensor_copy(WIK[:, :, ID * k:ID * (k + 1)], WI[:, :, LAT + IH * ID:LAT + IH * ID + ID]
                                 ).then_inc(wcopy, 1)
            pool.tensor_copy(WD[:, :, 0:LAT], WI[:, :, 0:LAT]).then_inc(wcopy, 1)
            pool.tensor_copy(WD[:, :, LAT:LAT + IH], WI[:, :, NIDX - IH:NIDX]).then_inc(wcopy, 1)
            for r in range(NROW):
                w = ada[r % 4]
                pool.wait_ge(ada_in[r % 4], 16 * (r // 4 + 2))
                for j in range(KC):
                    pool.tensor_scalar(w[:, j, :], w[:, j, :], cact[:, j:j + 1], 0.0, ALU.mult, ALU.add
                                       ).then_inc(pchain, 1)
                link.n += KC
                pool.wait_ge(pchain, link.n)
                for n in (4, 2):
                    link(pool.tensor_tensor(w[:, 0:n, :], w[:, 0:n, :], w[:, n:2 * n, :], ALU.add))
                pool.tensor_tensor(w[:, 0, :], w[:, 0, :], w[:, 1, :], ALU.add).then_inc(acc_rows, 1)
            pool.wait_ge(lat_sq, T)
            rstd(T, T, LAT).then_inc(lat_rstd, 1)
            for i, t in enumerate(sel_tiles):
                pool.wait_ge(ix_acc, IH * (i + 1))
                diag = SC[:, sc_off[t] + P * t:sc_off[t] + P * (t + 1)]
                pool.affine_select(out=diag, in_=diag, compare_op=ALU.is_ge, fill=LOW, base=0,
                                   pattern=[[-1, P]], channel_multiplier=1).then_inc(ix_mask, 1)

            def load_qk(kind, u, p, i):
                s = at_s[kind]
                c0 = S // 2 * (i // 2)
                dst, src = ((qst[kind][p], q_at[kind]), (kst[kind][p], k_at[kind]))[i % 2]
                pool.wait_ge(s["qk_done"], (u - 1) * 16 + AT)
                settle(pool)
                pool.tensor_copy(dst[:, c0:c0 + S // 2], QKV[:, bass.ds(u * S + (src + c0), S // 2)]
                                 ).then_inc(s["qk_loaded"], 1)

            def diff_bias(p):
                pool.tensor_scalar(BIAS[:, p, :], R[:, :], slopes[:, 0:1], 0.0, ALU.mult, ALU.add
                                   ).then_inc(at_s["diff"]["bias_ready"], 1)

            def next_slopes(c0, factor):
                link(pool.tensor_scalar(slopes[:, c0:c0 + 2], slopes[:, c0:c0 + 2], factor, 0.0, ALU.mult, ALU.add))

            def o_rstd(u, k):
                s = at_s["diff"]
                pool.wait_ge(s["o_square"], u * T + k + 1 + AT)
                settle(pool)
                link(pool.tensor_scalar(oss[:, 2 + k % 2:3 + k % 2], oss[:, k % 2:k % 2 + 1], 1.0 / DV, EPS,
                                        ALU.mult, ALU.add))
                pool.tensor_tensor(oss[:, 2 + k % 2:3 + k % 2], oss[:, 2 + k % 2:3 + k % 2], neghalf[:, 0:1],
                                   ALU.pow).then_inc(s["o_rstd"], 1)

            def first_qk(kind):
                s = at_s[kind]
                for dst, src in ((qst[kind][0], q_at[kind]), (kst[kind][0], k_at[kind])):
                    pool.tensor_copy(dst, QKV[:, src:src + S]).then_inc(s["qk_loaded"], 2)

            pool.wait_ge(sel_done, 1)
            pool.wait_ge(pj_sb, 32)
            first_qk("diff")
            diff_bias(0)
            pool.wait_ge(at_s["diff"]["bias_ready"], 1 + AT)
            next_slopes(0, 2.0 ** (-8 / NDIFF))
            with pool.Fori(0, UNITS // 2) as a:
                link.loop(a, 2 * (T + 1))
                for p in range(2):
                    u = a * 2 + p
                    for k in range(T):
                        o_rstd(u, k)
                        if k < 4:
                            if p == 0:
                                load_qk("diff", u + 1, 1 - p, k)
                            else:
                                with pool.If(a < last):
                                    load_qk("diff", u + 1, 1 - p, k)
                        if k == 4:
                            pool.wait_ge(at_s["diff"]["max_done"], u * 16 + AT)
                            settle(pool)
                            if p == 0:
                                diff_bias(1 - p)
                            else:
                                with pool.If(a < last):
                                    diff_bias(1 - p)
                                    pool.wait_ge(at_s["diff"]["bias_ready"], u + 2 + AT)
                                    settle(pool)
                            if p == 0:
                                pool.wait_ge(at_s["diff"]["bias_ready"], u + 2 + AT)
                                settle(pool)
                            next_slopes(0, 2.0 ** (-8 / NDIFF))
            link.leave(UNITS // 2)

            s = at_s["dsa"]
            pool.wait_ge(at_s["diff"]["qk_done"], 16 * UNITS + AT)
            pool.wait_ge(at_s["diff"]["max_done"], 16 * UNITS + AT)
            pool.wait_ge(at_s["diff"]["pv_done"], 24 * UNITS + AT)
            first_qk("dsa")
            with pool.Fori(0, UNITS // 2) as a:
                link.loop(a, 2)
                for p in range(2):
                    u = a * 2 + p
                    for i in range(2 * T):
                        t, m = T - 1 - i // 2, i % 2
                        w = P * (t + 1)
                        src = SC[:, sc_off[t]:sc_off[t] + w] if t >= T0 else dist(t)
                        n, c0 = bias_place(i)
                        pool.wait_ge(s["max_done"], u * 16 + (0 if i == 1 else i - 2) + AT)
                        settle(pool)
                        pool.tensor_scalar(BIAS[:, n, c0:c0 + w], src, slopes[:, 2 + m:3 + m], 0.0, ALU.mult, ALU.add
                                           ).then_inc(s["bias_ready"], 1)
                        if i in (2, 5, 8, 11):
                            if p == 0:
                                load_qk("dsa", u + 1, 1 - p, (i - 2) // 3)
                            else:
                                with pool.If(a < last):
                                    load_qk("dsa", u + 1, 1 - p, (i - 2) // 3)
                    pool.wait_ge(s["bias_ready"], u * 16 + 16 + AT)
                    settle(pool)
                    next_slopes(2, 2.0 ** (-16 / NH))
            link.leave(UNITS // 2)

            pool.wait_ge(mod_rows_in, 16)
            pool.wait_ge(at_s["dsa"]["max_done"], 16 * UNITS + AT)
            pool.tensor_copy(R[:, :], mod_rows[:, 3 * D:4 * D]).then_inc(rows_done, 1)
            link(pool.tensor_scalar(rows[2], rows[2], 1.0, None, ALU.add))
            pool.wait_ge(gmoe_in, 16)
            pool.tensor_tensor(rows[2], rows[2], gmoe, ALU.mult).then_inc(rows_done, 1)
            for t in range(T):
                pool.wait_ge(x2_sq, t + 1)
                rstd(2 * T + t, 1, D).then_inc(x2_rstd, 1)

            def gather(e, b):
                if not isinstance(e, int):
                    pool.wait_ge(t_ps, e - 1)
                pool.tensor_copy(idx[:, b:b + 1], lst[:, bass.ds(e, 1)]).then_inc(idx_done, 1)
                pool.wait_ge(idx_done, e + 1)
                settle(pool)
                pool.indirect_dma_start(out=xg[b], out_offset=None, in_=h2_dram,
                                        in_offset=bass.IndirectOffsetOnAxis(ap=idx[:, b:b + 1].bitcast(U32), axis=0)
                                        ).then_inc(xg_in[b], 16)

            pool.wait_ge(route_done, 1)
            for i in range(2):
                pool.wait_ge(h2_out[i], 16 * (T // 2))
            gather(0, 0)
            gather(1, 1)
            with pool.Fori(0, NE // 2 - 1) as i:
                for b in range(2):
                    gather(2 * i + 2 + b, b)
            n_ov = pool.value_load(ovi[0:1, NOV:NOV + 1], min_val=0, max_val=NOV)
            with pool.Fori(0, NOV // 2) as i:
                for b in range(2):
                    with pool.If(n_ov > 2 * i + b):
                        gather(2 * i + (NE + b), b)

            def fetch(t):
                for k in range(2):
                    pool.indirect_dma_start(out=yg[t % 4][k], out_offset=None, in_=y_dram,
                                            in_offset=bass.IndirectOffsetOnAxis(
                                                ap=slot[:, k, t:t + 1].bitcast(U32), axis=0)
                                            ).then_inc(yg_in[t % 4], 16)

            pool.wait_ge(rows_out, 1)
            for t in range(4):
                fetch(t)
            for t in range(T):
                pool.wait_ge(fin_sq, t + 1)
                rstd(3 * T + t, 1, D).then_inc(fin_rstd, 1)
                if t + 4 < T:
                    fetch(t + 4)

        @block.scalar
        def _(act):
            start_at(act, ("exp_done", "pt_act", "o_square", "ot_copied"))
            act.dma_start(gkv[:, :], g_kv.partition_broadcast(P).rearrange("p o n -> p (o n)")).then_inc(small_in, 16)
            act.dma_start(gsub[:, :], g_sub.partition_broadcast(P).rearrange("p o n -> p (o n)")).then_inc(small_in, 16)
            for i, v in enumerate((lam_q1, lam_k1, lam_q2, lam_k2)):
                act.dma_start(lamv[:, i, :], v.partition_broadcast(P).rearrange("p o n -> p (o n)")
                              ).then_inc(small_in, 16)
            act.dma_start(bgr[:, 0:NG], b_group.partition_broadcast(P).rearrange("p o n -> p (o n)")
                          ).then_inc(small_in, 16)
            act.dma_start(bgr[:, NG:NR], b_router.partition_broadcast(P).rearrange("p o n -> p (o n)")
                          ).then_inc(small_in, 16)
            act.dma_start(wuk[:, :, :], w_uk[0].rearrange("h c d -> c h d")).then_inc(small_in, 16)
            act.dma_start(wuv[:, :, :], w_uv[0].rearrange("h c d -> c h d")).then_inc(small_in, 16)
            act.dma_start(wgr[:, :, 0:NG], w_group[0].rearrange("(j p) n -> p j n", p=P)).then_inc(small_in, 16)
            act.dma_start(wgr[:, :, NG:NR], w_router[0].rearrange("(j p) n -> p j n", p=P)).then_inc(small_in, 16)
            act.wait_ge(cols_sb, 1)
            act.activation(cexp[:, :], cols[:, MODC:MODC + KC], ACT.Exp, scale=-1.0).then_inc(cexp_done, 1)
            for t in range(T):
                act.wait_ge(x_in[t // 2], 16)
                if t:
                    act.wait_ge(sq_done, t)
                act.activation(BIAS[:, 2, :], XT[:, t, :], ACT.Square, accum_out=ss[:, t:t + 1]).then_inc(sq_done, 1)
            act.wait_ge(lam_ready, 2)
            act.activation(lam2[:, 2:4], lam2[:, 0:2], ACT.Exp).then_inc(lam_exp, 1)
            act.wait_ge(aff_done, 1)
            for g in range(0, 2 * KC, 2):
                act.wait_ge(xt_ps, g + 1)
                act.activation(HT[:, g // 2, 0:BANK], PS[:, g % 4, :], ACT.Identity, bias=mod[:, g // 2:g // 2 + 1],
                               scale=sc1[:, g // 2:g // 2 + 1]).then_inc(xt_act, 1)
            for n in range(4):
                act.wait_ge(iqk_ps, n + 1)
                act.activation((iqT if n < 2 else ikT)[:, BANK * (n % 2):BANK * (n % 2 + 1)], PS[:, n, :], ACT.Copy
                               ).then_inc(iqk_sb, 1)
            for t in range(T):
                act.wait_ge(lat_sb, 2 * t + 2)
                if t:
                    act.wait_ge(lat_sq, t)
                act.activation(BIAS[:, 2, 0:LAT], X[:, 2 * S + LAT * t:2 * S + LAT * (t + 1)], ACT.Square,
                               accum_out=ss[:, T + t:T + t + 1]).then_inc(lat_sq, 1)
            def keep_row(r):
                act.wait_ge(arow_ps, r + 1)
                if r >= 2:
                    act.wait_ge(row_out[r % 2], 16 * (r // 2))
                act.activation(mrow[:, r % 2, :], PS[0:1, 6 + r % 2, :], ACT.Copy).then_inc(arow_sb, 1)

            for n in range(IH * NS):
                t = sel_tiles[n // IH]
                act.wait_ge(ix_ps, n + 1)
                if n >= 2:
                    act.wait_ge(ix_acc, n - 1)
                act.activation(RL[:, n % 2, 0:P * (t + 1)],
                               PS[:, 2 * (n % 2):2 * (n % 2) + 2, :].rearrange("p a n -> p (a n)")[:, 0:P * (t + 1)],
                               ACT.Relu, scale=ID ** -0.5).then_inc(ix_relu, 1)
                if n % 3 == 1 and n > 1:
                    keep_row(n // 3 - 1)
            keep_row(NROW - 1)
            for n in range(2):
                act.wait_ge(ckvT_ps, n + 1)
                act.activation(ckvT[:, BANK * n:BANK * (n + 1)], PS[:, 4 + n, :], ACT.Copy).then_inc(ckvT_sb, 1)
            for n in range(2 * UNITS):
                act.wait_ge(kv_ps, n + 1)
                act.activation(QKV[:, k_at["dsa"] + BANK * n:k_at["dsa"] + BANK * (n + 1)], PS[:, 4 + n % 2, :], ACT.Copy).then_inc(kv_sb, 1)
            for t in range(T):
                act.wait_ge(kv_ps, 2 * UNITS + t + 1)
                act.activation(vd[:, t, :], PS[:, 4 + t % 2, :], ACT.Copy).then_inc(kv_sb, 1)
            for i in range(2):
                act.wait_ge(row_out[i], 8 * NROW)
            for a0, a1, scale in ((0, 4, DH ** -0.5), (4, 8, 1.0)):
                with act.Fori(a0, a1) as a:
                    for n in range(4):
                        act.wait_ge(pj_ps, 4 * a + n + 1)
                        act.activation(QKV[:, bass.ds(a * (4 * BANK) + (2 * 4096 + BANK * n), BANK)], PS[:, n, :],
                                       ACT.Copy, scale=scale).then_inc(pj_sb, 1)

            def exp(kind, a, q, m):
                u, _, k = at(a, q)
                s, sc = at_s[kind], scores(kind, k, m)
                act.wait_ge(s["max_done"], u * 16 + 2 * k + m + 1 + AT)
                act.activation(sc, sc, ACT.Exp, bias=nmx[:, k % 4, m:m + 1], scale=-1.0,
                               accum_out=rs[:, k % 4, m:m + 1]).then_inc(s["exp_done"], 1)

            def keep_turned(kind, a, q, i):
                u, _, k = at(a, q)
                s, g = at_s[kind], DONE[k] + i
                _, b0, b1 = groups_of(T - 1 - k)[i]
                act.wait_ge(s["tr_done"], u * 24 + g + 1 + AT)
                act.wait_ge(s["pv_done"], u * 24 + g - 3 + AT)
                act.activation(PT[:, g % 4, 0:P * (b1 - b0)], PS[:, 4 + g % 2, 0:P * (b1 - b0)], ACT.Copy
                               ).then_inc(s["pt_act"], 1)

            def square(kind, a, q):
                u, _, k = at(a, q)
                if kind == "diff":
                    act.wait_ge(at_s[kind]["o_done"], u * 2 * T + 2 * k + 1 + AT)
                    act.activation(osq[:, :], osb[:, k % 2, :], ACT.Square, accum_out=oss[:, k % 2:k % 2 + 1]
                                   ).then_inc(at_s[kind]["o_square"], 1)

            def copy_out(kind, a, q):
                u, _, k = at(a, q)
                chunk = u + (UNITS if kind == "diff" else 0)
                act.wait_ge(at_s[kind]["ot_done"], u * T + k + 1 + AT)
                act.activation(HF[:, bass.ds(chunk * S + P * (T - 1 - k), P)] if not isinstance(chunk, int)
                               else HF[:, chunk * S + P * (T - 1 - k):chunk * S + P * (T - k)],
                               PS[:, 6 + k % 2, 256:384], ACT.Copy).then_inc(at_s[kind]["ot_copied"], 1)

            act.wait_ge(fill_out, 16 * NOV)
            for kind in ("diff", "dsa"):
                exp(kind, 0, 0, 0)
                exp(kind, 0, 0, 1)
                with act.Fori(0, UNITS // 2) as a:
                    for q in range(2 * T):
                        four = len(groups_of(T - 1 - q % T)) == 4
                        if q >= 2:
                            copy_out(kind, a, q - 2)
                        else:
                            with act.If(a > 0):
                                copy_out(kind, last, q - 2)
                        keep_turned(kind, a, q, 0)
                        if q + 1 < 2 * T:
                            exp(kind, a, q + 1, 0)
                        if q:
                            square(kind, a, q - 1)
                        elif kind == "diff":
                            with act.If(a > 0):
                                square(kind, last, q - 1)
                        if four:
                            keep_turned(kind, a, q, 2)
                        if q + 1 < 2 * T:
                            exp(kind, a, q + 1, 1)
                        else:
                            with act.If(a < last):
                                exp(kind, 0, q + 1, 0)
                                exp(kind, 0, q + 1, 1)
                copy_out(kind, last, 2 * T - 2)
                square(kind, last, 2 * T - 1)
                copy_out(kind, last, 2 * T - 1)

            for t in range(T + 2):
                if t < T:
                    act.wait_ge(x2_done, t + 1)
                    if t:
                        act.wait_ge(x2_sq, t)
                    act.activation(junk, XT[:, t, :], ACT.Square, accum_out=ss[:, 2 * T + t:2 * T + t + 1]
                                   ).then_inc(x2_sq, 1)
                if t >= 2:
                    for h in range(2):
                        act.wait_ge(h2T_ps, 2 * (t - 2) + h + 1)
                        if t >= 4:
                            act.wait_ge(lg_ps, t - 3)
                        act.activation(h2T[:, t % 2, BANK * h:BANK * (h + 1)], PS[:, 4 + h, :], ACT.Copy
                                       ).then_inc(h2T_sb, 1)
            act.wait_ge(gmax_done, 1)
            act.activation(gx, gx, ACT.Exp).then_inc(gexp_done, 1)
            act.wait_ge(e2_in, 1)
            act.activation(rt[:, 3, :], rt[:, 3, :], ACT.Exp).then_inc(e2_done, 1)

            def ev_t(e, b):
                act.wait_ge(t_ps, e + 1)
                if not isinstance(e, int) or e >= 2:
                    act.wait_ge(gu_ps, e - 1)
                act.activation(hgT[b], PS[:, 0:2, :].rearrange("p a n -> p (a n)"), ACT.Copy).then_inc(t_sb, 1)

            def ev_sg(e, b):
                act.wait_ge(gu_ps, e + 1)
                if not isinstance(e, int) or e >= 2:
                    act.wait_ge(hid_done, e - 1)
                act.activation(sg[b], PS[:, 2 + b, 0:DE], ACT.Sigmoid).then_inc(sg_done, 1)

            def ev_h(e, b):
                act.wait_ge(ht_ps, e + 1)
                if not isinstance(e, int) or e >= 2:
                    act.wait_ge(dn_ps, e - 1)
                act.activation(hidT[b], PS[:, 4 + 3 * b, 0:DE], ACT.Copy).then_inc(ht_sb, 1)

            ev_t(0, 0)
            ev_sg(0, 0)
            ev_t(1, 1)
            for e in range(2):
                ev_h(e, e)
                ev_sg(e + 1, (e + 1) % 2)
                ev_t(e + 2, e % 2)
            with act.Fori(1, NE // 2 - 1) as i:
                for b in range(2):
                    e = 2 * i + b
                    ev_h(e, b)
                    ev_sg(e + 1, 1 - b)
                    ev_t(e + 2, b)
            ev_h(NE - 2, 0)
            ev_sg(NE - 1, 1)
            ev_h(NE - 1, 1)
            n_ov = act.value_load(ovi[0:1, NOV:NOV + 1], min_val=0, max_val=NOV)
            with act.Fori(0, NOV // 2) as i:
                for b in range(2):
                    with act.If(n_ov > 2 * i + b):
                        e = 2 * i + (NE + b)
                        ev_t(e, b)
                        ev_sg(e, b)
                        ev_h(e, b)
            act.wait_ge(route_done, 1)
            act.dma_start(gfin, g_final.partition_broadcast(P)).then_inc(gf_in, 16)
            for t in range(T):
                act.wait_ge(cb_done, t + 1)
                if t:
                    act.wait_ge(fin_sq, t)
                act.activation(HF[:, 0:D], XT[:, t, :], ACT.Square, accum_out=ss[:, 3 * T + t:3 * T + t + 1]
                               ).then_inc(fin_sq, 1)

        @block.vector
        def _(dve):
            start_at(dve, ("max_done", "pt_dve", "o_done"))
            link = Chain(dve, dchain)
            dve.wait_ge(cols_ps, 1)
            dve.tensor_copy(cols[:, :], PS[:, 6, 0:MODC + 2 * KC]).then_inc(cols_sb, 1)
            dve.wait_ge(cols_sb, 1)
            dve.wait_ge(cexp_done, 1)
            link(dve.tensor_scalar(cexp[:, :], cexp[:, :], 1.0, None, ALU.add))
            link(dve.reciprocal(cexp[:, :], cexp[:, :]))
            dve.tensor_tensor(cact[:, :], cexp[:, :], cols[:, MODC:MODC + KC], ALU.mult).then_inc(cact_done, 1)
            dve.wait_ge(rstd_done, 1)
            for t in range(T):
                dve.tensor_scalar(XT[:, t, :], XT[:, t, :], ss[:, t:t + 1], None, ALU.mult).then_inc(xn_done, 1)
            dve.wait_ge(small_in, 16 * 12)
            for i in range(2):
                dve.tensor_tensor_reduce(lamv[:, 2 * i, :], lamv[:, 2 * i, :], lamv[:, 2 * i + 1, :], 1.0, 0.0,
                                         ALU.mult, ALU.add, lam2[:, i:i + 1]).then_inc(lam_ready, 1)
            link(dve.tensor_scalar(gsub[:, :], gsub[:, :], 1.0 - LAM0, None, ALU.mult))
            dve.wait_ge(cact_done, 1)
            for i in range(4):
                dve.wait_ge(ada_in[i], 16)
                link(dve.tensor_scalar(ada[i][:, 0, :], ada[i][:, 0, :], cact[:, 0:1], None, ALU.mult))
                for j in range(1, KC):
                    link(dve.scalar_tensor_tensor(out=ada[i][:, 0, :], in0=ada[i][:, j, :], scalar=cact[:, j:j + 1],
                                                  in1=ada[i][:, 0, :], op0=ALU.mult, op1=ALU.add))
                dve.sem_inc(acc_cols, 1)
            dve.wait_ge(ada_done, 4)
            link(dve.tensor_tensor(mod[:, 0:2 * KC], PS[:, 7, 0:2 * KC], cols[:, 0:2 * KC], ALU.add))
            link(dve.tensor_scalar(sc1[:, :], mod[:, KC:2 * KC], 1.0, None, ALU.add))
            link(dve.tensor_tensor(sc1[:, :], sc1[:, :], cols[:, MODC + KC:MODC + 2 * KC], ALU.mult))
            dve.tensor_copy(cexp[:, :], sc1[:, :]).then_inc(aff_done, 1)
            for g in range(1, 2 * KC, 2):
                dve.wait_ge(xt_ps, g + 1)
                dve.tensor_scalar(HT[:, g // 2, BANK:2 * BANK], PS[:, g % 4, :], sc1[:, g // 2:g // 2 + 1],
                                  mod[:, g // 2:g // 2 + 1], ALU.mult, ALU.add).then_inc(xt_dve, 1)
            dve.wait_ge(lam_exp, 1)
            link(dve.tensor_tensor(lam2[:, 0:1], lam2[:, 3:4], lam2[:, 2:3], ALU.subtract))
            link(dve.tensor_scalar(lam2[:, 0:1], lam2[:, 0:1], -LAM0, None, ALU.add))
            for t in range(T):
                dve.wait_ge(lat_ps, t + 1)
                dve.tensor_copy(ckv[:, LAT * t:LAT * (t + 1)], PS[:, 4 + t % 2, 0:LAT]).then_inc(lat_sb, 1)
                dve.tensor_scalar(iw[:, t, :], PS[:, 4 + t % 2, LAT:LAT + IH], IH ** -0.5, None, ALU.mult
                                  ).then_inc(lat_sb, 1)
            dve.wait_ge(lat_sb, 2 * T)
            for n in range(IH * NS):
                t, h = sel_tiles[n // IH], n % IH
                w = P * (t + 1)
                dst = SC[:, sc_off[t]:sc_off[t] + w]
                dve.wait_ge(ix_relu, n + 1)
                if h == 0:
                    dve.tensor_scalar(dst, RL[:, n % 2, 0:w], iw[:, t, h:h + 1], None, ALU.mult).then_inc(ix_acc, 1)
                else:
                    dve.wait_ge(ix_acc, n)
                    dve.scalar_tensor_tensor(out=dst, in0=RL[:, n % 2, 0:w], scalar=iw[:, t, h:h + 1], in1=dst,
                                             op0=ALU.mult, op1=ALU.add).then_inc(ix_acc, 1)

            dve.wait_ge(lat_rstd, 1)
            for t in range(T):
                dve.scalar_tensor_tensor(out=ckv[:, LAT * t:LAT * (t + 1)], in0=ckv[:, LAT * t:LAT * (t + 1)],
                                         scalar=ss[:, T + t:T + t + 1], in1=gkv[:, :], op0=ALU.mult, op1=ALU.mult
                                         ).then_inc(ckv_done, 1)

            u_, bit, trial, mask, thr, keep = (tk[:, i, :] for i in range(6))
            link(dve.memset(u_.bitcast(F32), 0.0))
            link(dve.memset(bit.bitcast(F32), -0.0))
            dve.wait_ge(ix_mask, NS)

            def threshold(src):
                link(dve.tensor_scalar(mask.bitcast(I32), src.bitcast(I32), 31, -1, ALU.arith_shift_right,
                                       ALU.bitwise_xor))
                link(dve.scalar_tensor_tensor(out=thr.bitcast(I32), in0=mask.bitcast(I32), scalar=-2147483648,
                                              in1=src.bitcast(I32), op0=ALU.bitwise_or, op1=ALU.bitwise_xor))

            with dve.Fori(0, 32) as it:
                link.loop(it, 6 + NS)
                link(dve.tensor_tensor(trial, u_, bit, ALU.bitwise_or))
                threshold(trial)
                for i, t in enumerate(sel_tiles):
                    w = P * (t + 1)
                    if i >= 3:
                        dve.wait_ge(dchain, link.base + (link.n + i - 2))
                    dve.tensor_scalar(BIAS[:, i % 3, 0:w], SC[:, sc_off[t]:sc_off[t] + w],
                                      thr.bitcast(F32)[:, i:i + 1], 0.0, ALU.is_ge, ALU.add,
                                      accum_out=cnt[:, 0, i:i + 1]).then_inc(dchain, 1)
                link.n += NS
                dve.wait_ge(dchain, link.base + link.n)
                link(dve.tensor_scalar(keep, cnt[:, 0, :], float(TOPK), None, ALU.is_ge))
                settle(dve)
                link(dve.copy_predicated(u_, keep, trial))
                link(dve.tensor_scalar(bit, bit, 1, None, ALU.logical_shift_right))
            link.leave(32)
            threshold(u_)
            for i, t in enumerate(sel_tiles):
                w = P * (t + 1)
                sc = SC[:, sc_off[t]:sc_off[t] + w]
                above, on, run = (BIAS[:, a, 0:w] for a in range(3))
                th = thr.bitcast(F32)[:, i:i + 1]
                link(dve.tensor_scalar(above, sc, th, 0.0, ALU.is_gt, ALU.add, accum_out=cnt[:, 1, i:i + 1]))
                link(dve.tensor_scalar(on, sc, th, None, ALU.is_equal))
                link(dve.tensor_tensor_scan(run, dist(t), on, 0.0, ALU.max, ALU.add))
                link(dve.tensor_scalar(cnt[:, 1, i:i + 1], cnt[:, 1, i:i + 1], -1.0, float(TOPK), ALU.mult, ALU.add))
                link(dve.scalar_tensor_tensor(out=run, in0=run, scalar=cnt[:, 1, i:i + 1], in1=on, op0=ALU.is_le,
                                              op1=ALU.mult))
                link(dve.tensor_tensor(run, run, above, ALU.add))
                link(dve.tensor_scalar(run, run, -1.0, -NEG, ALU.add, ALU.mult))
                link(dve.tensor_tensor(sc, run, dist(t), ALU.add))
            dve.sem_inc(sel_done, 1)

            def score(kind, a, q, m):
                u, p, k = at(a, q)
                s, w = at_s[kind], P * (T - k)
                dve.wait_ge(s["qk_done"], u * 16 + 2 * k + m + 1 + AT)
                dve.wait_ge(s["bias_ready"], (u + 1 if kind == "diff" else u * 16 + 2 * k + m + 1) + AT)
                dve.wait_ge(s["tr_done"], u * 24 + (DONE[k - 2] if k >= 3 else DONE[k + 6] - 24) + AT)
                settle(dve)
                n, c0 = (p, S - w) if kind == "diff" else bias_place(2 * k + m)
                dve.tensor_tensor_reduce(
                    scores(kind, k, m), PS[:, 2 * m:2 * m + 2, :].rearrange("p a n -> p (a n)")[:, 0:w],
                    BIAS[:, n, c0:c0 + w], -1.0, 3.0e38, ALU.add, ALU.min, nmx[:, k % 4, m:m + 1]
                ).then_inc(s["max_done"], 1)

            def keep_turned(kind, a, q, i):
                u, _, k = at(a, q)
                s, g = at_s[kind], DONE[k] + i
                _, b0, b1 = groups_of(T - 1 - k)[i]
                dve.wait_ge(s["tr_done"], u * 24 + g + 1 + AT)
                dve.wait_ge(s["pv_done"], u * 24 + g - 3 + AT)
                dve.tensor_copy(PT[:, g % 4, 0:P * (b1 - b0)], PS[:, 4 + g % 2, 0:P * (b1 - b0)]
                                ).then_inc(s["pt_dve"], 1)

            def norm(kind, a, q):
                u, _, k = at(a, q)
                s, r, o, b = at_s[kind], k % 4, k % 2, 6 + k % 2
                dve.wait_ge(s["pv_done"], u * 24 + DONE[k + 1] + AT)
                dve.wait_ge(s["ot_done"], u * T + k - 1 + AT)
                link(dve.reciprocal(rin[:, r, :], rs[:, r, :]))
                if kind == "dsa":
                    for m in range(2):
                        dve.tensor_scalar(osb[:, o, DH * m:DH * (m + 1)], PS[:, b, DH * m:DH * (m + 1)],
                                          rin[:, r, m:m + 1], None, ALU.mult).then_inc(s["o_done"], 1)
                    return
                link(dve.tensor_scalar(rin[:, r, 1:2], rin[:, r, 1:2], lam2[:, 0:1], None, ALU.mult))
                link(dve.tensor_scalar(osb[:, o, :], PS[:, b, 0:DV], rin[:, r, 0:1], None, ALU.mult))
                dve.scalar_tensor_tensor(out=osb[:, o, :], in0=PS[:, b, DV:2 * DV], scalar=rin[:, r, 1:2],
                                         in1=osb[:, o, :], op0=ALU.mult, op1=ALU.add).then_inc(s["o_done"], 1)

            def sub_norm(kind, a, q):
                u, _, k = at(a, q)
                if kind == "diff":
                    dve.wait_ge(at_s[kind]["o_rstd"], u * T + k + 1 + AT)
                    dve.scalar_tensor_tensor(out=osb[:, k % 2, :], in0=osb[:, k % 2, :],
                                             scalar=oss[:, 2 + k % 2:3 + k % 2], in1=gsub[:, :], op0=ALU.mult,
                                             op1=ALU.mult).then_inc(at_s[kind]["o_done"], 1)

            dve.wait_ge(fill_out, 16 * NOV)
            for kind in ("diff", "dsa"):
                late = 3 if kind == "diff" else 1
                for q in range(2):
                    for m in range(2):
                        score(kind, 0, q, m)
                with dve.Fori(0, UNITS // 2) as a:
                    link.loop(a, 2 * T * late)
                    for q in range(2 * T):
                        four = len(groups_of(T - 1 - q % T)) == 4
                        keep_turned(kind, a, q, 1)
                        if q:
                            norm(kind, a, q - 1)
                        else:
                            with dve.If(a > 0):
                                link.n = -late
                                norm(kind, last, q - 1)
                                sub_norm(kind, last, q - 1)
                        if q + 2 < 2 * T:
                            score(kind, a, q + 2, 0)
                            if four:
                                keep_turned(kind, a, q, 3)
                            score(kind, a, q + 2, 1)
                        else:
                            with dve.If(a < last):
                                score(kind, 0, q + 2, 0)
                                score(kind, 0, q + 2, 1)
                        if q:
                            sub_norm(kind, a, q - 1)
                link.leave(UNITS // 2, late)
                norm(kind, last, 2 * T - 1)
                sub_norm(kind, last, 2 * T - 1)

            dve.wait_ge(vec_in, 16 * 4)
            for t in range(T + 3):
                if t < T:
                    for h in range(2):
                        n = 2 * t + h
                        part = slice(BANK * h, BANK * (h + 1))
                        dve.wait_ge(op_ps, n + 1)
                        if n >= 2:
                            dve.wait_ge(x2_half, n - 1)
                        dve.tensor_tensor(proj[:, h, :], PS[:, n % 4, :], rows[0][:, part], ALU.mult
                                          ).then_inc(op_sb, 1)
                        dve.wait_ge(op_sb, n + 1)
                        if n == 0:
                            dve.wait_ge(x_in[0], 16 + 16)
                        elif n == 2:
                            dve.wait_ge(x_in[1], 16 + 16 * (T - 1))
                        ins = dve.tensor_tensor(XT[:, t, part], proj[:, h, :], XT[:, t, part], ALU.add)
                        ins.then_inc(x2_half, 1)
                    dve.wait_ge(x2_half, 2 * t + 2)
                    dve.sem_inc(x2_done, 1)
                if 1 <= t <= T:
                    q = t - 1
                    if q == 0:
                        dve.wait_ge(rows_done, 2)
                    if q >= 2:
                        dve.wait_ge(h2_out[q % 2], 16 * (q // 2))
                        dve.wait_ge(h2T_ps, 2 * (q - 1))
                    dve.wait_ge(x2_rstd, q + 1)
                    link(dve.scalar_tensor_tensor(out=h2[:, q % 2, :], in0=XT[:, q, :],
                                                  scalar=ss[:, 2 * T + q:2 * T + q + 1], in1=rows[2], op0=ALU.mult,
                                                  op1=ALU.mult))
                    dve.tensor_tensor(h2[:, q % 2, :], h2[:, q % 2, :], rows[1], ALU.add).then_inc(h2_done, 1)
                if t >= 3:
                    q = t - 3
                    dve.wait_ge(lg_ps, q + 1)
                    dve.tensor_tensor(logits[:, q, :], PS[:, 6 + q % 2, 0:NR], bgr[:, :], ALU.add
                                      ).then_inc(lg_sb, 1)

            def over(a, n):
                return a.unsqueeze(2).to_broadcast([P, T, n])

            gl, el = logits[:, :, 0:NG], logits[:, :, NG:NR]
            pg, v1, v2, e2, key, w1, w2 = (rt[:, i, :] for i in (0, 1, 2, 3, 4, 5, 6))
            tile_of, row_of = [rt[:, 7, :], rt[:, 8, :]], [rt[:, 9, :], rt[:, 10, :]]
            em, tmp, tmp2, carry, fl, tl = rbig[0], rbig[1], rbig[2], rbig[5], rbig[6], rbig[7]
            pick = [rbig[3], rbig[4]]
            down = iota_t[:, 0:NE].unsqueeze(1)
            dve.wait_ge(lg_sb, T)
            dve.wait_ge(op_ps, 2 * T)
            link(dve.tensor_reduce(v1, gl, AX_X, ALU.max))
            link(dve.tensor_tensor(gx, gl, over(v1, NG), ALU.subtract))
            link(dve.tensor_scalar(gk, gx, 0.0, None, ALU.is_ge))
            link(dve.tensor_scalar(tmp2[:, 0, :], iota_t[:, 0:NE], -1.0, float(NE), ALU.mult, ALU.add))
            link(dve.tensor_tensor(gk, gk, tmp2[:, 0, 0:NG].unsqueeze(1).to_broadcast([P, T, NG]), ALU.mult))
            link(dve.tensor_reduce(key, gk, AX_X, ALU.max))
            link(dve.tensor_tensor(gk, gk, over(key, NG), ALU.is_equal))
            dve.sem_inc(gmax_done, 1)
            dve.wait_ge(gexp_done, 1)
            link(dve.tensor_reduce(pg, gx, AX_X, ALU.add))
            link(dve.reciprocal(pg, pg))
            link(dve.tensor_scalar(gk, gk, -1.0, -NEG, ALU.add, ALU.mult))
            link(dve.tensor_tensor(em.rearrange("p t (g e) -> p t g e", g=NG),
                                   el.rearrange("p t (g e) -> p t g e", g=NG),
                                   gk.unsqueeze(3).to_broadcast([P, T, NG, EPG]), ALU.add))
            fall = rbig[8]
            for t in range(T):
                dve.tensor_scalar(fall[:, t, :], iota_t[:, 0:NE], -1.0, float(NE), ALU.mult, ALU.add
                                  ).then_inc(dchain, 1)
            link.n += T
            dve.wait_ge(dchain, link.n)
            for k, v in enumerate((v1, v2)):
                link(dve.tensor_reduce(v, em, AX_X, ALU.max))
                link(dve.tensor_tensor(tmp, em, over(v, NE), ALU.is_equal))
                link(dve.tensor_tensor(tmp, tmp, fall, ALU.mult))
                link(dve.tensor_reduce(key, tmp, AX_X, ALU.max))
                link(dve.tensor_tensor(pick[k], tmp, over(key, NE), ALU.is_equal))
                if k == 0:
                    link(dve.scalar_tensor_tensor(out=em.rearrange("p t e -> p (t e)"),
                                                  in0=pick[0].rearrange("p t e -> p (t e)"), scalar=2 * NEG,
                                                  in1=em.rearrange("p t e -> p (t e)"), op0=ALU.mult, op1=ALU.add))
            dve.tensor_tensor(e2, v2, v1, ALU.subtract).then_inc(e2_in, 1)
            dve.tensor_tensor(rbig[9], pick[0], pick[1], ALU.add).then_inc(sel_in, 1)
            dve.wait_ge(e2_done, 1)
            link(dve.tensor_scalar(w1, e2, 1.0, None, ALU.add))
            link(dve.reciprocal(w1, w1))
            link(dve.tensor_tensor(w1, w1, pg, ALU.mult))
            link(dve.tensor_tensor(w2, w1, e2, ALU.mult))
            dve.wait_ge(sel_ps, 1)
            rank, total = PS[:, 0, 0:T * NE], PS[:, 1, 0:T * NE].rearrange("p (t e) -> p t e", t=T)
            link(dve.memset(carry[:, 0, :], 0.0))
            for t in range(1, T):
                link(dve.tensor_tensor(carry[:, t, :], carry[:, t - 1, :], total[:, t - 1, :], ALU.add))
            n_e, n_ov, ov_end, ov_base = (ovc[:, i, :] for i in range(4))
            link(dve.tensor_tensor(n_e, carry[:, T - 1, :], total[:, T - 1, :], ALU.add))
            flat = lambda a: a.rearrange("p t e -> p (t e)")
            link(dve.tensor_tensor(flat(tmp), rank, flat(carry), ALU.add))
            link(dve.tensor_scalar(flat(fl), flat(tmp), float(P), None, ALU.is_ge))
            link(dve.tensor_scalar(n_ov, n_e, float(P), None, ALU.is_gt))
            for m in range(2, T):
                link(dve.scalar_tensor_tensor(out=flat(fl), in0=flat(tmp), scalar=float(P * m), in1=flat(fl),
                                              op0=ALU.is_ge, op1=ALU.add))
                link(dve.scalar_tensor_tensor(out=n_ov, in0=n_e, scalar=float(P * m), in1=n_ov, op0=ALU.is_gt,
                                              op1=ALU.add))
            link(dve.memset(ovc[:, 4, :], 0.0))
            link(dve.tensor_tensor_scan(ov_end, ovc[:, 4, :], n_ov, 0.0, ALU.add, ALU.add))
            link(dve.tensor_tensor(ov_base, ov_end, n_ov, ALU.subtract))
            link(dve.scalar_tensor_tensor(out=flat(tmp2), in0=flat(fl), scalar=-float(P), in1=flat(tmp),
                                          op0=ALU.mult, op1=ALU.add))
            link(dve.tensor_scalar(ov_base, ov_base, float(NE - 1), None, ALU.add))
            link(dve.tensor_tensor(ov_base, ov_base, iota_t[:, 0:NE], ALU.subtract))
            link(dve.tensor_tensor(tl, fl, ov_base.unsqueeze(1).to_broadcast([P, T, NE]), ALU.add))
            link(dve.tensor_scalar(flat(fl), flat(fl), 1.0, None, ALU.min))
            link(dve.tensor_tensor(tl, tl, fl, ALU.mult))
            link(dve.tensor_tensor(tl, tl, down.to_broadcast([P, T, NE]), ALU.add))
            for k in range(2):
                for src, dst in ((tl, tile_of[k]), (tmp2, row_of[k])):
                    link(dve.tensor_tensor(tmp, src, pick[k], ALU.mult))
                    link(dve.tensor_reduce(dst, tmp, AX_X, ALU.add))
                link(dve.scalar_tensor_tensor(out=key, in0=tile_of[k], scalar=float(P), in1=row_of[k],
                                              op0=ALU.mult, op1=ALU.add))
                link(dve.tensor_copy(slot[:, k, :], key))
            for k in range(2):
                for t in range(T):
                    i = k * T + t
                    dve.tensor_scalar(ohr[i], iota_p[:, :], row_of[k][:, t:t + 1], None, ALU.is_equal
                                      ).then_inc(oh_done, 1)
                    dve.tensor_scalar(oht[i], iota_t[:, :], tile_of[k][:, t:t + 1], tok[:, t:t + 1], ALU.is_equal,
                                      ALU.mult).then_inc(oh_done, 1)
            link(dve.tensor_tensor(ovt, ov_end.unsqueeze(1).to_broadcast([P, NOV + 1, NE]),
                                   iota_t[:, 0:NOV + 1].unsqueeze(2).to_broadcast([P, NOV + 1, NE]), ALU.is_le))
            link(dve.tensor_reduce(ovx[:, 0:NOV + 1], ovt, AX_X, ALU.add))
            link(dve.tensor_scalar(ovx[:, 0:NOV], ovx[:, 0:NOV], float(NE - 1), None, ALU.min))
            link(dve.tensor_copy(ovx[:, NOV:NOV + 1], ov_end[:, NE - 1:NE]))
            link(dve.tensor_copy(ovi[:, 0:NOV + 1], ovx[:, 0:NOV + 1]))
            dve.wait_ge(lst_ps, 1)
            dve.tensor_copy(lst[:, :], PS[:, 2, 0:NT]).then_inc(route_done, 1)

            def ev_hid(e, b):
                dve.wait_ge(sg_done, e + 1)
                if not isinstance(e, int) or e >= 1:
                    dve.wait_ge(hid_done, e)
                if not isinstance(e, int) or e >= 2:
                    dve.wait_ge(ht_ps, e - 1)
                dve.tensor_tensor(hh, PS[:, 2 + b, 0:DE], sg[b], ALU.mult).then_inc(hh_done, 1)
                dve.wait_ge(hh_done, e + 1)
                dve.tensor_tensor(hid[b], hh, PS[:, 2 + b, DE:2 * DE], ALU.mult).then_inc(hid_done, 1)

            def ev_y(e, b, stored):
                dve.wait_ge(dn_ps, e + 1)
                dve.wait_ge(y_out[b], stored * 16)
                dve.tensor_tensor(ysb[b], PS[:, 5:7, :].rearrange("p a n -> p (a n)"), rows[3], ALU.mult
                                  ).then_inc(y_sb, 1)

            ev_hid(0, 0)
            for e in range(2):
                ev_hid(e + 1, (e + 1) % 2)
                ev_y(e, e, 0)
            with dve.Fori(1, NE // 2 - 1) as i:
                for b in range(2):
                    e = 2 * i + b
                    ev_hid(e + 1, 1 - b)
                    ev_y(e, b, i)
            ev_hid(NE - 1, 1)
            ev_y(NE - 2, 0, NE // 2 - 1)
            ev_y(NE - 1, 1, NE // 2 - 1)
            n_ov = dve.value_load(ovi[0:1, NOV:NOV + 1], min_val=0, max_val=NOV)
            with dve.Fori(0, NOV // 2) as i:
                for b in range(2):
                    with dve.If(n_ov > 2 * i + b):
                        ev_hid(2 * i + (NE + b), b)
                        ev_y(2 * i + (NE + b), b, i + NE // 2)

            dve.wait_ge(gf_in, 16)
            for t in range(T + 1):
                if t < T:
                    y1, y2 = yg[t % 4]
                    dve.wait_ge(yg_in[t % 4], 32 * (t // 4 + 1))
                    link(dve.scalar_tensor_tensor(out=XT[:, t, :], in0=y1, scalar=w1[:, t:t + 1], in1=XT[:, t, :],
                                                  op0=ALU.mult, op1=ALU.add))
                    dve.scalar_tensor_tensor(out=XT[:, t, :], in0=y2, scalar=w2[:, t:t + 1], in1=XT[:, t, :],
                                             op0=ALU.mult, op1=ALU.add).then_inc(cb_done, 1)
                if t:
                    dve.wait_ge(fin_rstd, t)
                    dve.scalar_tensor_tensor(out=XT[:, t - 1, :], in0=XT[:, t - 1, :],
                                             scalar=ss[:, 3 * T + t - 1:3 * T + t], in1=gfin, op0=ALU.mult,
                                             op1=ALU.mult).then_inc(fin_done, 1)

        @block.tensor
        def _(pe):
            start_at(pe, ("qk_done", "tr_done", "pv_done", "ot_done"))
            pe.wait_ge(consts, 8)
            pe.wait_ge(vec_in, 16 * 3)
            nv = MODC + 2 * KC
            pe.transpose(PS[:, 6, 0:nv], vrows, ident[0:nv, 0:nv]).then_inc(cols_ps, 1)

            pe.wait_ge(xn_done, T)
            for g in range(2 * KC):
                j, half = g // 2, g % 2
                if g >= 4:
                    pe.wait_ge(xt_act if half == 0 else xt_dve, (g - 4) // 2 + 1)
                for i in range(4):
                    end = pe.transpose(PS[:, g % 4, P * i:P * (i + 1)], XT[:, 4 * half + i, P * j:P * (j + 1)],
                                        ident[:, :])
                end.then_inc(xt_ps, 1)
                if g == 3:
                    for b in range(4):
                        pe.wait_ge(acc_cols, b + 1)
                        for q in range(4):
                            end = pe.matmul(PS[:, 7, 4 * b + q:4 * b + q + 1], ada[b][:, 0, P * q:P * (q + 1)],
                                             ones[:, 0:1], start=True, stop=True)
                        end.then_inc(ada_done, 1)
            pe.wait_ge(xt_act, KC)
            pe.wait_ge(xt_dve, KC)
            pe.wait_ge(wcopy, 6)
            for n in range(4):
                for j in range(KC):
                    end = pe.matmul(PS[:, n, :], WI[:, j, LAT:LAT + P] if n < 2 else WIK[:, j, :],
                                     HT[:, j, BANK * (n % 2):BANK * (n % 2 + 1)], start=(j == 0), stop=(j == KC - 1))
                end.then_inc(iqk_ps, 1)
            for t in range(T):
                if t >= 2:
                    pe.wait_ge(lat_sb, 2 * (t - 1))
                for j in range(KC):
                    end = pe.matmul(PS[:, 4 + t % 2, 0:LAT + IH], HT[:, j, P * t:P * (t + 1)], WD[:, j, :],
                                     start=(j == 0), stop=(j == KC - 1))
                end.then_inc(lat_ps, 1)
            pe.wait_ge(iqk_sb, 4)
            for n in range(IH * NS):
                t, h = sel_tiles[n // IH], n % IH
                w = P * (t + 1)
                if n >= 2:
                    pe.wait_ge(ix_relu, n - 1)
                for c0 in range(0, w, BANK):
                    c1 = min(c0 + BANK, w)
                    end = pe.matmul(PS[:, 2 * (n % 2) + c0 // BANK, 0:c1 - c0], iqT[ID * h:ID * (h + 1), P * t:P * (t + 1)],
                                     ikT[ID * h:ID * (h + 1), c0:c1], start=True, stop=True)
                end.then_inc(ix_ps, 1)
                if n % 3 == 2:
                    r = n // 3
                    pe.wait_ge(acc_rows, r + 1)
                    if r >= 2:
                        pe.wait_ge(arow_sb, r - 1)
                    pe.matmul(PS[0:1, 6 + r % 2, :], ones[:, 0:1], ada[r % 4][:, 0, :], start=True, stop=False)
                    pe.wait_ge(b_in[r % 2], 16 * (r // 2 + 1))
                    pe.matmul(PS[0:1, 6 + r % 2, :], ones[0:1, 0:1], brow[:, r % 2, :], start=False, stop=True
                              ).then_inc(arow_ps, 1)
            pe.wait_ge(ckv_done, T)
            for n in range(2):
                for i in range(4):
                    end = pe.transpose(PS[:, 4 + n, P * i:P * (i + 1)], ckv[:, P * (4 * n + i):P * (4 * n + i + 1)],
                                        ident[:, :])
                end.then_inc(ckvT_ps, 1)
            pe.wait_ge(ckvT_sb, 2)
            for n in range(2 * UNITS):
                if n >= 2:
                    pe.wait_ge(kv_sb, n - 1)
                pe.matmul(PS[:, 4 + n % 2, :], wuk[:, n // 2 * 2:n // 2 * 2 + 2, :].rearrange("p h d -> p (h d)"),
                          ckvT[:, BANK * (n % 2):BANK * (n % 2 + 1)], start=True, stop=True).then_inc(kv_ps, 1)
            for t in range(T):
                pe.wait_ge(kv_sb, 2 * UNITS + t - 1)
                pe.matmul(PS[:, 4 + t % 2, :], ckvT[:, P * t:P * (t + 1)],
                          wuv[:, :, :].rearrange("p h d -> p (h d)"), start=True, stop=True).then_inc(kv_ps, 1)

            def project(b, half):
                for j in range(KC):
                    end = pe.matmul(PS[:, 2 * b + half, :], WS[:, b, j, :], HT[:, j, BANK * half:BANK * (half + 1)],
                                     start=(j == 0), stop=(j == KC - 1))
                end.then_inc(pj_ps, 1)

            def project_rows(b, half):
                for i in range(4):
                    t = 4 * half + i
                    for j in range(KC):
                        end = pe.matmul(PS[:, 2 * b + half, P * i:P * (i + 1)], HT[:, j, P * t:P * (t + 1)],
                                         WS[:, b, j, :], start=(j == 0), stop=(j == KC - 1))
                end.then_inc(pj_ps, 1)

            pe.wait_ge(ix_relu, IH * NS)
            for b in range(2):
                pe.wait_ge(ws_in[b], 16)
                for half in range(2):
                    project(b, half)
            for a0, a1, what in ((1, 6, project), (6, 8, project_rows)):
                with pe.Fori(a0, a1) as a:
                    for b in range(2):
                        pe.wait_ge(ws_in[b], a * 16 + 16)
                        for half in range(2):
                            pe.wait_ge(pj_sb, a * 4 + (2 * b + half - 3))
                            what(b, half)
            pe.wait_ge(kv_sb, 2 * UNITS + T)
            pe.wait_ge(pj_sb, 32)

            def qk(kind, a, q, m):
                u, p, k = at(a, q)
                s, t, w = at_s[kind], T - 1 - k, P * (T - k)
                if k == 0 and m == 0:
                    pe.wait_ge(s["qk_loaded"], u * 4 + 4 + AT)
                pe.wait_ge(s["max_done"], u * 16 + 2 * k + m - 1 + AT)
                for c0 in range(0, w, BANK):
                    c1 = min(c0 + BANK, w)
                    end = pe.matmul(PS[:, 2 * m + c0 // BANK, 0:c1 - c0],
                                     qst[kind][p][DH * m:DH * (m + 1), P * t:P * (t + 1)],
                                     kst[kind][p][DH * m:DH * (m + 1), c0:c1], start=True, stop=True)
                end.then_inc(s["qk_done"], 1)

            def turn(kind, a, q, i):
                u, _, k = at(a, q)
                s, g = at_s[kind], DONE[k] + i
                m, b0, b1 = groups_of(T - 1 - k)[i]
                pe.wait_ge(s["exp_done"], u * 16 + 2 * k + m + 1 + AT)
                pe.wait_ge(s["pt_dve" if g % 2 else "pt_act"], u * 12 + g // 2 + AT)
                for b in range(b0, b1):
                    end = pe.transpose(PS[:, 4 + g % 2, P * (b - b0):P * (b - b0 + 1)],
                                        scores(kind, k, m)[:, P * b:P * (b + 1)], ident[:, :])
                end.then_inc(s["tr_done"], 1)

            def pv(kind, a, q, i):
                u, _, k = at(a, q)
                s, g, width = at_s[kind], DONE[k] + i, DH if kind == "dsa" else DV
                m, b0, b1 = groups_of(T - 1 - k)[i]
                if i == 0:
                    pe.wait_ge(s["ot_copied"], u * T + k - 1 + AT)
                pe.wait_ge(s["pt_dve" if g % 2 else "pt_act"], u * 12 + g // 2 + 1 + AT)
                for b in range(b0, b1):
                    v = (vd[:, b, bass.ds(u * (2 * DH) + DH * m, DH)] if kind == "dsa"
                         else vf[:, bass.ds(u * S + P * b, DV)])
                    end = pe.matmul(PS[:, 6 + k % 2, width * m:width * (m + 1)],
                                     PT[:, g % 4, P * (b - b0):P * (b - b0 + 1)], v, start=(b == 0),
                                     stop=(b == T - 1 - k))
                end.then_inc(s["pv_done"], 1)

            def turn_out(kind, a, q):
                u, _, k = at(a, q)
                pe.wait_ge(at_s[kind]["o_done"], u * 2 * T + 2 * k + 2 + AT)
                pe.transpose(PS[:, 6 + k % 2, 256:384], osb[:, k % 2, :], ident[:, :]
                             ).then_inc(at_s[kind]["ot_done"], 1)

            for kind in ("diff", "dsa"):
                for q in range(2):
                    for m in range(2):
                        qk(kind, 0, q, m)
                with pe.Fori(0, UNITS // 2) as a:
                    for q in range(2 * T):
                        four = len(groups_of(T - 1 - q % T)) == 4
                        turn(kind, a, q, 0)
                        turn(kind, a, q, 1)
                        if q + 2 < 2 * T:
                            qk(kind, a, q + 2, 0)
                        else:
                            with pe.If(a < last):
                                qk(kind, 0, q + 2, 0)
                                qk(kind, 0, q + 2, 1)
                        pv(kind, a, q, 0)
                        if four:
                            turn(kind, a, q, 2)
                            pv(kind, a, q, 1)
                            turn(kind, a, q, 3)
                        if q + 2 < 2 * T:
                            qk(kind, a, q + 2, 1)
                        for i in ((2, 3) if four else (1,)):
                            pv(kind, a, q, i)
                        if q:
                            turn_out(kind, a, q - 1)
                        else:
                            with pe.If(a > 0):
                                turn_out(kind, last, q - 1)
                turn_out(kind, last, 2 * T - 1)
                pe.wait_ge(at_s[kind]["ot_copied"], UNITS * T + AT)

            pe.wait_ge(wo_in, 16)
            for t in range(T + 3):
                if t < T:
                    for h in range(2):
                        n = 2 * t + h
                        if n >= 4:
                            pe.wait_ge(op_sb, n - 3)
                        for k in range(KC):
                            end = pe.matmul(PS[:, n % 4, :], HT[:, k, P * t:P * (t + 1)],
                                             wo[:, k, BANK * h:BANK * (h + 1)], start=(k == 0), stop=(k == KC - 1))
                        end.then_inc(op_ps, 1)
                if 2 <= t < T + 2:
                    q = t - 2
                    pe.wait_ge(h2_done, q + 1)
                    for h in range(2):
                        if q:
                            pe.wait_ge(h2T_sb, 2 * (q - 1) + h + 1)
                        for i in range(4):
                            end = pe.transpose(PS[:, 4 + h, P * i:P * (i + 1)],
                                                h2[:, q % 2, P * (4 * h + i):P * (4 * h + i + 1)], ident[:, :])
                        end.then_inc(h2T_ps, 1)
                if t >= 3:
                    q = t - 3
                    pe.wait_ge(h2T_sb, 2 * q + 2)
                    if q >= 2:
                        pe.wait_ge(lg_sb, q - 1)
                    for j in range(KC):
                        end = pe.matmul(PS[:, 6 + q % 2, 0:NR], h2T[:, q % 2, P * j:P * (j + 1)],
                                         wgr[:, j, :], start=(j == 0), stop=(j == KC - 1))
                    end.then_inc(lg_ps, 1)

            pe.wait_ge(sel_in, 1)
            chosen = rbig[9].rearrange("p t e -> p (t e)")
            pe.matmul(PS[:, 0, 0:T * NE], before[:, :], chosen, start=True, stop=True)
            pe.matmul(PS[:, 1, 0:T * NE], ones[:, :], chosen, start=True, stop=True).then_inc(sel_ps, 1)
            for i in range(2 * T):
                pe.wait_ge(oh_done, 2 * i + 2)
                end = pe.matmul(PS[:, 2, 0:NT], ohr[i], oht[i], start=(i == 0), stop=(i == 2 * T - 1))
            end.then_inc(lst_ps, 1)
            pe.wait_ge(route_done, 1)

            def turn_rows(e, b, arrived):
                pe.wait_ge(xg_in[b], arrived)
                if not isinstance(e, int) or e >= 1:
                    pe.wait_ge(t_sb, e)
                for c_ in range(KC):
                    end = pe.transpose(PS[:, c_ // 4, P * (c_ % 4):P * (c_ % 4 + 1)],
                                        xg[b].rearrange("p (k c) -> p c k", c=KC)[:, c_, :], ident[:, :])
                end.then_inc(t_ps, 1)

            def gate_up(e, b, w, arrived):
                pe.wait_ge(t_sb, e + 1)
                pe.wait_ge(w_in_s[w], arrived)
                if not isinstance(e, int) or e >= 2:
                    pe.wait_ge(hid_done, e - 1)
                for c_ in range(KC):
                    end = pe.matmul(PS[:, 2 + b, :], hgT[b][:, P * c_:P * (c_ + 1)], WGU[w][:, c_, :, :],
                                     start=(c_ == 0), stop=(c_ == KC - 1))
                end.then_inc(gu_ps, 1)

            def turn_hidden(e, b):
                pe.wait_ge(hid_done, e + 1)
                if not isinstance(e, int) or e >= 2:
                    pe.wait_ge(ht_sb, e - 1)
                for c_ in range(2):
                    end = pe.transpose(PS[:, 4 + 3 * b, P * c_:P * (c_ + 1)],
                                        hid[b].rearrange("p (k c) -> p c k", c=2)[:, c_, :], ident[:, :])
                end.then_inc(ht_ps, 1)

            def down_proj(e, b, w):
                pe.wait_ge(ht_sb, e + 1)
                if not isinstance(e, int) or e >= 1:
                    pe.wait_ge(y_sb, e)
                for h in range(2):
                    for c_ in range(2):
                        end = pe.matmul(PS[:, 5 + h, :], hidT[b][:, P * c_:P * (c_ + 1)],
                                         WDN[w][:, c_, BANK * h:BANK * (h + 1)], start=(c_ == 0), stop=(c_ == 1))
                end.then_inc(dn_ps, 1)

            def step(e, j, i, last2=None):
                b = j % 2
                turn_hidden(e, b)
                if last2 != 1:
                    w = (j + 1) % 4
                    gate_up(e + 1, 1 - b, w, (i + 1 + (j + 1) // 4) * 48)
                if last2 is None:
                    turn_rows(e + 2, b, (2 * i + (j + 2) // 2 + 1) * 16)
                down_proj(e, b, j)

            turn_rows(0, 0, 16)
            gate_up(0, 0, 0, 48)
            turn_rows(1, 1, 16)
            for j in range(4):
                step(j, j, 0)
            with pe.Fori(1, NE // 4 - 1) as i:
                for j in range(4):
                    step(i * 4 + j, j, i)
            for j in range(4):
                step(NE - 4 + j, j, NE // 4 - 1, None if j < 2 else j - 2)

            n_ov = pe.value_load(ovi[0:1, NOV:NOV + 1], min_val=0, max_val=NOV)
            with pe.Fori(0, NOV // 2) as i:
                for b in range(2):
                    with pe.If(n_ov > 2 * i + b):
                        e = 2 * i + (NE + b)
                        turn_rows(e, b, i * 16 + 16 * (NE // 2 + 1))
                        gate_up(e, b, b, i * 48 + 48 * (NE // 4 + 1))
                        turn_hidden(e, b)
                        down_proj(e, b, b)


_INS = ["x", "c", "w_ada", "b_ada", "g_attn", "w_in", "g_kv", "w_uk", "w_uv", "lam_q1", "lam_k1", "lam_q2", "lam_k2",
        "g_sub", "w_out", "g_moe", "w_group", "b_group", "w_router", "b_router", "w_gate", "w_up", "w_down", "g_final"]


def kernel(**inputs):
    import numpy as _np
    import concourse.bacc as _bacc
    from concourse import mybir as _mybir
    from concourse.bass_utils import run_bass_kernel_spmd as _run

    nc = _bacc.Bacc("TRN2", target_bir_lowering=False, num_devices=1)
    arrays, args = {}, []
    for name in _INS:
        a = _np.ascontiguousarray(inputs[name])
        arrays[f"in_{name}_dram"] = a
        args.append(nc.dram_tensor(f"in_{name}_dram", a.shape, _mybir.dt.from_np(a.dtype), kind="ExternalInput").ap())
    shape = inputs["x"].shape
    args.append(nc.dram_tensor("out_0_dram", shape, _mybir.dt.float32, kind="ExternalOutput").ap())
    hybrid_layer(nc, *args)
    r = _run(nc, [arrays], core_ids=[0])
    return r.results[0]["out_0_dram"]
```

```python
import math
from contextlib import ExitStack

import concourse.bass as bass
from concourse import mybir

F32 = mybir.dt.float32
I32 = mybir.dt.int32
U32 = mybir.dt.uint32
ALU = mybir.AluOpType
ACT = mybir.ActivationFunctionType
AX_X = mybir.AxisListType.X
P = 128
BANK = 512


def groups_of(t):
    return [(m, b, min(b + 4, t + 1)) for m in range(2) for b in range(0, t + 1, 4)]


def place(k):
    return (k % 3, 0) if k < 6 else (2, 384 if k == 6 else 640)


def bias_place(i):
    return (i % 3, 0) if i < 12 else ((2, 384), (2, 640), (2, 896), (1, 384))[i - 12]


def hybrid_layer(nc, x, c, w_ada, b_ada, g_attn, w_in, g_kv, w_uk, w_uv, lam_q1, lam_k1, lam_q2, lam_k2,
                 g_sub, w_out, g_moe, w_group, b_group, w_router, b_router, w_gate, w_up, w_down, g_final, out):
    _, S, D = x.shape
    T = S // P
    KC = D // P
    _, NH, LAT, DH = w_uk.shape
    DV = g_sub.shape[1]
    QD = lam_q1.shape[1]
    NG = w_group.shape[2]
    NE = w_router.shape[2]
    EPG = NE // NG
    NR = NG + NE
    DE = w_gate.shape[3]
    IH = 4
    ID = 32
    OFF_LAT = NH * DH
    OFF_FQ = OFF_LAT + LAT + IH * ID + ID + IH
    NIDX = OFF_FQ - OFF_LAT
    DIFF = (w_in.shape[2] - OFF_FQ) // 3
    NDIFF = DIFF // DV
    TOPK = min(256, S // 4)
    T0 = TOPK // P
    EPS = 1e-6
    LAM0 = 0.8 - 0.6 * math.exp(0.0)
    NEG = -1e30
    LOW = -3.0e38
    NOV = 2 * S // P
    NT = NE + NOV
    MODC = 2 * KC
    NROW = 6 * D // BANK - 4
    UNITS = 4
    AT = 5
    last = UNITS // 2 - 1
    assert last == 1
    DONE = [0]
    for k in range(T):
        DONE.append(DONE[-1] + len(groups_of(T - 1 - k)))
    assert D == 1024 and S == 1024 and DH == 64 and QD == 64 and DV == 128 and LAT == 128
    assert NH == 2 * UNITS and NDIFF == UNITS and DE == 256 and NE == 32 and NG == 4 and T0 == 2

    sel_tiles = list(range(T0, T))
    sc_off, at = {}, 0
    for t in sel_tiles:
        sc_off[t] = at
        at += P * (t + 1)
    SCW = at
    NS = len(sel_tiles)

    h2_dram = nc.dram_tensor("h2_rows", [S, D], F32, kind="Internal").ap()
    mod_dram = nc.dram_tensor("modulation_row", [1, NROW * BANK], F32, kind="Internal").ap()
    y_dram = nc.dram_tensor("expert_rows", [NT * P, D], F32, kind="Internal").ap()

    ctx = ExitStack()
    with ctx:
        def sb(name, shape, dt=F32):
            return ctx.enter_context(nc.sbuf_tensor(name, shape, dt))

        def sem(name):
            return ctx.enter_context(nc.semaphore(name))

        class Chain:

            def __init__(self, eng, s):
                self.eng, self.s, self.base, self.n = eng, s, 0, 0

            def __call__(self, ins):
                ins.then_inc(self.s, 1)
                self.n += 1
                self.eng.wait_ge(self.s, self.base + self.n)

            def loop(self, u, per):
                self.start = self.n if isinstance(self.base, int) and self.base == 0 else self.start
                self.base, self.n, self.per = self.start + u * per, 0, per

            def leave(self, times, late=0):
                assert self.n == self.per - late, (self.n, self.per, late)
                self.n, self.base = self.start + times * self.per - late, 0

        HT = sb("HT", [P, KC, S])
        QKV = sb("QKV", [P, 6 * 4096])
        X = sb("X", [P, 8192])
        SC = sb("SC", [P, SCW])
        BIAS = sb("BIAS", [P, 3, S])
        R = sb("R", [P, S])
        ident = sb("ident", [P, P])
        ones = sb("ones", [P, P])
        before = sb("before", [P, P])
        iota_p = sb("iota_p", [P, P])
        iota_t = sb("iota_t", [P, NT])
        tok = sb("tok", [P, T])
        neghalf = sb("neghalf", [P, T])
        slopes = sb("slopes", [P, 4])
        cols = sb("cols", [P, MODC + 2 * KC])
        cact = sb("cact", [P, KC])
        cexp = sb("cexp", [P, KC])
        mod = sb("mod", [P, MODC])
        sc1 = sb("sc1", [P, KC])
        ss = sb("ss", [P, 4 * T])
        gkv = sb("gkv", [P, LAT])
        gsub = sb("gsub", [P, DV])
        lam2 = sb("lam2", [P, 4])
        wuk = sb("wuk", [P, NH, DH])
        wuv = sb("wuv", [P, NH, DH])
        wgr = sb("wgr", [P, KC, NR])
        bgr = sb("bgr", [P, NR])
        iw = sb("iw", [P, T, IH])
        tk = sb("tk", [P, 6, NS], U32)
        cnt = sb("cnt", [P, 2, NS])
        nmx = sb("nmx", [P, 4, 2])
        rs = sb("rs", [P, 4, 2])
        rin = sb("rin", [P, 4, 2])
        osb = sb("osb", [P, 2, P])
        osq = sb("osq", [P, P])
        oss = sb("oss", [P, 4])
        logits = sb("logits", [P, T, NR])
        rt = sb("rt", [P, 14, T])
        falling = sb("falling", [P, NE])
        lst = sb("lst", [P, NT], I32)
        slot = sb("slot", [P, 2, T], I32)
        idx = sb("idx", [P, 2], I32)
        ovi = sb("ovi", [P, NOV + 2], I32)
        PS = ctx.enter_context(nc.psum_tensor("PS", [P, 8, BANK], F32))

        vrows = BIAS[0:MODC + 2 * KC, 0, 0:P]
        lamv = BIAS[:, 1, 0:4 * QD].rearrange("p (a n) -> p a n", a=4)
        ada = [QKV[:, 4096 * i:4096 * (i + 1)].rearrange("p (j n) -> p j n", j=KC) for i in range(4)]
        WI = QKV[:, 4 * 4096:4 * 4096 + KC * NIDX].rearrange("p (j n) -> p j n", j=KC)
        brow = QKV[0:1, 18720:18720 + 2 * BANK].rearrange("p (a n) -> p a n", a=2)
        mrow = QKV[0:1, 22560:22560 + 2 * BANK].rearrange("p (a n) -> p a n", a=2)
        WIK = QKV[:, 5 * 4096:5 * 4096 + KC * P].rearrange("p (j n) -> p j n", j=KC)
        WD = QKV[:, 5 * 4096 + 1024:5 * 4096 + 1024 + KC * (LAT + IH)].rearrange("p (j n) -> p j n", j=KC)
        XT = X[:, :].rearrange("p (t d) -> p t d", t=T)
        iqT = [X[:, S * i:S * (i + 1)] for i in (0, 5, 6, 7)]
        ikT = X[:, S:2 * S]
        ckvT, ckv = X[:, 0:S], X[:, 2 * S:3 * S]
        RL = X[:, 3 * S:5 * S].rearrange("p (a n) -> p a n", a=2)
        WS = X[:, 5 * S:7 * S].rearrange("p (a j n) -> p a j n", a=2, j=KC)
        zero_rows = X[:, 7 * S:8 * S]
        k_at = {"dsa": 0, "diff": 4 * 4096}
        q_at = {"dsa": 2 * 4096, "diff": 3 * 4096}
        vd = QKV[:, 4096:2 * 4096].rearrange("p (t n) -> p t n", t=T)
        vf = QKV[:, 5 * 4096:6 * 4096]
        HF = HT[:, :, :].rearrange("p k n -> p (k n)")
        more = {"diff": HF[:, 0:4 * S], "dsa": QKV[:, 5 * 4096:6 * 4096]}
        sc_buf = {kind: [X[:, 2 * S:4 * S], X[:, 4 * S:6 * S], m[:, 0:2 * S]] for kind, m in more.items()}
        qst = {kind: [X[:, 0:S], m[:, 2 * S:3 * S]] for kind, m in more.items()}
        kst = {kind: [X[:, S:2 * S], m[:, 3 * S:4 * S]] for kind, m in more.items()}
        PT = X[:, 6 * S:8 * S].rearrange("p (g n) -> p g n", g=4)
        wo = QKV[:, 3 * 4096:5 * 4096].rearrange("p (k n) -> p k n", k=KC)
        mod_rows = QKV[:, 5 * 4096:6 * 4096]
        rows = [mod_rows[:, D * i:D * (i + 1)] for i in range(3)] + [R[:, :]]
        gmoe = BIAS[:, 0, :]
        h2 = SC[:, 0:2 * D].rearrange("p (a n) -> p a n", a=2)
        h2T = SC[:, 2 * D:4 * D].rearrange("p (a n) -> p a n", a=2)
        junk = BIAS[:, 1, :]
        proj = BIAS[:, 2, :].rearrange("p (a n) -> p a n", a=2)

        def scores(kind, k, m):
            n, c0 = place(k)
            return sc_buf[kind][n][:, m * S + c0:m * S + c0 + P * (T - k)]

        def at(a, q):
            return a * 2 + q // T, q // T % 2, q % T

        sel_tmp = [[BIAS[:, i, :] for i in range(3)], [X[:, S * i:S * (i + 1)] for i in (2, 3, 4)]]

        def dist(t):
            return R[:, S - P * (t + 1):S]

        consts, pchain = sem("consts"), sem("pchain")
        small_in = sem("small_in")
        x_in = [sem(f"x_in{i}") for i in range(T // 2)]
        ada_in = [sem(f"ada_in{i}") for i in range(4)]
        vec_in, acc_cols, ada_done, acc_rows, acc_pool, arow_ps, arow_sb = (
            sem(n) for n in ("vec_in", "acc_cols", "ada_done", "acc_rows", "acc_pool", "arow_ps", "arow_sb"))
        b_in, row_out = [sem(f"b_in{i}") for i in range(2)], [sem(f"row_out{i}") for i in range(2)]
        oht_done, place_done = sem("oht_done"), sem("place_done")
        iq_zero, sel_kept = sem("iq_zero"), sem("sel_kept")
        mod_rows_in, gmoe_in, rows_done = sem("mod_rows_in"), sem("gmoe_in"), sem("rows_done")
        wi_in, ws_in = sem("wi_in"), [sem(f"ws_in{i}") for i in range(2)]
        lam_ready, lam_exp, op_sb = sem("lam_ready"), sem("lam_exp"), sem("op_sb")
        cols_ps, cols_sb, cexp_done, cact_done = sem("cols_ps"), sem("cols_sb"), sem("cexp_done"), sem("cact_done")
        sq_done, rstd_done, xn_done = sem("sq_done"), sem("rstd_done"), sem("xn_done")
        xt_ps, xt_act, xt_dve, aff_done = sem("xt_ps"), sem("xt_act"), sem("xt_dve"), sem("aff_done")
        wcopy = sem("wcopy")
        iqk_ps, iqk_sb, lat_ps, lat_sb, lat_sq, lat_rstd, ckv_done = (
            sem(n) for n in ("iqk_ps", "iqk_sb", "lat_ps", "lat_sb", "lat_sq", "lat_rstd", "ckv_done"))
        ckvT_ps, ckvT_sb = sem("ckvT_ps"), sem("ckvT_sb")
        ix_ps, ix_relu, ix_acc, ix_mask = sem("ix_ps"), sem("ix_relu"), sem("ix_acc"), sem("ix_mask")
        kv_ps, kv_sb, pj_ps, pj_sb = sem("kv_ps"), sem("kv_sb"), sem("pj_ps"), sem("pj_sb")
        dchain, sel_done = sem("dchain"), sem("sel_done")
        at_s = {k: {n: sem(f"{k}_{n}") for n in (
            "qk_loaded", "bias_ready", "qk_done", "max_done", "exp_done", "tr_done", "pt_act", "pt_dve",
            "pv_done", "o_done", "ot_done", "ot_copied")} for k in ("diff", "dsa")}
        for n in ("o_square", "o_rstd"):
            at_s["diff"][n] = sem("diff_" + n)
        wo_in, gf_in = sem("wo_in"), sem("gf_in")
        op_ps, x2_done, x2_sq, x2_rstd, h2_done = (
            sem(n) for n in ("op_ps", "x2_done", "x2_sq", "x2_rstd", "h2_done"))
        h2_out = [sem(f"h2_out{i}") for i in range(2)]
        h2T_ps, h2T_sb, lg_ps, lg_sb = (sem(n) for n in ("h2T_ps", "h2T_sb", "lg_ps", "lg_sb"))
        gexp_done, gmax_done, e2_in, e2_done, sel_ps, sel_in = (
            sem(n) for n in ("gexp_done", "gmax_done", "e2_in", "e2_done", "sel_ps", "sel_in"))
        oh_done, lst_ps, route_done = sem("oh_done"), sem("lst_ps"), sem("route_done")
        w_in_s = [sem(f"w_expert{i}") for i in range(4)]
        xg_in = [sem(f"xg_in{i}") for i in range(2)]
        y_out = [sem(f"y_out{i}") for i in range(2)]
        idx_done, t_ps, t_sb, gu_ps, sg_done, hid_done, ht_ps, ht_sb, dn_ps, y_sb, rows_out = (
            sem(n) for n in ("idx_done", "t_ps", "t_sb", "gu_ps", "sg_done", "hid_done", "ht_ps",
                             "ht_sb", "dn_ps", "y_sb", "rows_out"))
        yg_in = [sem(f"yg_in{i}") for i in range(4)]
        cb_done, fin_sq, fin_rstd, fin_done, fin_out = (
            sem(n) for n in ("cb_done", "fin_sq", "fin_rstd", "fin_done", "fin_out"))

        WE = [QKV[:, 6144 * i:6144 * (i + 1)] for i in range(4)]
        WGU = [w[:, 0:4096].rearrange("p (g c n) -> p c g n", g=2, c=KC) for w in WE]
        WG = [w[:, 0:2048].rearrange("p (c n) -> p c n", c=KC) for w in WE]
        WU = [w[:, 2048:4096].rearrange("p (c n) -> p c n", c=KC) for w in WE]
        WDN = [w[:, 4096:6144].rearrange("p (c n) -> p c n", c=2) for w in WE]
        xg = [HF[:, 1024 * i:1024 * (i + 1)] for i in range(2)]
        hgT = [HF[:, 2048 + 1024 * i:3072 + 1024 * i] for i in range(2)]
        ysb = [HF[:, 4096 + 1024 * i:5120 + 1024 * i] for i in range(2)]
        sg = [HF[:, 6144 + 256 * i:6400 + 256 * i] for i in range(2)]
        hh_done, x2_half = sem("hh_done"), sem("x2_half")
        hh = HF[:, 6656:6912]
        hid = [HF[:, 6912 + 256 * i:7168 + 256 * i] for i in range(2)]
        hidT = [HF[:, 7424 + 256 * i:7680 + 256 * i] for i in range(2)]
        gfin = SC[:, 0:D]
        yg = [[QKV[:, D * (2 * i + k):D * (2 * i + k + 1)] for k in range(2)] for i in range(4)]
        rbig = [HF[:, T * NE * i:T * NE * (i + 1)].rearrange("p (t e) -> p t e", t=T) for i in range(14)]
        gx = HF[:, 3584:3584 + T * NG].rearrange("p (t g) -> p t g", g=NG)
        gk = HF[:, 3616:3616 + T * NG].rearrange("p (t g) -> p t g", g=NG)
        ohr = [HF[:, 4096 + P * i:4096 + P * (i + 1)] for i in range(2 * T)]
        oht = [HF[:, 6144 + NT * i:6144 + NT * (i + 1)] for i in range(2 * T)]
        ovt = HF[:, 7000:7000 + NE * (NOV + 1)].rearrange("p (j e) -> p j e", e=NE)
        ovx = HF[:, 7800:7800 + NOV + 1]
        ovc = HF[:, 7600:7600 + 5 * NE].rearrange("p (a e) -> p a e", e=NE)

        wg_d = w_gate[0].rearrange("e (p c) n -> e p (c n)", c=KC)
        wu_d = w_up[0].rearrange("e (p c) n -> e p (c n)", c=KC)
        wd_d = w_down[0].rearrange("e (p c) n -> e p (c n)", c=2)
        x_d = x[0].rearrange("(t p) d -> t p d", p=P)
        win_d = w_in[0].rearrange("(j p) n -> p j n", p=P)

        def expert_load(sp, e, b, s):
            for dst, src in ((WE[b][:, 0:2048], wg_d), (WE[b][:, 2048:4096], wu_d), (WE[b][:, 4096:6144], wd_d)):
                sp.dma_start(dst, src[bass.ds(e, 1)].rearrange("o p n -> (o p) n")).then_inc(s, 16)

        passed, zero_done, fill_out = sem("passed"), sem("zero_done"), sem("fill_out")

        def settle(eng):
            eng.sem_inc(passed, 1)

        def start_at(eng, names):
            for kind in ("diff", "dsa"):
                for n in names:
                    if n in at_s[kind]:
                        eng.sem_inc(at_s[kind][n], AT)

        block = ctx.enter_context(nc.Block())

        @block.sync
        def _(sp):
            sp.dma_start(vrows[0:MODC, :], b_ada[0, 0:2 * D].rearrange("(j p) -> j p", p=P)).then_inc(vec_in, 16)
            for i, v in enumerate((c, g_attn)):
                sp.dma_start(vrows[MODC + KC * i:MODC + KC * (i + 1), :], v[0].rearrange("(j p) -> j p", p=P)
                             ).then_inc(vec_in, 16)
            for t in range(0, T, 2):
                sp.dma_start(XT[:, t:t + 2, :], x[0, P * t:P * (t + 2), :].rearrange("(t p) d -> p t d", p=P)
                             ).then_inc(x_in[t // 2], 16)
            sp.dma_start(WI, win_d[:, :, OFF_LAT:OFF_FQ]).then_inc(wi_in, 16)

            def ada_load(i):
                sp.dma_start(ada[i % 4], w_ada[0, :, BANK * i:BANK * (i + 1)].rearrange("(j p) n -> p j n", p=P)
                             ).then_inc(ada_in[i % 4], 16)

            def b_load(r):
                sp.dma_start(brow[:, r % 2, :], b_ada[:, BANK * (4 + r):BANK * (5 + r)]).then_inc(b_in[r % 2], 16)

            for i in range(4):
                ada_load(i)
            for r in range(2):
                b_load(r)
            for i in range(4):
                sp.wait_ge(ada_done, i + 1)
                ada_load(4 + i)
            for r in range(NROW):
                if r == 6:
                    sp.wait_ge(ix_ps, IH * NS)
                    for i in range(2):
                        sp.dma_start(WS[:, i], win_d[:, :, P * i:P * (i + 1)]).then_inc(ws_in[i], 16)
                sp.wait_ge(arow_sb, r + 1)
                sp.dma_start(mod_dram[:, BANK * r:BANK * (r + 1)], mrow[:, r % 2, :]).then_inc(row_out[r % 2], 16)
                if r + 2 < NROW:
                    b_load(r + 2)
                if r + 4 < NROW:
                    ada_load(8 + r)
            for i in range(2, 4):
                sp.wait_ge(pj_ps, 2 * (i - 1))
                sp.dma_start(WS[:, i % 2], win_d[:, :, P * i:P * (i + 1)]).then_inc(ws_in[i % 2], 16)
            sp.wait_ge(zero_done, 1)
            for j in range(NOV - 12):
                sp.dma_start(y_dram[(NE + j) * P:(NE + j + 1) * P, :], zero_rows).then_inc(fill_out, 16)
            with sp.Fori(2, 8) as a:
                for b in range(2):
                    sp.wait_ge(pj_ps, 4 * a + 2 * b - 2)
                    sp.dma_start(WS[:, b], win_d[:, :, bass.ds(a * (2 * P) + (OFF_FQ + P * (b - 4)), P)]
                                 ).then_inc(ws_in[b], 16)
                    sp.dma_start(y_dram[bass.ds(a * (2 * P) + (NE + NOV - 16 + b) * P, P), :], zero_rows
                                 ).then_inc(fill_out, 16)
            sp.wait_ge(at_s["diff"]["pv_done"], 24 * UNITS + AT)
            sp.dma_start(wo, w_out[0].rearrange("(k p) n -> p k n", p=P)).then_inc(wo_in, 16)
            sp.wait_ge(at_s["dsa"]["pv_done"], 24 * UNITS + AT)
            for i in range(2):
                sp.wait_ge(row_out[i], 8 * NROW)
            sp.dma_start(mod_rows[:, 0:D], mod_dram[:, 0:D].partition_broadcast(P).rearrange("p o n -> p (o n)")
                         ).then_inc(vec_in, 16)
            for t in range(T):
                sp.dma_start(XT[:, t, :], x_d[t]).then_inc(x_in[min(t, 1)], 16)
                if t == 0:
                    sp.dma_start(mod_rows[:, D:4 * D], mod_dram[:, D:4 * D].partition_broadcast(P).rearrange(
                        "p o n -> p (o n)")).then_inc(mod_rows_in, 16)
                    sp.dma_start(gmoe, g_moe.partition_broadcast(P).rearrange("p o n -> p (o n)")
                                 ).then_inc(gmoe_in, 16)
            for e in range(2):
                expert_load(sp, e, e, w_in_s[e])
            for t in range(T):
                sp.wait_ge(h2_done, t + 1)
                sp.dma_start(h2_dram[P * t:P * (t + 1), :], h2[:, t % 2, :]).then_inc(h2_out[t % 2], 16)
            for e in range(2, 4):
                sp.wait_ge(op_ps, 2 * T)
                sp.wait_ge(h2_done, T)
                expert_load(sp, e, e, w_in_s[e])

            def store(e, b):
                sp.wait_ge(y_sb, e + 1)
                sp.dma_start(y_dram[bass.ds(e * P, P), :], ysb[b]).then_inc(y_out[b], 16)

            with sp.Fori(0, NE // 4 - 1) as i:
                for j in range(4):
                    store(4 * i + j, j % 2)
                    sp.wait_ge(dn_ps, 4 * i + j + 1)
                    expert_load(sp, 4 * i + j + 4, j, w_in_s[j])
            sp.wait_ge(route_done, 2)
            n_ov = sp.value_load(ovi[0:1, NOV:NOV + 1], min_val=0, max_val=NOV)

            def overflow_load(j, b):
                e = sp.value_load(ovi[0:1, bass.ds(j, 1)], min_val=0, max_val=NE - 1)
                expert_load(sp, e, b, w_in_s[b])

            for j in range(4):
                store(NE - 4 + j, j % 2)
                if j < 2:
                    sp.wait_ge(dn_ps, NE - 3 + j)
                    with sp.If(n_ov > j):
                        overflow_load(j, j)
            with sp.Fori(0, NOV // 2) as i:
                for b in range(2):
                    with sp.If(n_ov > 2 * i + b):
                        store(NE + 2 * i + b, b)
                        settle(sp)
                        with sp.If(n_ov > 2 * i + b + 2):
                            overflow_load(2 * i + b + 2, b)
                        sp.wait_ge(y_out[b], i * 16 + 16 * (NE // 2 + 1))
                        settle(sp)
            for b in range(2):
                sp.wait_ge(y_out[b], 16 * (NE // 2))
            sp.sem_inc(rows_out, 1)
            for t in range(T):
                sp.wait_ge(fin_done, t + 1)
                sp.dma_start(out[0, P * t:P * (t + 1), :], XT[:, t, :]).then_inc(fin_out, 16)
            sp.wait_ge(fin_out, 16 * T)

        @block.gpsimd
        def _(pool):
            start_at(pool, ("qk_loaded", "bias_ready", "o_rstd"))
            link = Chain(pool, pchain)
            pool.memset(ident[:, :], 0.0).then_inc(pchain, 1)
            pool.memset(before[:, :], 1.0).then_inc(pchain, 1)
            link.n = 2
            pool.wait_ge(pchain, 2)
            pool.affine_select(out=ident[:, :], in_=ident[:, :], compare_op=ALU.not_equal, fill=1.0, base=0,
                               pattern=[[-1, P]], channel_multiplier=1).then_inc(consts, 1)
            pool.memset(ones[:, :], 1.0).then_inc(consts, 1)
            pool.affine_select(out=before[:, :], in_=before[:, :], compare_op=ALU.is_ge, fill=0.0, base=-1,
                               pattern=[[1, P]], channel_multiplier=-1).then_inc(consts, 1)
            pool.memset(neghalf[:, :], -0.5).then_inc(consts, 1)
            pool.iota(iota_p[:, :], pattern=[[1, P]], base=0, channel_multiplier=0,
                      allow_small_or_imprecise_dtypes=True).then_inc(consts, 1)
            pool.iota(iota_t[:, :], pattern=[[1, NT]], base=0, channel_multiplier=0,
                      allow_small_or_imprecise_dtypes=True).then_inc(consts, 1)
            pool.iota(tok[:, :], pattern=[[P, T]], base=0, channel_multiplier=1,
                      allow_small_or_imprecise_dtypes=True).then_inc(consts, 1)
            link(pool.iota(R[:, :], pattern=[[1, S]], base=P - S, channel_multiplier=-1,
                           allow_small_or_imprecise_dtypes=True))
            pool.affine_select(out=R[:, :], in_=R[:, :], compare_op=ALU.is_ge, fill=NEG, base=S - P,
                               pattern=[[-1, S]], channel_multiplier=1).then_inc(consts, 1)
            for i, v in enumerate((2.0 ** (-8 / NDIFF), 2.0 ** (-8 / NDIFF), 2.0 ** (-8 / NH), 2.0 ** (-16 / NH))):
                link(pool.memset(slopes[:, i:i + 1], v))

            def rstd(col, n, width, scale=1.0):
                link(pool.tensor_scalar(ss[:, col:col + n], ss[:, col:col + n], 1.0 / width, EPS, ALU.mult, ALU.add))
                return pool.tensor_tensor(ss[:, col:col + n], ss[:, col:col + n], neghalf[:, 0:n], ALU.pow)

            pool.wait_ge(sq_done, T)
            rstd(0, T, D).then_inc(rstd_done, 1)
            pool.wait_ge(wi_in, 16)
            for k in range(4):
                pool.tensor_copy(WIK[:, :, ID * k:ID * (k + 1)], WI[:, :, LAT + IH * ID:LAT + IH * ID + ID]
                                 ).then_inc(wcopy, 1)
            pool.tensor_copy(WD[:, :, 0:LAT], WI[:, :, 0:LAT]).then_inc(wcopy, 1)
            pool.tensor_copy(WD[:, :, LAT:LAT + IH], WI[:, :, NIDX - IH:NIDX]).then_inc(wcopy, 1)
            pool.wait_ge(xt_ps, 2 * KC)
            for iq in iqT:
                pool.memset(iq, 0.0).then_inc(iq_zero, 1)
            def chunk_sums(r):
                w = ada[r % 4]
                pool.wait_ge(ada_in[r % 4], 16 * (r // 4 + 2))
                for j in range(KC):
                    pool.tensor_scalar(w[:, j, :], w[:, j, :], cact[:, j:j + 1], 0.0, ALU.mult, ALU.add
                                       ).then_inc(pchain, 1)
                link.n += KC
                pool.wait_ge(pchain, link.n)
                for n in (4, 2):
                    link(pool.tensor_tensor(w[:, 0:n, :], w[:, 0:n, :], w[:, n:2 * n, :], ALU.add))
                pool.tensor_tensor(w[:, 0, :], w[:, 0, :], w[:, 1, :], ALU.add).then_inc(acc_pool, 1)

            for r in (4, 5):
                chunk_sums(r)
            pool.wait_ge(lat_sq, T)
            rstd(T, T, LAT).then_inc(lat_rstd, 1)
            chunk_sums(6)
            for i, t in enumerate(sel_tiles):
                pool.wait_ge(ix_acc, IH * (i + 1))
                diag = SC[:, sc_off[t] + P * t:sc_off[t] + P * (t + 1)]
                pool.affine_select(out=diag, in_=diag, compare_op=ALU.is_ge, fill=LOW, base=0,
                                   pattern=[[-1, P]], channel_multiplier=1).then_inc(ix_mask, 1)

            chunk_sums(7)
            pool.wait_ge(ix_ps, IH * NS)
            pool.memset(zero_rows, 0.0).then_inc(zero_done, 1)

            def load_qk(kind, u, p, i):
                s = at_s[kind]
                c0 = S // 2 * (i // 2)
                dst, src = ((qst[kind][p], q_at[kind]), (kst[kind][p], k_at[kind]))[i % 2]
                if isinstance(u, int):
                    pool.wait_ge(at_s["diff"]["qk_done"], 16 * (UNITS - 1) + AT)
                    part = QKV[:, u * S + src + c0:u * S + src + c0 + S // 2]
                else:
                    pool.wait_ge(s["qk_done"], (u - 1) * 16 + AT)
                    settle(pool)
                    part = QKV[:, bass.ds(u * S + (src + c0), S // 2)]
                pool.tensor_copy(dst[:, c0:c0 + S // 2], part).then_inc(s["qk_loaded"], 1)

            def diff_bias(p):
                pool.tensor_scalar(BIAS[:, p, :], R[:, :], slopes[:, 0:1], 0.0, ALU.mult, ALU.add
                                   ).then_inc(at_s["diff"]["bias_ready"], 1)

            def next_slopes(c0, factor):
                link(pool.tensor_scalar(slopes[:, c0:c0 + 2], slopes[:, c0:c0 + 2], factor, 0.0, ALU.mult, ALU.add))

            def o_rstd(u, k):
                s = at_s["diff"]
                pool.wait_ge(s["o_square"], u * T + k + 1 + AT)
                settle(pool)
                link(pool.tensor_scalar(oss[:, 2 + k % 2:3 + k % 2], oss[:, k % 2:k % 2 + 1], 1.0 / DV, EPS,
                                        ALU.mult, ALU.add))
                pool.tensor_tensor(oss[:, 2 + k % 2:3 + k % 2], oss[:, 2 + k % 2:3 + k % 2], neghalf[:, 0:1],
                                   ALU.pow).then_inc(s["o_rstd"], 1)

            def dsa_bias(u, i):
                s = at_s["dsa"]
                t, m = T - 1 - i // 2, i % 2
                w = P * (t + 1)
                src = SC[:, sc_off[t]:sc_off[t] + w] if t >= T0 else dist(t)
                n, c0 = bias_place(i)
                pool.wait_ge(s["max_done"], u * 16 + (0 if i == 1 else i - 2) + AT)
                settle(pool)
                pool.tensor_scalar(BIAS[:, n, c0:c0 + w], src, slopes[:, 2 + m:3 + m], 0.0, ALU.mult, ALU.add
                                   ).then_inc(s["bias_ready"], 1)

            pool.wait_ge(kv_ps, 2 * UNITS + T)
            for dst, src, done in ((qst["diff"][0], q_at["diff"], 10), (kst["diff"][0], k_at["diff"], 18)):
                pool.wait_ge(pj_sb, done)
                pool.tensor_copy(dst, QKV[:, src:src + S]).then_inc(at_s["diff"]["qk_loaded"], 2)
            for i, t in enumerate(sel_tiles):
                w = P * (t + 1)
                sc = SC[:, sc_off[t]:sc_off[t] + w]
                above, _, run = (a[:, 0:w] for a in sel_tmp[i % 2])
                pool.wait_ge(sel_kept, i + 1)
                link(pool.tensor_tensor(run, run, above, ALU.add))
                link(pool.tensor_scalar(run, run, -1.0, -NEG, ALU.add, ALU.mult))
                pool.tensor_tensor(sc, run, dist(t), ALU.add).then_inc(sel_done, 1)
            diff_bias(0)
            pool.wait_ge(at_s["diff"]["bias_ready"], 1 + AT)
            next_slopes(0, 2.0 ** (-8 / NDIFF))
            with pool.Fori(0, UNITS // 2) as a:
                link.loop(a, 2 * (T + 1))
                for p in range(2):
                    u = a * 2 + p
                    for k in range(T):
                        o_rstd(u, k)
                        if k < 4:
                            if p == 0:
                                load_qk("diff", u + 1, 1 - p, k)
                            else:
                                with pool.If(a < last):
                                    load_qk("diff", u + 1, 1 - p, k)
                                with pool.If(a > last - 1):
                                    load_qk("dsa", 0, 0, k)
                        if k == 6 and p == 1:
                            with pool.If(a > last - 1):
                                pool.wait_ge(at_s["diff"]["max_done"], 16 * UNITS + AT)
                                for i in range(3):
                                    dsa_bias(0, i)
                        if k == 4:
                            pool.wait_ge(at_s["diff"]["max_done"], u * 16 + AT)
                            settle(pool)
                            if p == 0:
                                diff_bias(1 - p)
                            else:
                                with pool.If(a < last):
                                    diff_bias(1 - p)
                                    pool.wait_ge(at_s["diff"]["bias_ready"], u + 2 + AT)
                                    settle(pool)
                            if p == 0:
                                pool.wait_ge(at_s["diff"]["bias_ready"], u + 2 + AT)
                                settle(pool)
                            next_slopes(0, 2.0 ** (-8 / NDIFF))
            link.leave(UNITS // 2)

            with pool.Fori(0, UNITS // 2) as a:
                link.loop(a, 2)
                for p in range(2):
                    u = a * 2 + p
                    for i in range(3, 2 * T):
                        dsa_bias(u, i)
                        if i in (3, 6, 9, 11):
                            k = (3, 6, 9, 11).index(i)
                            if p == 0:
                                load_qk("dsa", u + 1, 1 - p, k)
                            else:
                                with pool.If(a < last):
                                    load_qk("dsa", u + 1, 1 - p, k)
                    pool.wait_ge(at_s["dsa"]["bias_ready"], u * 16 + 16 + AT)
                    settle(pool)
                    next_slopes(2, 2.0 ** (-16 / NH))
                    settle(pool)
                    if p == 0:
                        for i in range(3):
                            dsa_bias(u + 1, i)
                    else:
                        with pool.If(a < last):
                            for i in range(3):
                                dsa_bias(u + 1, i)
            link.leave(UNITS // 2)

            pool.wait_ge(mod_rows_in, 16)
            pool.wait_ge(at_s["dsa"]["max_done"], 16 * UNITS + AT)
            pool.tensor_copy(R[:, :], mod_rows[:, 3 * D:4 * D]).then_inc(rows_done, 1)
            link(pool.tensor_scalar(rows[2], rows[2], 1.0, None, ALU.add))
            pool.wait_ge(gmoe_in, 16)
            pool.tensor_tensor(rows[2], rows[2], gmoe, ALU.mult).then_inc(rows_done, 1)
            for t in range(T):
                pool.wait_ge(x2_sq, t + 1)
                rstd(2 * T + t, 1, D).then_inc(x2_rstd, 1)

            def gather(e, b):
                if not isinstance(e, int):
                    pool.wait_ge(t_ps, e - 1)
                pool.tensor_copy(idx[:, b:b + 1], lst[:, bass.ds(e, 1)]).then_inc(idx_done, 1)
                pool.wait_ge(idx_done, e + 1)
                settle(pool)
                pool.indirect_dma_start(out=xg[b], out_offset=None, in_=h2_dram,
                                        in_offset=bass.IndirectOffsetOnAxis(ap=idx[:, b:b + 1].bitcast(U32), axis=0)
                                        ).then_inc(xg_in[b], 16)

            pool.wait_ge(place_done, 1)
            for t in range(2, T):
                pool.tensor_scalar(oht[T + t], iota_t[:, :], rt[:, 8, t:t + 1], tok[:, t:t + 1],
                                   ALU.is_equal, ALU.mult).then_inc(oht_done, 1)
            pool.wait_ge(route_done, 1)
            for i in range(2):
                pool.wait_ge(h2_out[i], 16 * (T // 2))
            gather(0, 0)
            gather(1, 1)
            with pool.Fori(0, NE // 2 - 1) as i:
                for b in range(2):
                    gather(2 * i + 2 + b, b)
            pool.wait_ge(route_done, 2)
            n_ov = pool.value_load(ovi[0:1, NOV:NOV + 1], min_val=0, max_val=NOV)
            with pool.Fori(0, NOV // 2) as i:
                for b in range(2):
                    with pool.If(n_ov > 2 * i + b):
                        gather(2 * i + (NE + b), b)

            def fetch(t):
                for k in range(2):
                    pool.indirect_dma_start(out=yg[t % 4][k], out_offset=None, in_=y_dram,
                                            in_offset=bass.IndirectOffsetOnAxis(
                                                ap=slot[:, k, t:t + 1].bitcast(U32), axis=0)
                                            ).then_inc(yg_in[t % 4], 16)

            pool.wait_ge(rows_out, 1)
            for t in range(4):
                fetch(t)
            for t in range(T):
                pool.wait_ge(fin_sq, t + 1)
                rstd(3 * T + t, 1, D).then_inc(fin_rstd, 1)
                if t + 4 < T:
                    fetch(t + 4)

        @block.scalar
        def _(act):
            start_at(act, ("exp_done", "pt_act", "o_square", "ot_copied"))
            act.dma_start(gkv[:, :], g_kv.partition_broadcast(P).rearrange("p o n -> p (o n)")).then_inc(small_in, 16)
            act.dma_start(gsub[:, :], g_sub.partition_broadcast(P).rearrange("p o n -> p (o n)")).then_inc(small_in, 16)
            for i, v in enumerate((lam_q1, lam_k1, lam_q2, lam_k2)):
                act.dma_start(lamv[:, i, :], v.partition_broadcast(P).rearrange("p o n -> p (o n)")
                              ).then_inc(small_in, 16)
            act.dma_start(bgr[:, 0:NG], b_group.partition_broadcast(P).rearrange("p o n -> p (o n)")
                          ).then_inc(small_in, 16)
            act.dma_start(bgr[:, NG:NR], b_router.partition_broadcast(P).rearrange("p o n -> p (o n)")
                          ).then_inc(small_in, 16)
            act.wait_ge(cols_sb, 1)
            act.activation(cexp[:, :], cols[:, MODC:MODC + KC], ACT.Exp, scale=-1.0).then_inc(cexp_done, 1)
            for t in range(T):
                act.wait_ge(x_in[t // 2], 16)
                if t:
                    act.wait_ge(sq_done, t)
                act.activation(BIAS[:, 2, :], XT[:, t, :], ACT.Square, accum_out=ss[:, t:t + 1]).then_inc(sq_done, 1)
            act.dma_start(wuk[:, :, :], w_uk[0].rearrange("h c d -> c h d")).then_inc(small_in, 16)
            act.dma_start(wuv[:, :, :], w_uv[0].rearrange("h c d -> c h d")).then_inc(small_in, 16)
            act.dma_start(wgr[:, :, 0:NG], w_group[0].rearrange("(j p) n -> p j n", p=P)).then_inc(small_in, 16)
            act.dma_start(wgr[:, :, NG:NR], w_router[0].rearrange("(j p) n -> p j n", p=P)).then_inc(small_in, 16)
            act.wait_ge(aff_done, 1)
            for g in range(0, 2 * KC, 2):
                act.wait_ge(xt_ps, g + 1)
                act.activation(HT[:, g // 2, 0:BANK], PS[:, g % 4, :], ACT.Identity, bias=mod[:, g // 2:g // 2 + 1],
                               scale=sc1[:, g // 2:g // 2 + 1]).then_inc(xt_act, 1)
            act.wait_ge(lam_ready, 2)
            act.activation(lam2[:, 2:4], lam2[:, 0:2], ACT.Exp).then_inc(lam_exp, 1)
            act.wait_ge(iq_zero, IH)
            for n in range(4):
                act.wait_ge(iqk_ps, n + 1)
                part = slice(BANK * (n % 2), BANK * (n % 2 + 1))
                if n < 2:
                    for h in range(IH):
                        rows_h = slice(ID * h, ID * (h + 1))
                        act.activation(iqT[h][rows_h, part], PS[rows_h, n, :], ACT.Copy).then_inc(iqk_sb, 1)
                else:
                    act.activation(ikT[:, part], PS[:, n, :], ACT.Copy).then_inc(iqk_sb, 1)
            for t in range(T):
                act.wait_ge(lat_sb, 2 * t + 2)
                if t:
                    act.wait_ge(lat_sq, t)
                act.activation(BIAS[:, 2, 0:LAT], X[:, 2 * S + LAT * t:2 * S + LAT * (t + 1)], ACT.Square,
                               accum_out=ss[:, T + t:T + t + 1]).then_inc(lat_sq, 1)
            for n in range(IH * NS):
                t = sel_tiles[n // IH]
                act.wait_ge(ix_ps, n + 1)
                if n >= 2:
                    act.wait_ge(ix_acc, n - 1)
                act.activation(RL[:, n % 2, 0:P * (t + 1)],
                               PS[:, 2 * (n % 2):2 * (n % 2) + 2, :].rearrange("p a n -> p (a n)")[:, 0:P * (t + 1)],
                               ACT.Relu, scale=ID ** -0.5).then_inc(ix_relu, 1)
            for n in range(2):
                act.wait_ge(ckvT_ps, n + 1)
                act.activation(ckvT[:, BANK * n:BANK * (n + 1)], PS[:, 4 + n, :], ACT.Copy).then_inc(ckvT_sb, 1)
            for n in range(2 * UNITS):
                act.wait_ge(kv_ps, n + 1)
                act.activation(QKV[:, k_at["dsa"] + BANK * n:k_at["dsa"] + BANK * (n + 1)], PS[:, 4 + n % 2, :], ACT.Copy).then_inc(kv_sb, 1)
            for t in range(T):
                act.wait_ge(kv_ps, 2 * UNITS + t + 1)
                act.activation(vd[:, t, :], PS[:, 4 + t % 2, :], ACT.Copy).then_inc(kv_sb, 1)
            for r in (6, 7):
                act.wait_ge(arow_ps, r + 1)
                act.wait_ge(row_out[r % 2], 16 * (r // 2))
                act.activation(mrow[:, r % 2, :], PS[0:1, 6 + r % 2, :], ACT.Copy).then_inc(arow_sb, 1)
            for i in range(2):
                act.wait_ge(row_out[i], 8 * NROW)
            for a0, a1, scale in ((0, 4, DH ** -0.5), (4, 8, 1.0)):
                with act.Fori(a0, a1) as a:
                    for n in range(4):
                        act.wait_ge(pj_ps, 4 * a + n + 1)
                        act.activation(QKV[:, bass.ds(a * (4 * BANK) + (2 * 4096 + BANK * n), BANK)], PS[:, n, :],
                                       ACT.Copy, scale=scale).then_inc(pj_sb, 1)

            def exp(kind, a, q, m):
                u, _, k = at(a, q)
                s, sc = at_s[kind], scores(kind, k, m)
                act.wait_ge(s["max_done"], u * 16 + 2 * k + m + 1 + AT)
                act.activation(sc, sc, ACT.Exp, bias=nmx[:, k % 4, m:m + 1], scale=-1.0,
                               accum_out=rs[:, k % 4, m:m + 1]).then_inc(s["exp_done"], 1)

            def keep_turned(kind, a, q, i):
                u, _, k = at(a, q)
                s, g = at_s[kind], DONE[k] + i
                _, b0, b1 = groups_of(T - 1 - k)[i]
                act.wait_ge(s["tr_done"], u * 24 + g + 1 + AT)
                act.wait_ge(s["pv_done"], u * 24 + g - 3 + AT)
                act.activation(PT[:, g % 4, 0:P * (b1 - b0)], PS[:, 4 + g % 2, 0:P * (b1 - b0)], ACT.Copy
                               ).then_inc(s["pt_act"], 1)

            def square(kind, a, q):
                u, _, k = at(a, q)
                if kind == "diff":
                    act.wait_ge(at_s[kind]["o_done"], u * 2 * T + 2 * k + 1 + AT)
                    act.activation(osq[:, :], osb[:, k % 2, :], ACT.Square, accum_out=oss[:, k % 2:k % 2 + 1]
                                   ).then_inc(at_s[kind]["o_square"], 1)

            def copy_out(kind, a, q):
                u, _, k = at(a, q)
                chunk = u + (UNITS if kind == "diff" else 0)
                act.wait_ge(at_s[kind]["ot_done"], u * T + k + 1 + AT)
                act.activation(HF[:, bass.ds(chunk * S + P * (T - 1 - k), P)] if not isinstance(chunk, int)
                               else HF[:, chunk * S + P * (T - 1 - k):chunk * S + P * (T - k)],
                               PS[:, 6 + k % 2, 256:384], ACT.Copy).then_inc(at_s[kind]["ot_copied"], 1)

            act.wait_ge(fill_out, 16 * NOV)
            for m in range(2):
                exp("diff", 0, 0, m)
            for kind in ("diff", "dsa"):
                with act.Fori(0, UNITS // 2) as a:
                    for q in range(2 * T):
                        four = len(groups_of(T - 1 - q % T)) == 4
                        keep_turned(kind, a, q, 0)
                        if q >= 2:
                            copy_out(kind, a, q - 2)
                        else:
                            with act.If(a > 0):
                                copy_out(kind, last, q - 2)
                            if kind == "dsa":
                                with act.If(a < last):
                                    copy_out("diff", last, q + 2 * T - 2)
                        if q + 1 < 2 * T:
                            exp(kind, a, q + 1, 0)
                        if q:
                            square(kind, a, q - 1)
                        elif kind == "diff":
                            with act.If(a > 0):
                                square(kind, last, q - 1)
                        else:
                            with act.If(a < last):
                                square("diff", last, 2 * T - 1)
                        if four:
                            keep_turned(kind, a, q, 2)
                        if q + 1 < 2 * T:
                            exp(kind, a, q + 1, 1)
                        else:
                            with act.If(a < last):
                                exp(kind, 0, q + 1, 0)
                                exp(kind, 0, q + 1, 1)
                if kind == "diff":
                    for m in range(2):
                        exp("dsa", 0, 0, m)
            copy_out("dsa", last, 2 * T - 2)
            copy_out("dsa", last, 2 * T - 1)

            for t in range(T + 1):
                if t < T:
                    act.wait_ge(x2_done, t + 1)
                    if t:
                        act.wait_ge(x2_sq, t)
                    act.activation(junk, XT[:, t, :], ACT.Square, accum_out=ss[:, 2 * T + t:2 * T + t + 1]
                                   ).then_inc(x2_sq, 1)
                if t >= 1:
                    for h in range(2):
                        act.wait_ge(h2T_ps, 2 * (t - 1) + h + 1)
                        if t >= 3:
                            act.wait_ge(lg_ps, t - 2)
                        act.activation(h2T[:, (t - 1) % 2, BANK * h:BANK * (h + 1)], PS[:, 4 + h, :], ACT.Copy
                                       ).then_inc(h2T_sb, 1)
            act.wait_ge(gmax_done, 1)
            act.activation(gx, gx, ACT.Exp).then_inc(gexp_done, 1)
            act.wait_ge(e2_in, 1)
            act.activation(rt[:, 3, :], rt[:, 3, :], ACT.Exp).then_inc(e2_done, 1)

            def ev_t(e, b):
                act.wait_ge(t_ps, e + 1)
                if not isinstance(e, int) or e >= 2:
                    act.wait_ge(gu_ps, e - 1)
                act.activation(hgT[b], PS[:, 0:2, :].rearrange("p a n -> p (a n)"), ACT.Copy).then_inc(t_sb, 1)

            def ev_sg(e, b):
                act.wait_ge(gu_ps, e + 1)
                if not isinstance(e, int) or e >= 2:
                    act.wait_ge(hid_done, e - 1)
                act.activation(sg[b], PS[:, 2 + b, 0:DE], ACT.Sigmoid).then_inc(sg_done, 1)

            def ev_h(e, b):
                act.wait_ge(ht_ps, e + 1)
                if not isinstance(e, int) or e >= 2:
                    act.wait_ge(dn_ps, e - 1)
                act.activation(hidT[b], PS[:, 4 + 3 * b, 0:DE], ACT.Copy).then_inc(ht_sb, 1)

            ev_t(0, 0)
            ev_sg(0, 0)
            ev_t(1, 1)
            for e in range(2):
                ev_h(e, e)
                ev_sg(e + 1, (e + 1) % 2)
                ev_t(e + 2, e % 2)
            with act.Fori(1, NE // 2 - 1) as i:
                for b in range(2):
                    e = 2 * i + b
                    ev_h(e, b)
                    ev_sg(e + 1, 1 - b)
                    ev_t(e + 2, b)
            ev_h(NE - 2, 0)
            ev_sg(NE - 1, 1)
            ev_h(NE - 1, 1)
            act.wait_ge(route_done, 2)
            n_ov = act.value_load(ovi[0:1, NOV:NOV + 1], min_val=0, max_val=NOV)
            with act.Fori(0, NOV // 2) as i:
                for b in range(2):
                    with act.If(n_ov > 2 * i + b):
                        e = 2 * i + (NE + b)
                        ev_t(e, b)
                        ev_sg(e, b)
                        ev_h(e, b)
            act.wait_ge(route_done, 1)
            act.dma_start(gfin, g_final.partition_broadcast(P)).then_inc(gf_in, 16)
            for t in range(T):
                act.wait_ge(cb_done, t + 1)
                if t:
                    act.wait_ge(fin_sq, t)
                act.activation(HF[:, 0:D], XT[:, t, :], ACT.Square, accum_out=ss[:, 3 * T + t:3 * T + t + 1]
                               ).then_inc(fin_sq, 1)

        @block.vector
        def _(dve):
            start_at(dve, ("max_done", "pt_dve", "o_done"))
            link = Chain(dve, dchain)
            dve.wait_ge(cols_ps, 1)
            dve.tensor_copy(cols[:, :], PS[:, 6, 0:MODC + 2 * KC]).then_inc(cols_sb, 1)
            dve.wait_ge(cols_sb, 1)
            dve.wait_ge(cexp_done, 1)
            link(dve.tensor_scalar(cexp[:, :], cexp[:, :], 1.0, None, ALU.add))
            link(dve.reciprocal(cexp[:, :], cexp[:, :]))
            dve.tensor_tensor(cact[:, :], cexp[:, :], cols[:, MODC:MODC + KC], ALU.mult).then_inc(cact_done, 1)
            dve.wait_ge(rstd_done, 1)
            for t in range(T):
                dve.tensor_scalar(XT[:, t, :], XT[:, t, :], ss[:, t:t + 1], None, ALU.mult).then_inc(xn_done, 1)
            def ada_sums(b, count):
                w = ada[b]
                link(dve.tensor_scalar(w[:, 0, :], w[:, 0, :], cact[:, 0:1], None, ALU.mult))
                for j in range(1, KC):
                    link(dve.scalar_tensor_tensor(out=w[:, 0, :], in0=w[:, j, :], scalar=cact[:, j:j + 1],
                                                  in1=w[:, 0, :], op0=ALU.mult, op1=ALU.add))
                dve.sem_inc(count, 1)

            def keep_row(r):
                dve.wait_ge(arow_ps, r + 1)
                dve.wait_ge(b_in[r % 2], 16 * (r // 2 + 1))
                if r >= 2:
                    dve.wait_ge(row_out[r % 2], 16 * (r // 2))
                dve.tensor_tensor(mrow[:, r % 2, :], PS[0:1, 6 + r % 2, :], brow[:, r % 2, :], ALU.add
                                  ).then_inc(arow_sb, 1)

            dve.wait_ge(cact_done, 1)
            for i in range(4):
                dve.wait_ge(ada_in[i], 16)
                ada_sums(i, acc_cols)
            dve.wait_ge(ada_done, 4)
            link(dve.tensor_tensor(mod[:, 0:2 * KC], PS[:, 7, 0:2 * KC], cols[:, 0:2 * KC], ALU.add))
            link(dve.tensor_scalar(sc1[:, :], mod[:, KC:2 * KC], 1.0, None, ALU.add))
            link(dve.tensor_tensor(sc1[:, :], sc1[:, :], cols[:, MODC + KC:MODC + 2 * KC], ALU.mult))
            dve.tensor_copy(cexp[:, :], sc1[:, :]).then_inc(aff_done, 1)
            for g in range(1, 2 * KC, 2):
                dve.wait_ge(xt_ps, g + 1)
                dve.tensor_scalar(HT[:, g // 2, BANK:2 * BANK], PS[:, g % 4, :], sc1[:, g // 2:g // 2 + 1],
                                  mod[:, g // 2:g // 2 + 1], ALU.mult, ALU.add).then_inc(xt_dve, 1)
            for r in range(4):
                dve.wait_ge(ada_in[r], 32)
                ada_sums(r, acc_rows)
            dve.wait_ge(small_in, 16 * 12)
            for i in range(2):
                dve.tensor_tensor_reduce(lamv[:, 2 * i, :], lamv[:, 2 * i, :], lamv[:, 2 * i + 1, :], 1.0, 0.0,
                                         ALU.mult, ALU.add, lam2[:, i:i + 1]).then_inc(lam_ready, 1)
            link(dve.tensor_scalar(gsub[:, :], gsub[:, :], 1.0 - LAM0, None, ALU.mult))
            dve.wait_ge(lam_exp, 1)
            link(dve.tensor_tensor(lam2[:, 0:1], lam2[:, 3:4], lam2[:, 2:3], ALU.subtract))
            link(dve.tensor_scalar(lam2[:, 0:1], lam2[:, 0:1], -LAM0, None, ALU.add))
            for r in range(4):
                keep_row(r)
            for t in range(T):
                dve.wait_ge(lat_ps, t + 1)
                dve.tensor_copy(ckv[:, LAT * t:LAT * (t + 1)], PS[:, 4 + t % 2, 0:LAT]).then_inc(lat_sb, 1)
                dve.tensor_scalar(iw[:, t, :], PS[:, 4 + t % 2, LAT:LAT + IH], IH ** -0.5, None, ALU.mult
                                  ).then_inc(lat_sb, 1)
            dve.wait_ge(lat_sb, 2 * T)
            for n in range(IH * NS):
                t, h = sel_tiles[n // IH], n % IH
                w = P * (t + 1)
                dst = SC[:, sc_off[t]:sc_off[t] + w]
                dve.wait_ge(ix_relu, n + 1)
                if h == 0:
                    dve.tensor_scalar(dst, RL[:, n % 2, 0:w], iw[:, t, h:h + 1], None, ALU.mult).then_inc(ix_acc, 1)
                else:
                    dve.wait_ge(ix_acc, n)
                    dve.scalar_tensor_tensor(out=dst, in0=RL[:, n % 2, 0:w], scalar=iw[:, t, h:h + 1], in1=dst,
                                             op0=ALU.mult, op1=ALU.add).then_inc(ix_acc, 1)
                if n in (19, 23):
                    keep_row(4 if n == 19 else 5)

            dve.wait_ge(lat_rstd, 1)
            for t in range(T):
                dve.scalar_tensor_tensor(out=ckv[:, LAT * t:LAT * (t + 1)], in0=ckv[:, LAT * t:LAT * (t + 1)],
                                         scalar=ss[:, T + t:T + t + 1], in1=gkv[:, :], op0=ALU.mult, op1=ALU.mult
                                         ).then_inc(ckv_done, 1)

            u_, bit, trial, mask, thr, keep = (tk[:, i, :] for i in range(6))
            link(dve.memset(u_.bitcast(F32), 0.0))
            link(dve.memset(bit.bitcast(F32), -0.0))
            dve.wait_ge(ix_mask, NS)

            def threshold(src, beside=None):
                if beside is not None:
                    beside.then_inc(dchain, 1)
                    link.n += 1
                link(dve.tensor_scalar(mask.bitcast(I32), src.bitcast(I32), 31, -1, ALU.arith_shift_right,
                                       ALU.bitwise_xor))
                link(dve.scalar_tensor_tensor(out=thr.bitcast(I32), in0=mask.bitcast(I32), scalar=-2147483648,
                                              in1=src.bitcast(I32), op0=ALU.bitwise_or, op1=ALU.bitwise_xor))

            with dve.Fori(0, 8) as it:
                link.loop(it, 4 * (6 + NS))
                for _ in range(4):
                    link(dve.tensor_tensor(trial, u_, bit, ALU.bitwise_or))
                    threshold(trial, dve.tensor_scalar(bit, bit, 1, None, ALU.logical_shift_right))
                    for i, t in enumerate(sel_tiles):
                        w = P * (t + 1)
                        if i >= 3:
                            dve.wait_ge(dchain, link.base + (link.n + i - 2))
                        dve.tensor_scalar(BIAS[:, i % 3, 0:w], SC[:, sc_off[t]:sc_off[t] + w],
                                          thr.bitcast(F32)[:, i:i + 1], 0.0, ALU.is_ge, ALU.add,
                                          accum_out=cnt[:, 0, i:i + 1]).then_inc(dchain, 1)
                    link.n += NS
                    dve.wait_ge(dchain, link.base + link.n)
                    link(dve.tensor_scalar(keep, cnt[:, 0, :], float(TOPK), None, ALU.is_ge))
                    settle(dve)
                    link(dve.copy_predicated(u_, keep, trial))
            link.leave(8)
            threshold(u_)
            dve.wait_ge(ckvT_ps, 2)
            for i, t in enumerate(sel_tiles):
                w = P * (t + 1)
                sc = SC[:, sc_off[t]:sc_off[t] + w]
                above, on, run = (a[:, 0:w] for a in sel_tmp[i % 2])
                th = thr.bitcast(F32)[:, i:i + 1]
                if i >= 2:
                    dve.wait_ge(sel_done, i - 1)
                dve.tensor_scalar(above, sc, th, 0.0, ALU.is_gt, ALU.add, accum_out=cnt[:, 1, i:i + 1]
                                  ).then_inc(dchain, 1)
                link.n += 1
                link(dve.tensor_scalar(on, sc, th, None, ALU.is_equal))
                dve.tensor_scalar(cnt[:, 1, i:i + 1], cnt[:, 1, i:i + 1], -1.0, float(TOPK), ALU.mult, ALU.add
                                  ).then_inc(dchain, 1)
                link.n += 1
                link(dve.tensor_tensor_scan(run, dist(t), on, 0.0, ALU.max, ALU.add))
                dve.scalar_tensor_tensor(out=run, in0=run, scalar=cnt[:, 1, i:i + 1], in1=on, op0=ALU.is_le,
                                         op1=ALU.mult).then_inc(sel_kept, 1)

            def score(kind, a, q, m):
                u, p, k = at(a, q)
                s, w = at_s[kind], P * (T - k)
                dve.wait_ge(s["qk_done"], u * 16 + 2 * k + m + 1 + AT)
                dve.wait_ge(s["bias_ready"], (u + 1 if kind == "diff" else u * 16 + 2 * k + m + 1) + AT)
                dve.wait_ge(s["tr_done"], u * 24 + (DONE[k - 2] if k >= 3 else DONE[k + 6] - 24) + AT)
                settle(dve)
                n, c0 = (p, S - w) if kind == "diff" else bias_place(2 * k + m)
                dve.tensor_tensor_reduce(
                    scores(kind, k, m), PS[:, 2 * m:2 * m + 2, :].rearrange("p a n -> p (a n)")[:, 0:w],
                    BIAS[:, n, c0:c0 + w], -1.0, 3.0e38, ALU.add, ALU.min, nmx[:, k % 4, m:m + 1]
                ).then_inc(s["max_done"], 1)

            def keep_turned(kind, a, q, i):
                u, _, k = at(a, q)
                s, g = at_s[kind], DONE[k] + i
                _, b0, b1 = groups_of(T - 1 - k)[i]
                dve.wait_ge(s["tr_done"], u * 24 + g + 1 + AT)
                dve.wait_ge(s["pv_done"], u * 24 + g - 3 + AT)
                dve.tensor_copy(PT[:, g % 4, 0:P * (b1 - b0)], PS[:, 4 + g % 2, 0:P * (b1 - b0)]
                                ).then_inc(s["pt_dve"], 1)

            def norm(kind, a, q):
                u, _, k = at(a, q)
                s, r, o, b = at_s[kind], k % 4, k % 2, 6 + k % 2
                dve.wait_ge(s["pv_done"], u * 24 + DONE[k + 1] + AT)
                dve.wait_ge(s["ot_done"], u * T + k - 1 + AT)
                link(dve.reciprocal(rin[:, r, :], rs[:, r, :]))
                if kind == "dsa":
                    for m in range(2):
                        dve.tensor_scalar(osb[:, o, DH * m:DH * (m + 1)], PS[:, b, DH * m:DH * (m + 1)],
                                          rin[:, r, m:m + 1], None, ALU.mult).then_inc(s["o_done"], 1)
                    return
                link(dve.tensor_scalar(rin[:, r, 1:2], rin[:, r, 1:2], lam2[:, 0:1], None, ALU.mult))
                link(dve.tensor_scalar(osb[:, o, :], PS[:, b, 0:DV], rin[:, r, 0:1], None, ALU.mult))
                dve.scalar_tensor_tensor(out=osb[:, o, :], in0=PS[:, b, DV:2 * DV], scalar=rin[:, r, 1:2],
                                         in1=osb[:, o, :], op0=ALU.mult, op1=ALU.add).then_inc(s["o_done"], 1)

            def sub_norm(kind, a, q):
                u, _, k = at(a, q)
                if kind == "diff":
                    dve.wait_ge(at_s[kind]["o_rstd"], u * T + k + 1 + AT)
                    dve.scalar_tensor_tensor(out=osb[:, k % 2, :], in0=osb[:, k % 2, :],
                                             scalar=oss[:, 2 + k % 2:3 + k % 2], in1=gsub[:, :], op0=ALU.mult,
                                             op1=ALU.mult).then_inc(at_s[kind]["o_done"], 1)

            dve.wait_ge(fill_out, 16 * NOV)
            def first_scores(kind):
                for q in range(2):
                    for m in range(2):
                        score(kind, 0, q, m)

            first_scores("diff")
            for kind in ("diff", "dsa"):
                late = 3 if kind == "diff" else 1
                with dve.Fori(0, UNITS // 2) as a:
                    link.loop(a, 2 * T * late)
                    for q in range(2 * T):
                        four = len(groups_of(T - 1 - q % T)) == 4
                        keep_turned(kind, a, q, 1)
                        if q:
                            norm(kind, a, q - 1)
                        else:
                            with dve.If(a > 0):
                                link.n = -late
                                norm(kind, last, q - 1)
                                sub_norm(kind, last, q - 1)
                            if kind == "dsa":
                                with dve.If(a < last):
                                    sub_norm("diff", last, 2 * T - 1)
                        if q + 2 < 2 * T:
                            score(kind, a, q + 2, 0)
                            if four:
                                keep_turned(kind, a, q, 3)
                            score(kind, a, q + 2, 1)
                        else:
                            with dve.If(a < last):
                                score(kind, 0, q + 2, 0)
                                score(kind, 0, q + 2, 1)
                        if q:
                            sub_norm(kind, a, q - 1)
                link.leave(UNITS // 2, late)
                norm(kind, last, 2 * T - 1)
                if kind == "diff":
                    first_scores("dsa")

            dve.wait_ge(vec_in, 16 * 4)
            link(dve.tensor_scalar(falling[:, :], iota_t[:, 0:NE], -1.0, float(NE), ALU.mult, ALU.add))
            for t in range(T + 2):
                if 1 <= t <= T:
                    q = t - 1
                    if q == 0:
                        dve.wait_ge(rows_done, 2)
                    if q >= 2:
                        dve.wait_ge(h2_out[q % 2], 16 * (q // 2))
                        dve.wait_ge(h2T_ps, 2 * (q - 1))
                    dve.wait_ge(x2_rstd, q + 1)
                    link(dve.scalar_tensor_tensor(out=h2[:, q % 2, :], in0=XT[:, q, :],
                                                  scalar=ss[:, 2 * T + q:2 * T + q + 1], in1=rows[2], op0=ALU.mult,
                                                  op1=ALU.mult))
                    dve.tensor_tensor(h2[:, q % 2, :], h2[:, q % 2, :], rows[1], ALU.add).then_inc(h2_done, 1)
                if t < T:
                    for h in range(2):
                        n = 2 * t + h
                        part = slice(BANK * h, BANK * (h + 1))
                        dve.wait_ge(op_ps, n + 1)
                        if n >= 2:
                            dve.wait_ge(x2_half, n - 1)
                        dve.tensor_tensor(proj[:, h, :], PS[:, n % 4, :], rows[0][:, part], ALU.mult
                                          ).then_inc(op_sb, 1)
                        dve.wait_ge(op_sb, n + 1)
                        if n == 0:
                            dve.wait_ge(x_in[0], 16 + 16)
                        elif n == 2:
                            dve.wait_ge(x_in[1], 16 + 16 * (T - 1))
                        ins = dve.tensor_tensor(XT[:, t, part], proj[:, h, :], XT[:, t, part], ALU.add)
                        ins.then_inc(x2_half, 1)
                    dve.wait_ge(x2_half, 2 * t + 2)
                    dve.sem_inc(x2_done, 1)
                if t >= 2:
                    q = t - 2
                    dve.wait_ge(lg_ps, q + 1)
                    dve.tensor_tensor(logits[:, q, :], PS[:, 6 + q % 2, 0:NR], bgr[:, :], ALU.add
                                      ).then_inc(lg_sb, 1)

            def over(a, n):
                return a.unsqueeze(2).to_broadcast([P, T, n])

            gl, el = logits[:, :, 0:NG], logits[:, :, NG:NR]
            pg, v1, v2, e2, key, w1, w2 = (rt[:, i, :] for i in (0, 1, 2, 3, 4, 5, 6))
            tile_of, row_of = [rt[:, 7, :], rt[:, 8, :]], [rt[:, 9, :], rt[:, 10, :]]
            em, tmp, tmp2, carry, fl, tl = rbig[0], rbig[1], rbig[2], rbig[5], rbig[6], rbig[7]
            pick = [rbig[3], rbig[4]]
            down = iota_t[:, 0:NE].unsqueeze(1)
            dve.wait_ge(op_ps, 2 * T)
            dve.wait_ge(lg_sb, T)
            link(dve.tensor_reduce(v1, gl, AX_X, ALU.max))
            link(dve.tensor_tensor(gx, gl, over(v1, NG), ALU.subtract))
            link(dve.tensor_scalar(gk, gx, 0.0, None, ALU.is_ge))
            link(dve.tensor_tensor(gk, gk, falling[:, 0:NG].unsqueeze(1).to_broadcast([P, T, NG]), ALU.mult))
            link(dve.tensor_reduce(key, gk, AX_X, ALU.max))
            link(dve.tensor_tensor(gk, gk, over(key, NG), ALU.is_equal))
            dve.sem_inc(gmax_done, 1)
            link(dve.tensor_scalar(gk, gk, -1.0, -NEG, ALU.add, ALU.mult))
            link(dve.tensor_tensor(em.rearrange("p t (g e) -> p t g e", g=NG),
                                   el.rearrange("p t (g e) -> p t g e", g=NG),
                                   gk.unsqueeze(3).to_broadcast([P, T, NG, EPG]), ALU.add))
            for k, v in enumerate((v1, v2)):
                link(dve.tensor_reduce(v, em, AX_X, ALU.max))
                link(dve.tensor_tensor(tmp, em, over(v, NE), ALU.is_equal))
                link(dve.tensor_tensor(tmp, tmp, falling[:, :].unsqueeze(1).to_broadcast([P, T, NE]), ALU.mult))
                link(dve.tensor_reduce(key, tmp, AX_X, ALU.max))
                link(dve.tensor_tensor(pick[k], tmp, over(key, NE), ALU.is_equal))
                if k == 0:
                    link(dve.scalar_tensor_tensor(out=em.rearrange("p t e -> p (t e)"),
                                                  in0=pick[0].rearrange("p t e -> p (t e)"), scalar=2 * NEG,
                                                  in1=em.rearrange("p t e -> p (t e)"), op0=ALU.mult, op1=ALU.add))
            dve.tensor_tensor(e2, v2, v1, ALU.subtract).then_inc(e2_in, 1)
            dve.tensor_tensor(rbig[9], pick[0], pick[1], ALU.add).then_inc(sel_in, 1)
            link(dve.memset(carry[:, 0, :], 0.0))
            dve.wait_ge(sel_ps, 1)
            rank, total = PS[:, 0, 0:T * NE], PS[:, 1, 0:T * NE].rearrange("p (t e) -> p t e", t=T)
            flat = lambda a: a.rearrange("p t e -> p (t e)")
            n_ov, ov_end, ov_base = (ovc[:, i, :] for i in range(3))
            ri, rq = flat(rbig[10]).bitcast(I32), flat(rbig[11]).bitcast(I32)
            ni = ovc[:, 3, :].bitcast(I32)
            link(dve.tensor_copy(carry[:, 1, :], total[:, 0, :]))
            for t in range(2, T):
                link(dve.tensor_tensor(carry[:, t, :], carry[:, t - 1, :], total[:, t - 1, :], ALU.add))
            dve.tensor_tensor(ri, rank, flat(carry), ALU.add).then_inc(dchain, 1)
            link.n += 1
            link(dve.scalar_tensor_tensor(out=ni, in0=carry[:, T - 1, :], scalar=-1.0, in1=total[:, T - 1, :],
                                          op0=ALU.add, op1=ALU.add))
            dve.tensor_scalar(rq, ri, 7, None, ALU.arith_shift_right).then_inc(dchain, 1)
            dve.tensor_scalar(ri, ri, P - 1, None, ALU.bitwise_and).then_inc(dchain, 1)
            link.n += 2
            link(dve.tensor_scalar(ni, ni, 7, None, ALU.arith_shift_right))
            dve.tensor_copy(flat(fl), rq).then_inc(dchain, 1)
            dve.tensor_copy(flat(tmp2), ri).then_inc(dchain, 1)
            link.n += 2
            link(dve.tensor_scalar(n_ov, ni, 0.0, None, ALU.max))
            link(dve.memset(ovc[:, 4, :], 0.0))
            link(dve.tensor_tensor_scan(ov_end, ovc[:, 4, :], n_ov, 0.0, ALU.add, ALU.add))
            link(dve.tensor_tensor(ov_base, ov_end, n_ov, ALU.subtract))
            link(dve.tensor_scalar(ov_base, ov_base, float(NE - 1), None, ALU.add))
            link(dve.tensor_tensor(ov_base, ov_base, iota_t[:, 0:NE], ALU.subtract))
            link(dve.tensor_tensor(tl, fl, ov_base.unsqueeze(1).to_broadcast([P, T, NE]), ALU.add))
            link(dve.tensor_scalar(flat(fl), flat(fl), 1.0, None, ALU.min))
            link(dve.tensor_tensor(tl, tl, fl, ALU.mult))
            link(dve.tensor_tensor(tl, tl, down.to_broadcast([P, T, NE]), ALU.add))
            for k in range(2):
                for src, dst in ((tl, tile_of[k]), (tmp2, row_of[k])):
                    link(dve.tensor_tensor(tmp, src, pick[k], ALU.mult))
                    link(dve.tensor_reduce(dst, tmp, AX_X, ALU.add))
                link(dve.scalar_tensor_tensor(out=key, in0=tile_of[k], scalar=float(P), in1=row_of[k],
                                              op0=ALU.mult, op1=ALU.add))
                link(dve.tensor_copy(slot[:, k, :], key))
            dve.sem_inc(place_done, 1)
            for i in range(2 * T):
                k, t = i // T, i % T
                if i < T + 2:
                    dve.tensor_scalar(oht[i], iota_t[:, :], tile_of[k][:, t:t + 1], tok[:, t:t + 1],
                                      ALU.is_equal, ALU.mult).then_inc(oh_done, 1)
                dve.tensor_scalar(ohr[i], iota_p[:, :], row_of[k][:, t:t + 1], None, ALU.is_equal
                                  ).then_inc(oh_done, 1)
            dve.wait_ge(gexp_done, 1)
            link(dve.tensor_reduce(pg, gx, AX_X, ALU.add))
            link(dve.reciprocal(pg, pg))
            dve.wait_ge(lst_ps, 1)
            dve.tensor_copy(lst[:, :], PS[:, 2, 0:NT]).then_inc(route_done, 1)
            link(dve.tensor_tensor(ovt, ov_end.unsqueeze(1).to_broadcast([P, NOV + 1, NE]),
                                   iota_t[:, 0:NOV + 1].unsqueeze(2).to_broadcast([P, NOV + 1, NE]), ALU.is_le))
            link(dve.tensor_reduce(ovx[:, 0:NOV + 1], ovt, AX_X, ALU.add))
            link(dve.tensor_scalar(ovx[:, 0:NOV], ovx[:, 0:NOV], float(NE - 1), None, ALU.min))
            link(dve.tensor_copy(ovx[:, NOV:NOV + 1], ov_end[:, NE - 1:NE]))
            link(dve.tensor_copy(ovi[:, 0:NOV + 1], ovx[:, 0:NOV + 1]))
            dve.wait_ge(e2_done, 1)
            link(dve.tensor_scalar(w1, e2, 1.0, None, ALU.add))
            link(dve.reciprocal(w1, w1))
            link(dve.tensor_tensor(w1, w1, pg, ALU.mult))
            link(dve.tensor_tensor(w2, w1, e2, ALU.mult))
            dve.sem_inc(route_done, 1)

            def ev_hid(e, b):
                dve.wait_ge(sg_done, e + 1)
                if not isinstance(e, int) or e >= 1:
                    dve.wait_ge(hid_done, e)
                if not isinstance(e, int) or e >= 2:
                    dve.wait_ge(ht_ps, e - 1)
                dve.tensor_tensor(hh, PS[:, 2 + b, 0:DE], sg[b], ALU.mult).then_inc(hh_done, 1)
                dve.wait_ge(hh_done, e + 1)
                dve.tensor_tensor(hid[b], hh, PS[:, 2 + b, DE:2 * DE], ALU.mult).then_inc(hid_done, 1)

            def ev_y(e, b, stored):
                dve.wait_ge(dn_ps, e + 1)
                dve.wait_ge(y_out[b], stored * 16)
                dve.tensor_tensor(ysb[b], PS[:, 5:7, :].rearrange("p a n -> p (a n)"), rows[3], ALU.mult
                                  ).then_inc(y_sb, 1)

            ev_hid(0, 0)
            for e in range(2):
                ev_hid(e + 1, (e + 1) % 2)
                ev_y(e, e, 0)
            with dve.Fori(1, NE // 2 - 1) as i:
                for b in range(2):
                    e = 2 * i + b
                    ev_hid(e + 1, 1 - b)
                    ev_y(e, b, i)
            ev_hid(NE - 1, 1)
            ev_y(NE - 2, 0, NE // 2 - 1)
            ev_y(NE - 1, 1, NE // 2 - 1)
            dve.wait_ge(route_done, 2)
            n_ov = dve.value_load(ovi[0:1, NOV:NOV + 1], min_val=0, max_val=NOV)
            with dve.Fori(0, NOV // 2) as i:
                for b in range(2):
                    with dve.If(n_ov > 2 * i + b):
                        ev_hid(2 * i + (NE + b), b)
                        ev_y(2 * i + (NE + b), b, i + NE // 2)

            dve.wait_ge(gf_in, 16)
            for t in range(T + 1):
                if t < T:
                    y1, y2 = yg[t % 4]
                    dve.wait_ge(yg_in[t % 4], 32 * (t // 4 + 1))
                    link(dve.scalar_tensor_tensor(out=XT[:, t, :], in0=y1, scalar=w1[:, t:t + 1], in1=XT[:, t, :],
                                                  op0=ALU.mult, op1=ALU.add))
                    dve.scalar_tensor_tensor(out=XT[:, t, :], in0=y2, scalar=w2[:, t:t + 1], in1=XT[:, t, :],
                                             op0=ALU.mult, op1=ALU.add).then_inc(cb_done, 1)
                if t:
                    dve.wait_ge(fin_rstd, t)
                    dve.scalar_tensor_tensor(out=XT[:, t - 1, :], in0=XT[:, t - 1, :],
                                             scalar=ss[:, 3 * T + t - 1:3 * T + t], in1=gfin, op0=ALU.mult,
                                             op1=ALU.mult).then_inc(fin_done, 1)

        @block.tensor
        def _(pe):
            start_at(pe, ("qk_done", "tr_done", "pv_done", "ot_done"))
            pe.wait_ge(consts, 8)
            pe.wait_ge(vec_in, 16 * 3)
            nv = MODC + 2 * KC
            pe.transpose(PS[:, 6, 0:nv], vrows, ident[0:nv, 0:nv]).then_inc(cols_ps, 1)

            pe.wait_ge(xn_done, T)
            for g in range(2 * KC):
                j, half = g // 2, g % 2
                if g >= 4:
                    pe.wait_ge(xt_act if half == 0 else xt_dve, (g - 4) // 2 + 1)
                for i in range(4):
                    end = pe.transpose(PS[:, g % 4, P * i:P * (i + 1)], XT[:, 4 * half + i, P * j:P * (j + 1)],
                                        ident[:, :])
                end.then_inc(xt_ps, 1)
                if g == 3:
                    for b in range(4):
                        pe.wait_ge(acc_cols, b + 1)
                        for q in range(4):
                            end = pe.matmul(PS[:, 7, 4 * b + q:4 * b + q + 1], ada[b][:, 0, P * q:P * (q + 1)],
                                             ones[:, 0:1], start=True, stop=True)
                        end.then_inc(ada_done, 1)
            pe.wait_ge(xt_act, KC)
            pe.wait_ge(xt_dve, KC)
            pe.wait_ge(wcopy, 6)
            for n in range(4):
                for j in range(KC):
                    end = pe.matmul(PS[:, n, :], WI[:, j, LAT:LAT + P] if n < 2 else WIK[:, j, :],
                                     HT[:, j, BANK * (n % 2):BANK * (n % 2 + 1)], start=(j == 0), stop=(j == KC - 1))
                end.then_inc(iqk_ps, 1)

            def ada_row(r):
                if r >= 4:
                    pe.wait_ge(acc_pool, r - 3)
                else:
                    pe.wait_ge(acc_rows, r + 1)
                if r >= 2:
                    pe.wait_ge(arow_sb, r - 1)
                end = pe.matmul(PS[0:1, 6 + r % 2, :], ones[:, 0:1], ada[r % 4][:, 0, :], start=True, stop=(r < 6))
                if r >= 6:
                    pe.wait_ge(b_in[r % 2], 16 * (r // 2 + 1))
                    end = pe.matmul(PS[0:1, 6 + r % 2, :], ones[0:1, 0:1], brow[:, r % 2, :], start=False, stop=True)
                end.then_inc(arow_ps, 1)

            for r in range(4):
                ada_row(r)
            for t in range(T):
                if t >= 2:
                    pe.wait_ge(lat_sb, 2 * (t - 1))
                for j in range(KC):
                    end = pe.matmul(PS[:, 4 + t % 2, 0:LAT + IH], HT[:, j, P * t:P * (t + 1)], WD[:, j, :],
                                     start=(j == 0), stop=(j == KC - 1))
                end.then_inc(lat_ps, 1)
            pe.wait_ge(iqk_sb, 2 * IH + 2)
            for n in range(IH * NS):
                t, h = sel_tiles[n // IH], n % IH
                w = P * (t + 1)
                if n >= 2:
                    pe.wait_ge(ix_relu, n - 1)
                for c0 in range(0, w, BANK):
                    c1 = min(c0 + BANK, w)
                    end = pe.matmul(PS[:, 2 * (n % 2) + c0 // BANK, 0:c1 - c0], iqT[h][:, P * t:P * (t + 1)],
                                    ikT[:, c0:c1], start=True, stop=True)
                end.then_inc(ix_ps, 1)
                if n in (17, 21):
                    ada_row(4 + (17, 21).index(n))
            pe.wait_ge(ckv_done, T)
            for n in range(2):
                for i in range(4):
                    end = pe.transpose(PS[:, 4 + n, P * i:P * (i + 1)], ckv[:, P * (4 * n + i):P * (4 * n + i + 1)],
                                        ident[:, :])
                end.then_inc(ckvT_ps, 1)
            pe.wait_ge(ckvT_sb, 2)
            for n in range(2 * UNITS):
                if n >= 2:
                    pe.wait_ge(kv_sb, n - 1)
                pe.matmul(PS[:, 4 + n % 2, :], wuk[:, n // 2 * 2:n // 2 * 2 + 2, :].rearrange("p h d -> p (h d)"),
                          ckvT[:, BANK * (n % 2):BANK * (n % 2 + 1)], start=True, stop=True).then_inc(kv_ps, 1)
            for t in range(T):
                pe.wait_ge(kv_sb, 2 * UNITS + t - 1)
                pe.matmul(PS[:, 4 + t % 2, :], ckvT[:, P * t:P * (t + 1)],
                          wuv[:, :, :].rearrange("p h d -> p (h d)"), start=True, stop=True).then_inc(kv_ps, 1)

            def project(b, half):
                for j in range(KC):
                    end = pe.matmul(PS[:, 2 * b + half, :], WS[:, b, j, :], HT[:, j, BANK * half:BANK * (half + 1)],
                                     start=(j == 0), stop=(j == KC - 1))
                end.then_inc(pj_ps, 1)

            def project_rows(b, half):
                for i in range(4):
                    t = 4 * half + i
                    for j in range(KC):
                        end = pe.matmul(PS[:, 2 * b + half, P * i:P * (i + 1)], HT[:, j, P * t:P * (t + 1)],
                                         WS[:, b, j, :], start=(j == 0), stop=(j == KC - 1))
                end.then_inc(pj_ps, 1)

            for r in (6, 7):
                ada_row(r)
            pe.wait_ge(ix_relu, IH * NS)
            for b in range(2):
                pe.wait_ge(ws_in[b], 16)
                for half in range(2):
                    project(b, half)
            for a0, a1, what in ((1, 6, project), (6, 8, project_rows)):
                with pe.Fori(a0, a1) as a:
                    for b in range(2):
                        pe.wait_ge(ws_in[b], a * 16 + 16)
                        for half in range(2):
                            pe.wait_ge(pj_sb, a * 4 + (2 * b + half - 3))
                            what(b, half)
            pe.wait_ge(kv_sb, 2 * UNITS + T)
            pe.wait_ge(pj_sb, 32)

            def qk(kind, a, q, m):
                u, p, k = at(a, q)
                s, t, w = at_s[kind], T - 1 - k, P * (T - k)
                if k == 0 and m == 0:
                    pe.wait_ge(s["qk_loaded"], u * 4 + 4 + AT)
                pe.wait_ge(s["max_done"], u * 16 + 2 * k + m - 1 + AT)
                for c0 in range(0, w, BANK):
                    c1 = min(c0 + BANK, w)
                    end = pe.matmul(PS[:, 2 * m + c0 // BANK, 0:c1 - c0],
                                     qst[kind][p][DH * m:DH * (m + 1), P * t:P * (t + 1)],
                                     kst[kind][p][DH * m:DH * (m + 1), c0:c1], start=True, stop=True)
                end.then_inc(s["qk_done"], 1)

            def turn(kind, a, q, i):
                u, _, k = at(a, q)
                s, g = at_s[kind], DONE[k] + i
                m, b0, b1 = groups_of(T - 1 - k)[i]
                pe.wait_ge(s["exp_done"], u * 16 + 2 * k + m + 1 + AT)
                pe.wait_ge(s["pt_dve" if g % 2 else "pt_act"], u * 12 + g // 2 + AT)
                for b in range(b0, b1):
                    end = pe.transpose(PS[:, 4 + g % 2, P * (b - b0):P * (b - b0 + 1)],
                                        scores(kind, k, m)[:, P * b:P * (b + 1)], ident[:, :])
                end.then_inc(s["tr_done"], 1)

            def pv(kind, a, q, i):
                u, _, k = at(a, q)
                s, g, width = at_s[kind], DONE[k] + i, DH if kind == "dsa" else DV
                m, b0, b1 = groups_of(T - 1 - k)[i]
                if i == 0:
                    pe.wait_ge(s["ot_copied"], u * T + k - 1 + AT)
                pe.wait_ge(s["pt_dve" if g % 2 else "pt_act"], u * 12 + g // 2 + 1 + AT)
                for b in range(b0, b1):
                    v = (vd[:, b, bass.ds(u * (2 * DH) + DH * m, DH)] if kind == "dsa"
                         else vf[:, bass.ds(u * S + P * b, DV)])
                    end = pe.matmul(PS[:, 6 + k % 2, width * m:width * (m + 1)],
                                     PT[:, g % 4, P * (b - b0):P * (b - b0 + 1)], v, start=(b == 0),
                                     stop=(b == T - 1 - k))
                end.then_inc(s["pv_done"], 1)

            def turn_out(kind, a, q):
                u, _, k = at(a, q)
                pe.wait_ge(at_s[kind]["o_done"], u * 2 * T + 2 * k + 2 + AT)
                pe.transpose(PS[:, 6 + k % 2, 256:384], osb[:, k % 2, :], ident[:, :]
                             ).then_inc(at_s[kind]["ot_done"], 1)

            def first_qks(kind):
                for q in range(2):
                    for m in range(2):
                        qk(kind, 0, q, m)

            first_qks("diff")
            for kind in ("diff", "dsa"):
                with pe.Fori(0, UNITS // 2) as a:
                    for q in range(2 * T):
                        four = len(groups_of(T - 1 - q % T)) == 4
                        turn(kind, a, q, 0)
                        turn(kind, a, q, 1)
                        if q >= 2:
                            turn_out(kind, a, q - 2)
                        else:
                            with pe.If(a > 0):
                                turn_out(kind, last, q - 2)
                            if kind == "dsa":
                                with pe.If(a < last):
                                    turn_out("diff", last, q + 2 * T - 2)
                                    pe.wait_ge(at_s["diff"]["ot_copied"], UNITS * T - 1 + q + AT)
                                    settle(pe)
                        if q + 2 < 2 * T:
                            qk(kind, a, q + 2, 0)
                        else:
                            with pe.If(a < last):
                                qk(kind, 0, q + 2, 0)
                                qk(kind, 0, q + 2, 1)
                        pv(kind, a, q, 0)
                        if four:
                            turn(kind, a, q, 2)
                            pv(kind, a, q, 1)
                            turn(kind, a, q, 3)
                        if q + 2 < 2 * T:
                            qk(kind, a, q + 2, 1)
                        for i in ((2, 3) if four else (1,)):
                            pv(kind, a, q, i)
                if kind == "diff":
                    pe.wait_ge(at_s[kind]["max_done"], 16 * UNITS + AT)
                    first_qks("dsa")
            for q in range(2 * T - 2, 2 * T):
                turn_out("dsa", last, q)
            pe.wait_ge(at_s["dsa"]["ot_copied"], UNITS * T + AT)

            pe.wait_ge(wo_in, 16)
            for t in range(T + 2):
                if t < T:
                    for h in range(2):
                        n = 2 * t + h
                        if n >= 4:
                            pe.wait_ge(op_sb, n - 3)
                        for k in range(KC):
                            end = pe.matmul(PS[:, n % 4, :], HT[:, k, P * t:P * (t + 1)],
                                             wo[:, k, BANK * h:BANK * (h + 1)], start=(k == 0), stop=(k == KC - 1))
                        end.then_inc(op_ps, 1)
                if 1 <= t <= T:
                    q = t - 1
                    pe.wait_ge(h2_done, q + 1)
                    for h in range(2):
                        if q:
                            pe.wait_ge(h2T_sb, 2 * (q - 1) + h + 1)
                        for i in range(4):
                            end = pe.transpose(PS[:, 4 + h, P * i:P * (i + 1)],
                                                h2[:, q % 2, P * (4 * h + i):P * (4 * h + i + 1)], ident[:, :])
                        end.then_inc(h2T_ps, 1)
                if t >= 2:
                    q = t - 2
                    pe.wait_ge(h2T_sb, 2 * q + 2)
                    if q >= 2:
                        pe.wait_ge(lg_sb, q - 1)
                    for j in range(KC):
                        end = pe.matmul(PS[:, 6 + q % 2, 0:NR], h2T[:, q % 2, P * j:P * (j + 1)],
                                         wgr[:, j, :], start=(j == 0), stop=(j == KC - 1))
                    end.then_inc(lg_ps, 1)

            pe.wait_ge(sel_in, 1)
            chosen = rbig[9].rearrange("p t e -> p (t e)")
            pe.matmul(PS[:, 0, 0:T * NE], before[:, :], chosen, start=True, stop=True)
            pe.matmul(PS[:, 1, 0:T * NE], ones[:, :], chosen, start=True, stop=True).then_inc(sel_ps, 1)
            for i in range(2 * T):
                pe.wait_ge(oh_done, 2 * i + 2 if i < T + 2 else i + T + 3)
                if i >= T + 2:
                    pe.wait_ge(oht_done, i - T - 1)
                end = pe.matmul(PS[:, 2, 0:NT], ohr[i], oht[i], start=(i == 0), stop=(i == 2 * T - 1))
            end.then_inc(lst_ps, 1)
            pe.wait_ge(route_done, 1)

            def turn_rows(e, b, arrived):
                pe.wait_ge(xg_in[b], arrived)
                if not isinstance(e, int) or e >= 1:
                    pe.wait_ge(t_sb, e)
                for c_ in range(KC):
                    end = pe.transpose(PS[:, c_ // 4, P * (c_ % 4):P * (c_ % 4 + 1)],
                                        xg[b].rearrange("p (k c) -> p c k", c=KC)[:, c_, :], ident[:, :])
                end.then_inc(t_ps, 1)

            def gate_up(e, b, w, arrived):
                pe.wait_ge(t_sb, e + 1)
                pe.wait_ge(w_in_s[w], arrived)
                if not isinstance(e, int) or e >= 2:
                    pe.wait_ge(hid_done, e - 1)
                for c_ in range(KC):
                    end = pe.matmul(PS[:, 2 + b, :], hgT[b][:, P * c_:P * (c_ + 1)], WGU[w][:, c_, :, :],
                                     start=(c_ == 0), stop=(c_ == KC - 1))
                end.then_inc(gu_ps, 1)

            def turn_hidden(e, b):
                pe.wait_ge(hid_done, e + 1)
                if not isinstance(e, int) or e >= 2:
                    pe.wait_ge(ht_sb, e - 1)
                for c_ in range(2):
                    end = pe.transpose(PS[:, 4 + 3 * b, P * c_:P * (c_ + 1)],
                                        hid[b].rearrange("p (k c) -> p c k", c=2)[:, c_, :], ident[:, :])
                end.then_inc(ht_ps, 1)

            def down_proj(e, b, w):
                pe.wait_ge(ht_sb, e + 1)
                if not isinstance(e, int) or e >= 1:
                    pe.wait_ge(y_sb, e)
                for h in range(2):
                    for c_ in range(2):
                        end = pe.matmul(PS[:, 5 + h, :], hidT[b][:, P * c_:P * (c_ + 1)],
                                         WDN[w][:, c_, BANK * h:BANK * (h + 1)], start=(c_ == 0), stop=(c_ == 1))
                end.then_inc(dn_ps, 1)

            def step(e, j, i, last2=None):
                b = j % 2
                turn_hidden(e, b)
                if last2 != 1:
                    w = (j + 1) % 4
                    gate_up(e + 1, 1 - b, w, (i + 1 + (j + 1) // 4) * 48)
                if last2 is None:
                    turn_rows(e + 2, b, (2 * i + (j + 2) // 2 + 1) * 16)
                down_proj(e, b, j)

            turn_rows(0, 0, 16)
            gate_up(0, 0, 0, 48)
            turn_rows(1, 1, 16)
            for j in range(4):
                step(j, j, 0)
            with pe.Fori(1, NE // 4 - 1) as i:
                for j in range(4):
                    step(i * 4 + j, j, i)
            for j in range(4):
                step(NE - 4 + j, j, NE // 4 - 1, None if j < 2 else j - 2)

            pe.wait_ge(route_done, 2)
            n_ov = pe.value_load(ovi[0:1, NOV:NOV + 1], min_val=0, max_val=NOV)
            with pe.Fori(0, NOV // 2) as i:
                for b in range(2):
                    with pe.If(n_ov > 2 * i + b):
                        e = 2 * i + (NE + b)
                        turn_rows(e, b, i * 16 + 16 * (NE // 2 + 1))
                        gate_up(e, b, b, i * 48 + 48 * (NE // 4 + 1))
                        turn_hidden(e, b)
                        down_proj(e, b, b)


_INS = ["x", "c", "w_ada", "b_ada", "g_attn", "w_in", "g_kv", "w_uk", "w_uv", "lam_q1", "lam_k1", "lam_q2", "lam_k2",
        "g_sub", "w_out", "g_moe", "w_group", "b_group", "w_router", "b_router", "w_gate", "w_up", "w_down", "g_final"]


def kernel(**inputs):
    import numpy as _np
    import concourse.bacc as _bacc
    from concourse import mybir as _mybir
    from concourse.bass_utils import run_bass_kernel_spmd as _run

    nc = _bacc.Bacc("TRN2", target_bir_lowering=False, num_devices=1)
    arrays, args = {}, []
    for name in _INS:
        a = _np.ascontiguousarray(inputs[name])
        arrays[f"in_{name}_dram"] = a
        args.append(nc.dram_tensor(f"in_{name}_dram", a.shape, _mybir.dt.from_np(a.dtype), kind="ExternalInput").ap())
    shape = inputs["x"].shape
    args.append(nc.dram_tensor("out_0_dram", shape, _mybir.dt.float32, kind="ExternalOutput").ap())
    hybrid_layer(nc, *args)
    r = _run(nc, [arrays], core_ids=[0])
    return r.results[0]["out_0_dram"]
```
